# Optimizing a Trainium2 kernel written in Bass

```python
import jax, jax.numpy as jnp
from jax import lax
import numpy as np

D_MODEL = 1024
BATCH = 1
SEQ = 512
DEPTH = 2

N_EVEN = (DEPTH + 1) // 2
N_ODD = DEPTH // 2
EPS = 1e-6
N_MOD = 6

ATTN_WIDTH = D_MODEL // 2
HEAD_DIM = 64
N_HEADS = ATTN_WIDTH // HEAD_DIM
Q_PER_KV = 4
N_KV_HEADS = N_HEADS // Q_PER_KV
KV_WIDTH = N_KV_HEADS * HEAD_DIM
WINDOW = 128
BLOCK = 128

CONV_WIDTH = D_MODEL - ATTN_WIDTH
CONV_K = 3

IN_WIDTH = ATTN_WIDTH + 2 * KV_WIDTH + 3 * CONV_WIDTH
SPLITS = (ATTN_WIDTH,
          ATTN_WIDTH + KV_WIDTH,
          ATTN_WIDTH + 2 * KV_WIDTH,
          ATTN_WIDTH + 2 * KV_WIDTH + CONV_WIDTH,
          ATTN_WIDTH + 2 * KV_WIDTH + 2 * CONV_WIDTH)
MIX_OUT_WIDTH = ATTN_WIDTH + CONV_WIDTH

POOL_SIZES = (2, 4, 8, 16)
N_POOL_GROUPS = len(POOL_SIZES)
POOL_GROUP = D_MODEL // N_POOL_GROUPS

N_EXPERTS = 16
N_EXPERT_GROUPS = 4
EXPERTS_PER_GROUP = N_EXPERTS // N_EXPERT_GROUPS
TOP_K = 2
EXPERT_FF = 256

kernel_name = "hybrid_swa_conv_pool_grouped_moe_adaln"

def rms_norm(x, g):
    xf = x.astype(jnp.float32)
    y = xf * lax.rsqrt(jnp.mean(xf * xf, axis=-1, keepdims=True) + EPS)
    return (y * g.astype(jnp.float32)).astype(x.dtype)

def alibi_slopes(n):
    return 2.0 ** (-8.0 * (jnp.arange(n, dtype=jnp.float32) + 1.0) / n)

def sliding_window_attention(q, k, v, sinks):
    b, s, _ = q.shape
    nb = s // BLOCK
    qb = q.reshape(b, nb, BLOCK, N_KV_HEADS, Q_PER_KV, HEAD_DIM).astype(jnp.float32)
    kb = k.reshape(b, nb, BLOCK, N_KV_HEADS, HEAD_DIM).astype(jnp.float32)
    vb = v.reshape(b, nb, BLOCK, N_KV_HEADS, HEAD_DIM).astype(jnp.float32)

    def with_prev(t):
        prev = jnp.pad(t, ((0, 0), (1, 0), (0, 0), (0, 0), (0, 0)))[:, :nb]
        return jnp.concatenate([prev, t], axis=2)

    kk, vv = with_prev(kb), with_prev(vb)
    scores = jnp.einsum('bnqkgd,bnskd->bnkgqs', qb, kk) * (HEAD_DIM ** -0.5)
    dist = (jnp.arange(BLOCK)[:, None] + BLOCK) - jnp.arange(2 * BLOCK)[None, :]
    in_window = (dist >= 0) & (dist < WINDOW)
    has_prev = (jnp.arange(nb)[:, None, None] > 0) | (jnp.arange(2 * BLOCK) >= BLOCK)[None, None, :]
    mask = in_window[None] & has_prev
    slopes = alibi_slopes(N_HEADS).reshape(N_KV_HEADS, Q_PER_KV)
    scores = scores - slopes[:, :, None, None] * dist.astype(jnp.float32)
    scores = jnp.where(mask[None, :, None, None], scores, -jnp.inf)
    sink = sinks.astype(jnp.float32).reshape(N_KV_HEADS, Q_PER_KV)[None, None, :, :, None]
    m = jnp.maximum(scores.max(axis=-1), sink)
    p = jnp.exp(scores - m[..., None])
    denom = p.sum(axis=-1) + jnp.exp(sink - m)
    out = jnp.einsum('bnkgqs,bnskd->bnqkgd', p, vv)
    out = out / jnp.transpose(denom, (0, 1, 4, 2, 3))[..., None]
    return out.reshape(b, s, ATTN_WIDTH).astype(q.dtype)

def short_conv_mixer(b_gate, c_gate, xv, w):
    u = c_gate * xv
    y = lax.conv_general_dilated(u, w[:, None, :].astype(u.dtype), window_strides=(1,),
                                 padding=[(CONV_K - 1, 0)],
                                 dimension_numbers=('NWC', 'WIO', 'NWC'),
                                 feature_group_count=CONV_WIDTH)
    return b_gate * y

def multiscale_pool_mixer(h, w_pool, scale):
    b, s, d = h.shape
    hf = h.astype(jnp.float32)
    csum = jnp.cumsum(hf, axis=1)
    pos = jnp.arange(1, s + 1, dtype=jnp.float32)
    outs = []
    for g, w in enumerate(POOL_SIZES):
        sl = slice(g * POOL_GROUP, (g + 1) * POOL_GROUP)
        cg = csum[..., sl]
        lag = jnp.pad(cg, ((0, 0), (w, 0), (0, 0)))[:, :s]
        mean = (cg - lag) / jnp.minimum(pos, float(w))[None, :, None]
        outs.append(mean - hf[..., sl])
    pooled = jnp.stack(outs, axis=2)
    mixed = jnp.einsum('bsgc,gce->bsge', pooled, w_pool.astype(jnp.float32)).reshape(b, s, d)
    return (mixed * scale.astype(jnp.float32)).astype(h.dtype)

def grouped_moe(h, w_router, b_router, w_gate, w_up, w_down):
    b, s, d = h.shape
    t = h.reshape(b * s, d)
    scores = jax.nn.sigmoid(jnp.dot(t.astype(jnp.float32), w_router.astype(jnp.float32)))
    biased = (scores + b_router.astype(jnp.float32)).reshape(-1, N_EXPERT_GROUPS, EXPERTS_PER_GROUP)
    group_score = lax.top_k(biased, TOP_K)[0].sum(axis=-1)
    best_group = jnp.argmax(group_score, axis=-1)
    in_group = best_group[:, None] == jnp.arange(N_EXPERT_GROUPS)[None, :]
    masked = jnp.where(in_group[:, :, None], biased, -jnp.inf).reshape(-1, N_EXPERTS)
    _, idx = lax.top_k(masked, TOP_K)
    wts = jnp.take_along_axis(scores, idx, axis=-1)
    wts = wts / wts.sum(axis=-1, keepdims=True)
    gates = jnp.sum(jax.nn.one_hot(idx, N_EXPERTS, dtype=jnp.float32) * wts[..., None], axis=1)
    out = jnp.zeros((b * s, d), jnp.float32)
    for e in range(N_EXPERTS):
        hid = jax.nn.silu(t @ w_gate[e]) * (t @ w_up[e])
        out = out + gates[:, e:e + 1] * (hid @ w_down[e]).astype(jnp.float32)
    return out.reshape(b, s, d).astype(h.dtype)

def setup_inputs(seed: int = 0) -> dict:
    key = jax.random.key(seed)
    ks = jax.random.split(key, 20)
    f32 = jnp.float32
    nrm = lambda k, shape, sc: jax.random.normal(k, shape, f32) * sc
    return {
        "x": nrm(ks[0], (BATCH, SEQ, D_MODEL), 1.0),
        "c": nrm(ks[1], (BATCH, D_MODEL), 1.0),
        "w_ada": nrm(ks[2], (DEPTH, D_MODEL, N_MOD * D_MODEL), 0.5 * D_MODEL ** -0.5),
        "b_ada": nrm(ks[3], (DEPTH, N_MOD * D_MODEL), 0.02),
        "norm_mix": 1.0 + nrm(ks[4], (DEPTH, D_MODEL), 0.05),
        "norm_ffn": 1.0 + nrm(ks[5], (DEPTH, D_MODEL), 0.05),
        "w_in": nrm(ks[6], (N_EVEN, D_MODEL, IN_WIDTH), D_MODEL ** -0.5),
        "w_out": nrm(ks[7], (N_EVEN, MIX_OUT_WIDTH, D_MODEL), MIX_OUT_WIDTH ** -0.5),
        "sinks": nrm(ks[8], (N_EVEN, N_HEADS), 0.5),
        "conv_w": nrm(ks[9], (N_EVEN, CONV_K, CONV_WIDTH), CONV_K ** -0.5),
        "w_pool": nrm(ks[10], (N_ODD, N_POOL_GROUPS, POOL_GROUP, POOL_GROUP), POOL_GROUP ** -0.5),
        "pool_scale": 1.0 + nrm(ks[11], (N_ODD, D_MODEL), 0.1),
        "w_router": nrm(ks[12], (D_MODEL, N_EXPERTS), D_MODEL ** -0.5),
        "b_router": nrm(ks[13], (N_EXPERTS,), 0.01),
        "w_gate": nrm(ks[14], (DEPTH, N_EXPERTS, D_MODEL, EXPERT_FF), D_MODEL ** -0.5),
        "w_up": nrm(ks[15], (DEPTH, N_EXPERTS, D_MODEL, EXPERT_FF), D_MODEL ** -0.5),
        "w_down": nrm(ks[16], (DEPTH, N_EXPERTS, EXPERT_FF, D_MODEL), EXPERT_FF ** -0.5),
        "norm_final": 1.0 + nrm(ks[17], (D_MODEL,), 0.05),
    }

def reference(x, c, w_ada, b_ada, norm_mix, norm_ffn, w_in, w_out, sinks, conv_w,
              w_pool, pool_scale, w_router, b_router, w_gate, w_up, w_down, norm_final):
    cond = jax.nn.silu(c)
    h = x
    for layer in range(DEPTH):
        mod = cond @ w_ada[layer] + b_ada[layer]
        sh1, sc1, g1, sh2, sc2, g2 = [m[:, None, :] for m in jnp.split(mod, N_MOD, axis=-1)]
        u = rms_norm(h, norm_mix[layer]) * (1 + sc1) + sh1
        j = layer // 2
        if layer % 2 == 0:
            proj = u @ w_in[j]
            q, k, v, bg, cg, xv = jnp.split(proj, SPLITS, axis=-1)
            attn = sliding_window_attention(q, k, v, sinks[j])
            conv = short_conv_mixer(bg, cg, xv, conv_w[j])
            mix = jnp.concatenate([attn, conv], axis=-1) @ w_out[j]
        else:
            mix = multiscale_pool_mixer(u, w_pool[j], pool_scale[j])
        h = h + g1 * mix
        u = rms_norm(h, norm_ffn[layer]) * (1 + sc2) + sh2
        h = h + g2 * grouped_moe(u, w_router, b_router, w_gate[layer], w_up[layer], w_down[layer])
    return rms_norm(h, norm_final)


_drawn_inputs = setup_inputs


def setup_inputs(seed=0):
    import zlib

    import numpy as np

    out = dict(_drawn_inputs(seed))
    spreads = {}
    factors = {'sinks': 3.131}
    for name, (base, spread) in spreads.items():
        noise = np.random.default_rng([zlib.crc32(name.encode()), seed]).standard_normal(out[name].shape)
        drawn = base * np.exp(spread * noise) if base else spread * noise
        out[name] = __import__('jax').numpy.asarray(drawn.astype(out[name].dtype))
    for name, factor in factors.items():
        out[name] = (out[name] * factor).astype(out[name].dtype)
    return out
```

```python
from contextlib import ExitStack

import concourse.bass as bass
from concourse import mybir

F32 = mybir.dt.float32
BF16 = mybir.dt.bfloat16
I32 = mybir.dt.int32
U32 = mybir.dt.uint32
ALU = mybir.AluOpType
ACT = mybir.ActivationFunctionType
AX = mybir.AxisListType

P = 128
SEQ, D = 512, 1024
T = SEQ // P
KD = D // P
LAYERS = 2
EPS = 1e-6
MODW = 6 * D
AC = 384
NCH = MODW // AC
N_FIRST = 6
IN_W = 2304
HD, HEADS, KVH = 64, 8, 2
GH = HEADS // KVH
AW = HEADS * HD
K0, V0, B0, C0, X0 = AW, AW + 128, AW + 256, AW + 256 + 512, AW + 256 + 1024
CC = 4
E, EG, EPG, FF = 16, 4, 4, 256
NSLOT = 4
FAR = 4096.0
HEAD_AT = [[kv * GH + 2 * (g % 2) + g // 2 for g in range(GH)] for kv in range(KVH)]
ATT_U = T * KVH
ROUNDS = SEQ // P - 1

C_ID, C_BEF, C_DIST, C_SLOT, C_ONE, C_INV, C_TOK, C_JLT, C_FST, C_END = (
    0, 128, 256, 512, 640, 768, 784, 792, 808, 812)


def trunk(nc, x, c, w_ada, b_ada, norm_mix, norm_ffn, w_in, w_out, sinks, conv_w, w_pool, pool_scale,
          w_router, b_router, w_gate, w_up, w_down, norm_final, consts, out, mod_dram, xhat_dram, y_dram):
    ctx = ExitStack()
    with ctx:
        ctx.enter_context(nc.allow_non_contiguous_dma(reason="vectors of 1024 channels, 128k + p at partition p"))

        def sb(name, shape, dt=F32):
            return ctx.enter_context(nc.sbuf_tensor(name, shape, dt))

        def sem(name):
            return ctx.enter_context(nc.semaphore(name))

        h = sb("h", [P, T, D])
        xu = sb("xu", [P, 2 * T * D])
        xhat = xu[:, 0:T * D].rearrange("p (t d) -> p t d", t=T)
        uT = xu[:, T * D:2 * T * D].rearrange("p (k s) -> p k s", k=KD)
        cuT = xu[:, 0:CC * SEQ].rearrange("p (c s) -> p c s", c=CC)
        wo_att = xu[:, 0:4 * D].rearrange("p (c n) -> p c n", c=4)
        wo_conv = xu[:, 4 * D:8 * D].rearrange("p (c n) -> p c n", c=4)
        SLOT = 3 * KD * FF
        ring = sb("ring", [P, 3 * SLOT])
        win = ring[:, 0:KD * IN_W].rearrange("p (k n) -> p k n", k=KD)

        def wslot(j):
            return ring[:, j * SLOT:(j + 1) * SLOT] if j < 3 else xu[:, 0:SLOT]

        def w_gu(j):
            return wslot(j)[:, 0:2 * KD * FF].rearrange("p (a k f) -> p a k f", a=2, k=KD)

        def w_dn(j):
            return wslot(j)[:, 2 * KD * FF:SLOT].rearrange("p (a d) -> p a d", a=2)

        adaw = sb("adaw", [P, 2, KD, AC])
        wpool = adaw[:, 0].rearrange("p k n -> p (k n)")[:, 0:KD * 256].rearrange("p (a n) -> p a n", a=KD)
        acc = sb("acc", [P, 2, 2, AC])
        brow = sb("brow", [1, 2, AC])
        mrow = sb("mrow", [1, 2, AC])
        gbc = sb("gbc", [P, D])
        cst = sb("cst", [P, C_END])
        ident, before = cst[:, C_ID:C_ID + P], cst[:, C_BEF:C_BEF + P]
        ones = cst[:, C_ONE:C_ONE + P]

        WORK = 42 * 256
        work = sb("work", [P, WORK])
        at = [0]

        def take(n):
            at[0] += n
            assert at[0] <= WORK, at[0]
            return work[:, at[0] - n:at[0]]

        convT = take(CC * SEQ).rearrange("p (c s) -> p c s", c=CC)
        attnT = take(4 * SEQ).rearrange("p (c s) -> p c s", c=4)
        qT = take(4 * SEQ).rearrange("p (c s) -> p c s", c=4)
        kT = take(SEQ)
        kswap = take(SEQ)
        vtok = take(SEQ).rearrange("p (t n) -> p t n", t=T)
        prob = take(2 * GH * 256).rearrange("p (b h s) -> p b h s", b=2, h=GH)
        probT = take(2 * GH * P).rearrange("p (b n) -> p b n", b=2)
        at[0] = 0
        xg = take(4 * D).rearrange("p (b d) -> p b d", b=4)
        xgT = take(2 * D).rearrange("p (b k s) -> p b k s", b=2, k=KD)
        yrow = take(4 * D).rearrange("p (b d) -> p b d", b=4)[:, 0:2]
        at[0] -= 2 * D
        sil = take(2 * FF).rearrange("p (b f) -> p b f", b=2)
        hid = take(2 * FF).rearrange("p (b f) -> p b f", b=2)
        hT = take(2 * P).rearrange("p (a s) -> p a s", a=2)
        tok_i = take(E).bitcast(U32)
        dst_i = take(E).bitcast(U32)
        gslot = take(E)
        posm = take(T * E).rearrange("p (t e) -> p t e", t=T)
        rtab = take(T * E * 3).bitcast(BF16).rearrange("p (t e c) -> p t e c", t=T, e=E)
        ovtab = take(8)
        ovtok, ovdst = take(1).bitcast(U32), take(1).bitcast(U32)
        ovgate = take(1)
        ovr = take(T * 3).bitcast(BF16).rearrange("p (t c) -> p t c", t=T)
        onehot_ov = yrow[:, 1, 0:T * P // 2].bitcast(BF16).rearrange("p (t s) -> p t s", t=T)
        onehot = yrow.rearrange("p b d -> p (b d)").bitcast(BF16).rearrange(
            "p (b t e s) -> p b t e s", b=2, t=T, e=EPG)
        small = xgT.rearrange("p b k s -> p (b k s)")
        ycomb = work[:, 0:8 * D].rearrange("p (t a d) -> p t a d", t=T, a=2)
        pooled = work[:, 0:4 * D].rearrange("p (k s) -> p k s", k=KD)
        run = work[:, 4 * D:6 * D].rearrange("p (b k s) -> p b k s", b=2, k=2)
        psc = work[:, 6 * D:7 * D]
        junk = work[:, 10 * D:10 * D + D // 2].bitcast(BF16)
        mixt = work[:, 8 * D:10 * D].rearrange("p (b d) -> p b d", b=2)

        sel_tile = sb("sel_tile", [P, T * E])[:, :]
        sig_tile = sb("sig_tile", [P, T * E])[:, :]
        cond = sb("cond", [P, KD])
        craw = sb("craw", [P, KD])
        modc = sb("modc", [P, 4, 2, KD])
        normc = sb("normc", [P, 4, KD])
        scl = sb("scl", [P, 4, KD])
        wr = sb("wr", [P, KD, E])
        brb = sb("brb", [P, E])
        snk = sb("snk", [P, 2, HEADS])
        cvw = sb("cvw", [P, 3, CC])
        eps = sb("eps", [P, 1])
        ss = sb("ss", [P, T])
        rstd = sb("rstd", [P, T])
        sm = sb("sm", [P, 2, 6, GH])
        flag = sb("flag", [P, LAYERS], I32)
        maxn = sb("maxn", [P, LAYERS])

        psA = ctx.enter_context(nc.psum_tensor("psA", [P, 1024], F32))
        ps2 = ctx.enter_context(nc.psum_tensor("ps2", [P, 512], F32))
        ps3 = ctx.enter_context(nc.psum_tensor("ps3", [P, 512], F32))
        ps4 = ctx.enter_context(nc.psum_tensor("ps4", [P, 512], F32))
        ps5 = ctx.enter_context(nc.psum_tensor("ps5", [P, 512], F32))
        psY = ctx.enter_context(nc.psum_tensor("psY", [P, 1024], F32))
        pair = [psY, psA]
        gu_ps = [ps3, ps4]

        const_in = sem("const_in")
        x_in = sem("x_in")
        c_in, small_in, psc_in = sem("c_in"), sem("small_in"), sem("psc_in")
        eps_ready = sem("eps_ready")
        ada_in = [sem(f"ada_in{b}") for b in range(2)]
        win_in = [sem(f"win_in{b}") for b in range(2)]
        wout_in = sem("wout_in")
        wpool_in = sem("wpool_in")
        gu_in = [sem(f"gu_in{j}") for j in range(NSLOT)]
        dn_in = [sem(f"dn_in{j}") for j in range(NSLOT)]
        cond_ready = sem("cond_ready")
        mac_step = sem("mac_step")
        ada_mac = sem("ada_mac")
        ada_sum = sem("ada_sum")
        row_copied = sem("row_copied")
        mod_stored = [sem(f"mod_stored{b}") for b in range(2)]
        modc_in = [sem(f"modc_in{s}") for s in range(4)]
        gbc_in = sem("gbc_in")
        scl_ready = sem("scl_ready")
        sq_done = sem("sq_done")
        std_done = sem("std_done")
        xhat_ready = sem("xhat_ready")
        xhat_stored = sem("xhat_stored")
        uT_banked = sem("uT_banked")
        uT_act, uT_dve = sem("uT_act"), sem("uT_dve")
        h_ready = sem("h_ready")
        link_dve = sem("link_dve")
        link_act = sem("link_act")
        proj_ready = sem("proj_ready")
        kswap_in = sem("kswap_in")
        proj_act, proj_dve = sem("proj_act"), sem("proj_dve")
        scores_ready, scores_read = sem("scores_ready"), sem("scores_read")
        negmax_ready, exp_done = sem("negmax_ready"), sem("exp_done")
        rden_ready, prob_ready = sem("rden_ready"), sem("prob_ready")
        probT_banked, probT_ready = sem("probT_banked"), sem("probT_ready")
        att_banked, att_ready = sem("att_banked"), sem("att_ready")
        mix_banked = sem("mix_banked")
        pooled_ready = sem("pooled_ready")
        logits_ready, sig_ready = sem("logits_ready"), sem("sig_ready")
        sel_ready, pos_ready = sem("sel_ready"), sem("pos_ready")
        onehot_ready, table_banked, table_ready = sem("onehot_ready"), sem("table_banked"), sem("table_ready")
        flag_ready = sem("flag_ready")
        xg_clear = sem("xg_clear")
        xg_in = [sem(f"xg_in{j}") for j in range(4)]
        xT_banked, xT_act, xT_dve = sem("xT_banked"), sem("xT_act"), sem("xT_dve")
        gu_done, sil_ready, hid_ready = sem("gu_done"), sem("sil_ready"), sem("hid_ready")
        hT_banked, hT_ready = sem("hT_banked"), sem("hT_ready")
        dn_done, y_ready = sem("dn_done"), sem("y_ready")
        y_out = [sem(f"y_out{j}") for j in range(2)]
        y_in = [sem(f"y_in{j}") for j in range(T)]
        y_summed = sem("y_summed")
        out_ready, out_stored = sem("out_ready"), sem("out_stored")
        ov_w = [sem(f"ov_w{l}") for l in range(LAYERS)]
        ov_oh = [sem(f"ov_oh{l}") for l in range(LAYERS)]
        ov_link = [sem(f"ov_link{l}") for l in range(LAYERS)]
        ov_tab = [sem(f"ov_tab{l}") for l in range(LAYERS)]
        ov_idx = [sem(f"ov_idx{l}") for l in range(LAYERS)]
        ov_xg = [sem(f"ov_xg{l}") for l in range(LAYERS)]
        ov_xb = [sem(f"ov_xb{l}") for l in range(LAYERS)]
        ov_xT = [sem(f"ov_xT{l}") for l in range(LAYERS)]
        ov_gu = [sem(f"ov_gu{l}") for l in range(LAYERS)]
        ov_sil = [sem(f"ov_sil{l}") for l in range(LAYERS)]
        ov_hid = [sem(f"ov_hid{l}") for l in range(LAYERS)]
        ov_hb = [sem(f"ov_hb{l}") for l in range(LAYERS)]
        ov_hT = [sem(f"ov_hT{l}") for l in range(LAYERS)]
        ov_dn = [sem(f"ov_dn{l}") for l in range(LAYERS)]
        ov_y = [sem(f"ov_y{l}") for l in range(LAYERS)]
        ov_out = [sem(f"ov_out{l}") for l in range(LAYERS)]

        N_SMALL = 11

        PROJ = [("q", i) for i in range(4)] + [("k", 0), ("v", 0)] + [(n, i) for i in range(CC) for n in "cxb"]
        ACT_SIDE = {"q", "k", "v", "c"}
        act_before = [sum(n in ACT_SIDE for n, _ in PROJ[:m]) for m in range(len(PROJ) + 1)]
        BESIDE = [([6], [7]), ([8], []), ([9], [10]), ([11], []), ([12], [13]), ([14], []), ([15], [16]), ([17], []),
                  ([], [])]

        def mod_waits(eng, n):
            for q in (n, n - 1):
                eng.wait_ge(mod_stored[q % 2], 16 * (q // 2 + 1))

        def loop_experts(eng, body, last=E):
            with eng.Fori(0, E // 4 - 1) as i:
                for j in range(4):
                    body(4 * i + j, j, i)
            for j in range(4):
                if E - 4 + j < last:
                    body(E - 4 + j, j, E // 4 - 1)

        block = ctx.enter_context(nc.Block())

        def overflow_sync(sp, l):
            sp.wait_ge(dn_done, E * (l + 1))
            sp.wait_ge(flag_ready, l + 1)
            most = sp.value_load(flag[0:1, l:l + 1], min_val=0, max_val=SEQ)
            with sp.If(most > P):
                with sp.Fori(0, ROUNDS) as r:
                    with sp.Fori(0, E) as e:
                        n = r * E + e
                        gate = w_gate[l, bass.ds(e, 1)].rearrange("a (p k) f -> p (a k f)", k=KD)
                        up = w_up[l, bass.ds(e, 1)].rearrange("a (p k) f -> p (a k f)", k=KD)
                        down = w_down[l, bass.ds(e, 1)].rearrange("a (p c) d -> p (a c d)", c=2)
                        for s in (gate, up, down):
                            sp.lower_ap_dma(s)
                        sp.wait_ge(ov_dn[l], n)
                        sp.dma_start(wslot(0)[:, 0:KD * FF], gate).then_inc(ov_w[l], 16)
                        sp.dma_start(wslot(0)[:, KD * FF:2 * KD * FF], up).then_inc(ov_w[l], 16)
                        sp.dma_start(wslot(0)[:, 2 * KD * FF:SLOT], down).then_inc(ov_w[l], 16)
                sp.wait_ge(ov_out[l], 16 * ROUNDS * E)

        @block.sync
        def _(sp):
            def load_ada(n):
                b = n % 2
                if isinstance(n, int):
                    if n >= 2:
                        sp.wait_ge(ada_mac, n - 1)
                        sp.wait_ge(ada_sum, n - 1)
                    l, q = n // NCH, n % NCH
                    src = w_ada[l, :, q * AC:(q + 1) * AC].rearrange("(p k) n -> p k n", k=KD)
                    row = b_ada[l:l + 1, q * AC:(q + 1) * AC]
                    sp.dma_start(adaw[:, b], src).then_inc(ada_in[b], 16)
                    sp.dma_start(brow[0:1, b, :], row).then_inc(ada_in[b], 16)

            def load_ada_1(q, b):
                src = w_ada[1, :, bass.ds(q * AC, AC)].rearrange("(p k) n -> p k n", k=KD)
                row = b_ada[1:2, bass.ds(q * AC, AC)]
                if not isinstance(q, int):
                    sp.lower_ap_dma(src)
                    sp.lower_ap_dma(row)
                sp.wait_ge(ada_sum, NCH + q - 1)
                sp.dma_start(adaw[:, b], src).then_inc(ada_in[b], 16)
                sp.dma_start(brow[0:1, b, :], row).then_inc(ada_in[b], 16)

            def load_expert(l, e, j):
                gate = w_gate[l, bass.ds(e, 1)].rearrange("a (p k) f -> p (a k f)", k=KD)
                up = w_up[l, bass.ds(e, 1)].rearrange("a (p k) f -> p (a k f)", k=KD)
                down = w_down[l, bass.ds(e, 1)].rearrange("a (p c) d -> p (a c d)", c=2)
                if not isinstance(e, int):
                    for s in (gate, up, down):
                        sp.lower_ap_dma(s)
                if isinstance(e, int) and l * E + e < NSLOT:
                    pass
                else:
                    sp.wait_ge(dn_done, l * E + e - 3)
                flat = wslot(j)
                sp.dma_start(flat[:, 0:KD * FF], gate).then_inc(gu_in[j], 16)
                sp.dma_start(flat[:, KD * FF:2 * KD * FF], up).then_inc(gu_in[j], 16)
                sp.dma_start(flat[:, 2 * KD * FF:SLOT], down).then_inc(dn_in[j], 16)

            for n in range(N_FIRST):
                load_ada(n)
            for n in range(N_FIRST, NCH + 1):
                load_ada(n)
            sp.wait_ge(proj_ready, len(PROJ))
            sp.wait_ge(proj_dve, len(PROJ) - act_before[-1])
            sp.dma_start(wo_conv, w_out[0, AW:, :].rearrange("(c p) n -> p c n", p=P)).then_inc(wout_in, 16)
            sp.dma_start(wo_att, w_out[0, 0:AW, :].rearrange("(c p) n -> p c n", p=P)).then_inc(wout_in, 16)
            for e in range(3):
                load_expert(0, e, e)
            for l in range(LAYERS):
                for t in range(T):
                    sp.wait_ge(xhat_ready, (2 * l + 1) * T + t + 1)
                    sp.dma_start(xhat_dram[l][t * P:(t + 1) * P, :], xhat[:, t, :]).then_inc(xhat_stored, 16)
                if l == 0:
                    load_ada_1(1, 1)
                sp.wait_ge(xhat_stored, 16 * T * (l + 1))
                sp.wait_ge(logits_ready, l + 1)
                load_expert(l, 3, 3)
                with sp.Fori(1, E // 4) as i:
                    for j in range(4):
                        if l == 0:
                            load_ada_1(4 * i + j - 2, j % 2)
                        load_expert(l, 4 * i + j, j)
                if l == 0:
                    load_ada_1(NCH - 2, 0)
                    load_ada_1(NCH - 1, 1)
                    sp.wait_ge(ada_mac, 2 * NCH - 1)
                    sp.dma_start(wpool, w_pool[0].rearrange("g (c p) n -> p (g c) n", p=P)).then_inc(wpool_in, 16)
                overflow_sync(sp, l)
                for j in range(2):
                    sp.wait_ge(y_out[j], 16 * (E // 2) * (l + 1))
                sp.wait_ge(dn_done, E * (l + 1))
                for t in range(T):
                    for a in range(2):
                        sp.dma_start(ycomb[:, t, a, :], y_dram[l][a * SEQ + t * P:a * SEQ + (t + 1) * P, :]
                                     ).then_inc(y_in[t], 16)
                if l == 0:
                    for e in range(3):
                        load_expert(1, e, e)
            for t in range(T):
                sp.wait_ge(out_ready, t + 1)
                sp.dma_start(out[0, t * P:(t + 1) * P, :], xhat[:, t, :]).then_inc(out_stored, 16)
            sp.wait_ge(out_stored, 16 * T)

        @block.gpsimd
        def _(pool):
            def load_cols(s, last_chunk):
                l, half = s // 2, s % 2
                mod_waits(pool, l * NCH + last_chunk)
                off = 3 * half * D
                for a in range(2):
                    src = mod_dram[l, off + a * D:off + (a + 1) * D]
                    src = src.rearrange("(k p) -> p k", p=P) if s == 2 else src.rearrange("(p k) -> p k", k=KD)
                    pool.dma_start(modc[:, s, a, :], src).then_inc(modc_in[s], 16)

            def load_gate(l, half):
                off = (3 * half + 2) * D
                mod_waits(pool, l * NCH + ((off + D - 1) // AC))
                pool.dma_start(gbc[:, :], mod_dram[l:l + 1, off:off + D].partition_broadcast(P)
                               .rearrange("p a d -> p (a d)")).then_inc(gbc_in, 16)

            load_cols(0, N_FIRST - 1)
            load_gate(0, 0)
            for u in range(ATT_U):
                b = u // KVH
                pool.wait_ge(rden_ready, u + 1)
                lo = 0 if b else P
                part = prob[:, u % 2, :, lo:]
                pool.tensor_tensor(part, part, sm[:, u % 2, 4, :].unsqueeze(2).broadcast_to([P, GH, 256 - lo]),
                                   ALU.mult).then_inc(prob_ready, 1)
            for l in range(LAYERS):
                load_cols(2 * l + 1, (5 * D - 1) // AC)
                pool.wait_ge(h_ready, (2 * l + 1) * T)
                load_gate(l, 1)
                pool.memset(xg[:, :, :], 0.0).then_inc(xg_clear, 1)
                pool.wait_ge(xg_clear, l + 1)
                pool.wait_ge(xhat_stored, 16 * T * (l + 1))

                def scatter(e):
                    pool.wait_ge(y_ready, l * E + e + 1)
                    pool.indirect_dma_start(
                        out=y_dram[l], out_offset=bass.IndirectOffsetOnAxis(dst_i[:, e:e + 1], 0),
                        in_=yrow[:, e % 2, :], in_offset=None, bounds_check=2 * SEQ - 1, oob_is_err=False
                    ).then_inc(y_out[e % 2], 16)

                for e in range(E):
                    if e % EPG == 0:
                        pool.wait_ge(table_ready, l * EG + e // EPG + 1)
                    if e >= 4:
                        pool.wait_ge(xT_banked, l * E + e - 3)
                    pool.indirect_dma_start(
                        out=xg[:, e % 4, :], out_offset=None, in_=xhat_dram[l],
                        in_offset=bass.IndirectOffsetOnAxis(tok_i[:, e:e + 1], 0),
                        bounds_check=SEQ - 1, oob_is_err=False).then_inc(xg_in[e % 4], 16)
                    if e >= 3:
                        scatter(e - 3)
                for e in range(E - 3, E):
                    scatter(e)
                for j in range(2):
                    pool.wait_ge(y_out[j], 16 * (E // 2) * (l + 1))

                pool.wait_ge(flag_ready, l + 1)
                most = pool.value_load(flag[0:1, l:l + 1], min_val=0, max_val=SEQ)
                bound, zero = pool.alloc_register(f"bound{l}"), pool.to_reg(0)
                with pool.If(most > P):
                    with pool.Fori(0, ROUNDS * E) as n:
                        pool.wait_ge(ov_idx[l], n + 1)
                        pool.reg_add(bound, zero, SEQ - 1)
                        pool.indirect_dma_start(
                            out=xg[:, 0, :], out_offset=None, in_=xhat_dram[l],
                            in_offset=bass.IndirectOffsetOnAxis(ovtok[:, 0:1], 0),
                            bounds_check=bound, oob_is_err=False).then_inc(ov_xg[l], 16)
                        pool.wait_ge(ov_y[l], n + 1)
                        pool.reg_add(bound, zero, 2 * SEQ - 1)
                        pool.indirect_dma_start(
                            out=y_dram[l], out_offset=bass.IndirectOffsetOnAxis(ovdst[:, 0:1], 0),
                            in_=yrow[:, 0, :], in_offset=None, bounds_check=bound, oob_is_err=False
                        ).then_inc(ov_out[l], 16)

                for t in range(T):
                    pool.wait_ge(y_in[t], 32 * (l + 1))
                    pool.tensor_tensor(ycomb[:, t, 0, :], ycomb[:, t, 0, :], ycomb[:, t, 1, :], ALU.add
                                       ).then_inc(y_summed, 1)
                if l == 0:
                    load_cols(2, N_FIRST - 1)
                    load_gate(1, 0)
                    pool.wait_ge(h_ready, 2 * T)
                    pool.dma_start(psc, pool_scale.partition_broadcast(P).rearrange("p a d -> p (a d)")
                                   ).then_inc(psc_in, 16)
            pool.dma_start(gbc[:, :], norm_final.rearrange("(a d) -> a d", a=1).partition_broadcast(P)
                           .rearrange("p a d -> p (a d)")).then_inc(gbc_in, 16)

        @block.scalar
        def _(act):
            alink = [0]

            def link(ins):
                alink[0] += 1
                ins.then_inc(link_act, 1)
                act.wait_ge(link_act, alink[0])

            act.dma_start(craw[:, :], c[0].rearrange("(p k) -> p k", k=KD)).then_inc(c_in, 16)
            act.dma_start(cst[:, :], consts).then_inc(const_in, 16)
            for t in range(T):
                act.dma_start(h[:, t, :], x[0, t * P:(t + 1) * P, :]).then_inc(x_in, 16)
            for s in range(4):
                src = (norm_ffn if s % 2 else norm_mix)[s // 2]
                src = src.rearrange("(k p) -> p k", p=P) if s == 2 else src.rearrange("(p k) -> p k", k=KD)
                act.dma_start(normc[:, s, :], src).then_inc(small_in, 16)
            act.dma_start(wr[:, :, :], w_router.rearrange("(p k) e -> p k e", k=KD)).then_inc(small_in, 16)
            act.dma_start(brb[:, :], b_router.rearrange("(a e) -> a e", a=1).partition_broadcast(P)
                          .rearrange("p a e -> p (a e)")).then_inc(small_in, 16)
            for kv in range(KVH):
                for odd in range(2):
                    src = sinks[:, kv * GH + odd:(kv + 1) * GH:2].partition_broadcast(P).rearrange("p a e -> p (a e)")
                    act.dma_start(snk[:, 0, kv * GH + 2 * odd:kv * GH + 2 * odd + 2], src).then_inc(small_in, 16)
            act.dma_start(cvw[:, :, :], conv_w[0].rearrange("j (c p) -> p j c", p=P)).then_inc(small_in, 16)
            wsrc = w_in[0].rearrange("(p k) n -> p k n", k=KD)
            act.dma_start(win[:, :, 0:B0], wsrc[:, :, 0:B0]).then_inc(win_in[0], 16)
            act.dma_start(win[:, :, B0:IN_W], wsrc[:, :, B0:IN_W]).then_inc(win_in[1], 16)
            act.wait_ge(c_in, 16)
            act.activation(cond[:, :], craw[:, :], ACT.Silu).then_inc(cond_ready, 1)

            def ada_row(n, b, sent):
                act.wait_ge(ada_sum, n + 1)
                act.wait_ge(mod_stored[b], 16 * sent)
                act.activation(mrow[0:1, b, :], ps5[0:1, 0:AC], ACT.Copy).then_inc(row_copied, 1)

            def ada_store(n, b, dst):
                act.wait_ge(row_copied, n + 1)
                act.dma_start(dst, mrow[0:1, b, :]).then_inc(mod_stored[b], 16)

            def ada_out(n):
                l, q = n // NCH, n % NCH
                ada_row(n, n % 2, n // 2)
                ada_store(n, n % 2, mod_dram[l:l + 1, q * AC:(q + 1) * AC])

            def norm(s):
                for t in range(T):
                    if s == 0:
                        act.wait_ge(x_in, 16 * T)
                    else:
                        act.wait_ge(h_ready, (s - 1) * T + t + 1)
                    link(act.activation(junk, h[:, t, :], ACT.Square, accum_out=ss[:, t:t + 1]))
                act.wait_ge(eps_ready, 1)
                act.activation(rstd[:, :], ss[:, :], ACT.Sqrt, bias=eps[:, 0:1], scale=1.0 / D).then_inc(std_done, 1)

            def spread(s):
                for k in range(0, KD, 2):
                    if k == 0:
                        act.wait_ge(scl_ready, s + 1)
                    act.wait_ge(uT_banked, KD * s + k + 1)
                    act.activation(uT[:, k, :], psA[:, 0:512], ACT.Identity, scale=scl[:, s, k:k + 1],
                                   bias=modc[:, s, 0, k:k + 1]).then_inc(uT_act, 1)

            for n in range(N_FIRST):
                ada_out(n)
            norm(0)
            spread(0)

            def empty(m):
                name, i = PROJ[m]
                if name not in ACT_SIDE:
                    return
                act.wait_ge(proj_ready, m + 1)
                bank = psY[:, (m % 2) * 512:(m % 2 + 1) * 512]
                if name == "q":
                    dst = qT[:, i, :]
                elif name == "k":
                    dst = kT
                elif name == "v":
                    dst = vtok.rearrange("p t n -> p (t n)")
                else:
                    dst = cuT[:, i, :]
                act.activation(dst, bank, ACT.Copy).then_inc(proj_act, 1)
                if name == "k":
                    act.wait_ge(proj_act, act_before[m + 1])
                    act.dma_start(kswap[HD:P], kT[0:HD]).then_inc(kswap_in, 16)
                    act.dma_start(kswap[0:HD], kT[HD:P]).then_inc(kswap_in, 16)

            def exps(u):
                b, pb = u // KVH, u % 2
                act.wait_ge(negmax_ready, u + 1)
                lo = 0 if b else P
                for g in range(GH):
                    act.activation(prob[:, pb, g, lo:], prob[:, pb, g, lo:], ACT.Exp, scale=HD ** -0.5,
                                   bias=sm[:, pb, 1, g:g + 1], accum_out=sm[:, pb, 2, g:g + 1])
                act.activation(sm[:, pb, 3, :], sm[:, pb, 5, :], ACT.Exp).then_inc(exp_done, 1)

            def empty_probT(u):
                b = u // KVH
                act.wait_ge(probT_banked, u + 1)
                if u:
                    act.wait_ge(att_banked, u)
                if b:
                    act.activation(probT[:, 0, :], ps2[:, :], ACT.Copy)
                act.activation(probT[:, 1, :], ps3[:, :], ACT.Copy).then_inc(probT_ready, 1)

            def empty_att(b):
                act.wait_ge(att_banked, KVH * (b + 1))
                act.activation(attnT[:, :, b * P:(b + 1) * P], ps4[:, :].rearrange("p (c s) -> p c s", c=4),
                               ACT.Copy).then_inc(att_ready, 1)

            for m in range(6):
                empty(m)
                ada_out(N_FIRST + m)
            for u in range(ATT_U + 1):
                if u < ATT_U:
                    exps(u)
                for m in BESIDE[u][0]:
                    empty(m)
                if u:
                    empty_probT(u - 1)
                for m in BESIDE[u][1]:
                    empty(m)
                if u and u % KVH == 0:
                    empty_att(u // KVH - 1)
                if u < 4:
                    ada_out(12 + u)

            def expert_loop(l):
                def xT_half(e, j, i):
                    act.wait_ge(xT_banked, l * E + e + 1)
                    for k in range(KD // 2):
                        ins = act.activation(xgT[:, j % 2, k, :], psA[:, k * P:(k + 1) * P], ACT.Identity,
                                             scale=scl[:, 2 * l + 1, k:k + 1], bias=modc[:, 2 * l + 1, 0, k:k + 1])
                    ins.then_inc(xT_act, 1)

                def silu(e, j, i):
                    act.wait_ge(gu_done, l * E + e + 1)
                    act.activation(sil[:, j % 2, :], gu_ps[j % 2][:, 0:FF], ACT.Silu).then_inc(sil_ready, 1)

                def body(e, j, i):
                    static = isinstance(e, int)
                    if not static or e + 1 < E:
                        act.wait_ge(hid_ready, l * E + e)
                        silu(e + 1, j + 1, i)
                    act.wait_ge(hT_banked, l * E + e + 1)
                    act.wait_ge(dn_done, l * E + e)
                    act.activation(hT.rearrange("p a s -> p (a s)"), ps2[:, 0:2 * P], ACT.Copy).then_inc(hT_ready, 1)
                    if not static or e + 2 < E:
                        act.wait_ge(gu_done, l * E + e + 1)
                        xT_half(e + 2, j, i)
                    if l == 0:
                        ada_row(NCH + e, j % 2, NCH // 2 + 2 * i + j // 2)
                        ada_store(NCH + e, j % 2, mod_dram[1:2, bass.ds(e * AC, AC)])

                act.wait_ge(table_ready, EG * (l + 1))
                xT_half(0, 0, 0)
                xT_half(1, 1, 0)
                silu(0, 0, 0)
                loop_experts(act, body)

                act.wait_ge(flag_ready, l + 1)
                most = act.value_load(flag[0:1, l:l + 1], min_val=0, max_val=SEQ)
                with act.If(most > P):
                    with act.Fori(0, ROUNDS * E) as n:
                        act.wait_ge(ov_xb[l], n + 1)
                        for k in range(KD):
                            ins = act.activation(xgT[:, 0, k, :], psA[:, k * P:(k + 1) * P], ACT.Identity,
                                                 scale=scl[:, 2 * l + 1, k:k + 1],
                                                 bias=modc[:, 2 * l + 1, 0, k:k + 1])
                        ins.then_inc(ov_xT[l], 1)
                        act.wait_ge(ov_gu[l], n + 1)
                        act.activation(sil[:, 0, :], ps3[:, 0:FF], ACT.Silu).then_inc(ov_sil[l], 1)
                        act.wait_ge(ov_hb[l], n + 1)
                        act.activation(hT.rearrange("p a s -> p (a s)"), ps2[:, 0:2 * P], ACT.Copy
                                       ).then_inc(ov_hT[l], 1)

            for l in range(LAYERS):
                if l:
                    norm(2)
                    spread(2)
                norm(2 * l + 1)
                spread(2 * l + 1)
                act.wait_ge(logits_ready, l + 1)
                act.activation(sig_tile, ps2[:, 0:T * E], ACT.Sigmoid).then_inc(sig_ready, 1)
                expert_loop(l)
            norm(4)

        @block.vector
        def _(dve):
            dlink = [0]

            def link(ins):
                dlink[0] += 1
                ins.then_inc(link_dve, 1)
                dve.wait_ge(link_dve, dlink[0])

            def ada_mul(n, b, used):
                dve.wait_ge(ada_in[b], 32 * (used + 1))
                if not isinstance(n, int) or n >= 2:
                    dve.wait_ge(ada_sum, n - 1)
                for k in range(KD):
                    part = acc[:, b, k % 2, :]
                    if k < 2:
                        ins = dve.tensor_scalar(part, adaw[:, b, k, :], cond[:, k:k + 1], None, ALU.mult)
                    else:
                        dve.wait_ge(mac_step, n * (KD - 2) + k - 1)
                        ins = dve.scalar_tensor_tensor(part, adaw[:, b, k, :], cond[:, k:k + 1], part,
                                                       ALU.mult, ALU.add)
                    if k < KD - 2:
                        ins.then_inc(mac_step, 1)
                    elif k == KD - 1:
                        ins.then_inc(ada_mac, 1)

            def norm(s):
                dve.wait_ge(std_done, s + 1)
                link(dve.reciprocal(rstd[:, :], rstd[:, :]))
                for t in range(T):
                    dve.tensor_scalar(xhat[:, t, :], h[:, t, :], rstd[:, t:t + 1], None, ALU.mult
                                      ).then_inc(xhat_ready, 1)

            def spread(s):
                dve.wait_ge(modc_in[s], 32)
                dve.scalar_tensor_tensor(scl[:, s, :], modc[:, s, 1, :], 1.0, normc[:, s, :], ALU.add, ALU.mult
                                         ).then_inc(scl_ready, 1)
                dve.wait_ge(scl_ready, s + 1)
                for k in range(1, KD, 2):
                    dve.wait_ge(uT_banked, KD * s + k + 1)
                    dve.tensor_scalar(uT[:, k, :], psA[:, 512:1024], scl[:, s, k:k + 1], modc[:, s, 0, k:k + 1],
                                      ALU.mult, ALU.add).then_inc(uT_dve, 1)

            def mix_in(l, t):
                dve.wait_ge(mix_banked, l * T + t + 1)
                link(dve.tensor_tensor(mixt[:, t % 2, :], pair[t % 2][:, :], gbc[:, :], ALU.mult))
                dve.tensor_tensor(h[:, t, :], h[:, t, :], mixt[:, t % 2, :], ALU.add).then_inc(h_ready, 1)

            def ffn_in(l, t):
                dve.wait_ge(y_summed, l * T + t + 1)
                dve.tensor_tensor(h[:, t, :], h[:, t, :], ycomb[:, t, 0, :], ALU.add).then_inc(h_ready, 1)

            dve.memset(eps[:, :], EPS).then_inc(eps_ready, 1)
            dve.wait_ge(cond_ready, 1)
            dve.wait_ge(const_in, 16)
            for n in range(N_FIRST):
                ada_mul(n, n % 2, n // 2)
            norm(0)
            dve.wait_ge(small_in, 16 * N_SMALL)
            spread(0)
            link(dve.tensor_scalar(snk[:, 1, :], snk[:, 0, :], HD ** 0.5, None, ALU.mult))

            def empty(m):
                name, i = PROJ[m]
                if name in ACT_SIDE:
                    return
                dve.wait_ge(proj_ready, m + 1)
                bank = psY[:, (m % 2) * 512:(m % 2 + 1) * 512]
                if name == "x":
                    dve.wait_ge(proj_act, act_before[m])
                    ins = dve.tensor_tensor(cuT[:, i, :], cuT[:, i, :], bank, ALU.mult)
                    ins.then_inc(proj_dve, 1)
                    dve.wait_ge(proj_dve, m - act_before[m] + 1)
                    link(dve.tensor_scalar(convT[:, i, :], cuT[:, i, :], cvw[:, 2, i:i + 1], None, ALU.mult))
                    for back in (1, 2):
                        link(dve.scalar_tensor_tensor(convT[:, i, back:], cuT[:, i, 0:SEQ - back],
                                                      cvw[:, 2 - back, i:i + 1], convT[:, i, back:],
                                                      ALU.mult, ALU.add))
                else:
                    dve.tensor_tensor(convT[:, i, :], convT[:, i, :], bank, ALU.mult).then_inc(proj_dve, 1)

            def soften(u):
                b, kv, pb = u // KVH, u % KVH, u % 2
                lo = 0 if b else P
                dve.wait_ge(scores_ready, u + 1)
                if u >= 2:
                    dve.wait_ge(probT_banked, u - 1)
                for g in range(GH):
                    slope = 2.0 ** (-8.0 * (HEAD_AT[kv][g] + 1) / HEADS)
                    ins = dve.scalar_tensor_tensor(prob[:, pb, g, lo:], cst[:, C_DIST + lo:C_DIST + 256],
                                                   -slope * HD ** 0.5, psA[:, g * 256 + lo:(g + 1) * 256],
                                                   ALU.mult, ALU.add)
                ins.then_inc(scores_read, 1)
                dve.wait_ge(scores_read, u + 1)
                link(dve.tensor_reduce(sm[:, pb, 0, :], prob[:, pb, :, lo:], AX.X, ALU.max))
                link(dve.tensor_tensor(sm[:, pb, 0, :], sm[:, pb, 0, :], snk[:, 1, kv * GH:(kv + 1) * GH], ALU.max))
                link(dve.tensor_scalar(sm[:, pb, 1, :], sm[:, pb, 0, :], -(HD ** -0.5), None, ALU.mult))
                dve.tensor_tensor(sm[:, pb, 5, :], sm[:, pb, 1, :], snk[:, 0, kv * GH:(kv + 1) * GH], ALU.add
                                  ).then_inc(negmax_ready, 1)

            def divide(u):
                pb = u % 2
                dve.wait_ge(exp_done, u + 1)
                link(dve.tensor_tensor(sm[:, pb, 2, :], sm[:, pb, 2, :], sm[:, pb, 3, :], ALU.add))
                dve.reciprocal(sm[:, pb, 4, :], sm[:, pb, 2, :]).then_inc(rden_ready, 1)

            for m in range(6):
                ada_mul(N_FIRST + m, m % 2, (N_FIRST + m) // 2)
            for u in range(ATT_U):
                soften(u)
                for m in BESIDE[u][0]:
                    empty(m)
                divide(u)
                for m in BESIDE[u][1]:
                    empty(m)
                if u < 5:
                    ada_mul(12 + u, u % 2, (12 + u) // 2)
            dve.wait_ge(gbc_in, 16)
            for t in range(T):
                mix_in(0, t)

            def tiny(n, at0):
                return small[:, at0:at0 + n]

            bia = tiny(64, 64)
            prs = tiny(96, 128)
            gs = tiny(16, 224)
            gm = tiny(4, 240)
            ing = tiny(16, 244)
            vmx = tiny(4, 260)
            gtt = tiny(256, 264)
            eqt = tiny(256, 520)
            rank = tiny(64, 776)
            sel = sel_tile
            ws = tiny(64, 904)
            wsum = tiny(4, 968)
            gate = tiny(64, 972)
            rest = tiny(64, 1036)
            tab = tiny(24, 1100)

            def route(l):
                dve.wait_ge(sig_ready, l + 1)
                b3 = bia.rearrange("p (g i) -> p g i", i=EPG)
                pr = prs.rearrange("p (g c) -> p g c", c=6)
                link(dve.tensor_tensor(bia.rearrange("p (t e) -> p t e", t=T), sig_tile.rearrange("p (t e) -> p t e", t=T),
                                       brb[:, :].unsqueeze(1).broadcast_to([P, T, E]), ALU.add))
                b4 = bia.rearrange("p (g a i) -> p g a i", a=2, i=2)
                dve.tensor_tensor(pr[:, :, 0:2], b4[:, :, :, 0], b4[:, :, :, 1], ALU.add)
                dve.tensor_tensor(pr[:, :, 2:4], b3[:, :, 0:2], b3[:, :, 2:4], ALU.add)
                dve.tensor_tensor(pr[:, :, 4:5], b3[:, :, 0:1], b3[:, :, 3:4], ALU.add)
                link(dve.tensor_tensor(pr[:, :, 5:6], b3[:, :, 1:2], b3[:, :, 2:3], ALU.add))
                link(dve.tensor_reduce(gs, pr, AX.X, ALU.max))
                g3 = gs.rearrange("p (t g) -> p t g", t=T)
                v3 = ing.rearrange("p (t g) -> p t g", t=T)
                link(dve.tensor_reduce(gm, g3, AX.X, ALU.max))
                link(dve.tensor_tensor(v3, g3, gm.unsqueeze(2).broadcast_to([P, T, EG]), ALU.is_equal))
                link(dve.tensor_tensor(v3, v3, cst[:, C_FST:C_FST + EG].unsqueeze(1).broadcast_to([P, T, EG]), ALU.mult))
                link(dve.tensor_reduce(vmx, v3, AX.X, ALU.max))
                link(dve.tensor_tensor(v3, v3, vmx.unsqueeze(2).broadcast_to([P, T, EG]), ALU.is_equal))
                bj = b3.unsqueeze(2).broadcast_to([P, E, EPG, EPG])
                bi = b3.unsqueeze(3).broadcast_to([P, E, EPG, EPG])
                gt4 = gtt.rearrange("p (g i j) -> p g i j", i=EPG, j=EPG)
                eq4 = eqt.rearrange("p (g i j) -> p g i j", i=EPG, j=EPG)
                dve.tensor_tensor(gt4, bj, bi, ALU.is_gt)
                link(dve.tensor_tensor(eq4, bj, bi, ALU.is_equal))
                link(dve.tensor_tensor(eqt.rearrange("p (g q) -> p g q", q=16), eqt.rearrange("p (g q) -> p g q", q=16),
                                       cst[:, C_JLT:C_JLT + 16].unsqueeze(1).broadcast_to([P, E, 16]), ALU.mult))
                link(dve.tensor_tensor(gtt, gtt, eqt, ALU.add))
                link(dve.tensor_reduce(rank, gtt.rearrange("p (g j) -> p g j", j=EPG), AX.X, ALU.add))
                dve.scalar_tensor_tensor(sel.rearrange("p (g i) -> p g i", i=EPG), rank.rearrange("p (g i) -> p g i", i=EPG),
                                         2.0, ing.unsqueeze(2).broadcast_to([P, E, EPG]), ALU.is_lt, ALU.mult
                                         ).then_inc(sel_ready, 1)
                dve.wait_ge(sel_ready, l + 1)
                link(dve.tensor_tensor(ws, sig_tile, sel, ALU.mult))
                ws3 = ws.rearrange("p (t e) -> p t e", t=T)
                link(dve.tensor_reduce(wsum, ws3, AX.X, ALU.add))
                link(dve.reciprocal(wsum, wsum))
                gt3 = gate.rearrange("p (t e) -> p t e", t=T)
                rs3 = rest.rearrange("p (t e) -> p t e", t=T)
                link(dve.tensor_tensor(gt3, ws3, wsum.unsqueeze(2).broadcast_to([P, T, E]), ALU.mult))
                tokc = cst[:, C_TOK:C_TOK + 8].rearrange("p (t c) -> p t c", t=T)
                dve.tensor_copy(rtab[:, :, :, 0:2], tokc.unsqueeze(2).broadcast_to([P, T, E, 2]))
                dve.scalar_tensor_tensor(rtab[:, :, :, 2], rank.rearrange("p (t e) -> p t e", t=T), float(SEQ),
                                         tokc[:, :, 1:2].broadcast_to([P, T, E]), ALU.mult, ALU.add)
                link(dve.tensor_copy(rtab[:, :, :, 3], gt3))
                link(dve.tensor_tensor(rs3, gt3, rtab[:, :, :, 3], ALU.subtract))
                link(dve.tensor_copy(rtab[:, :, :, 4], rs3))
                link(dve.tensor_tensor(rs3, rs3, rtab[:, :, :, 4], ALU.subtract))
                link(dve.tensor_copy(rtab[:, :, :, 5], rs3))
                dve.wait_ge(pos_ready, l + 1)
                sel3 = sel.rearrange("p (t e) -> p t e", t=T)
                pos3 = ps3[:, 0:T * E].rearrange("p (t e) -> p t e", t=T)
                dve.tensor_reduce(maxn[:, l:l + 1], ps3[:, T * E:T * E + E], AX.X, ALU.max)
                link(dve.scalar_tensor_tensor(posm, pos3, 1.0, sel3, ALU.add, ALU.mult))
                dve.tensor_copy(flag[:, l:l + 1], maxn[:, l:l + 1]).then_inc(flag_ready, 1)
                link(dve.tensor_scalar(posm, posm, -1.0, None, ALU.add))
                for g in range(EG + 1):
                    if g < EG:
                        if g >= 2:
                            dve.wait_ge(table_banked, l * EG + g - 1)
                        dve.tensor_tensor(
                            onehot[:, g % 2], cst[:, C_SLOT:C_SLOT + P].unsqueeze(1).unsqueeze(1).broadcast_to(
                                [P, T, EPG, P]),
                            posm[:, :, g * EPG:(g + 1) * EPG].unsqueeze(3).broadcast_to([P, T, EPG, P]),
                            ALU.is_equal).then_inc(onehot_ready, 1)
                    if g >= 1:
                        q = g - 1
                        cols = slice(q * EPG, (q + 1) * EPG)
                        t3 = tab.rearrange("p (e c) -> p e c", c=6)
                        dve.wait_ge(table_banked, l * EG + q + 1)
                        link(dve.tensor_copy(tab, (ps5 if q % 2 else ps4)[:, 0:24]))
                        dve.scalar_tensor_tensor(tok_i[:, cols], t3[:, :, 0], FAR, t3[:, :, 1], ALU.add, ALU.add)
                        dve.scalar_tensor_tensor(dst_i[:, cols], t3[:, :, 0], FAR, t3[:, :, 2], ALU.add, ALU.add)
                        link(dve.tensor_tensor(gslot[:, cols], t3[:, :, 3], t3[:, :, 4], ALU.add))
                        dve.tensor_tensor(gslot[:, cols], gslot[:, cols], t3[:, :, 5], ALU.add).then_inc(table_ready, 1)
                        dve.wait_ge(table_ready, l * EG + g)

            def expert_loop(l):
                def xT_half(e, j, i):
                    dve.wait_ge(xT_banked, l * E + e + 1)
                    for k in range(KD // 2, KD):
                        ins = dve.tensor_scalar(xgT[:, j % 2, k, :], psA[:, k * P:(k + 1) * P],
                                                scl[:, 2 * l + 1, k:k + 1], modc[:, 2 * l + 1, 0, k:k + 1],
                                                ALU.mult, ALU.add)
                    ins.then_inc(xT_dve, 1)

                def times_up(e, j, i):
                    dve.wait_ge(sil_ready, l * E + e + 1)
                    dve.tensor_tensor(hid[:, j % 2, :], sil[:, j % 2, :], gu_ps[j % 2][:, FF:2 * FF], ALU.mult
                                      ).then_inc(hid_ready, 1)

                def body(e, j, i):
                    static = isinstance(e, int)
                    if not static or e + 1 < E:
                        dve.wait_ge(hT_banked, l * E + e)
                        times_up(e + 1, j + 1, i)
                    if not static or e + 2 < E:
                        dve.wait_ge(gu_done, l * E + e + 1)
                        xT_half(e + 2, j, i)
                    dve.wait_ge(dn_done, l * E + e + 1)
                    dve.wait_ge(y_out[j % 2], 16 * (l * (E // 2) + 2 * i + j // 2))
                    for a in range(2):
                        ins = dve.scalar_tensor_tensor(yrow[:, j % 2, a * 512:(a + 1) * 512],
                                                       psY[:, a * 512:(a + 1) * 512], gslot[:, bass.ds(e, 1)],
                                                       gbc[:, a * 512:(a + 1) * 512], ALU.mult, ALU.mult)
                    ins.then_inc(y_ready, 1)
                    if l == 0 and (not static or e + 1 < NCH):
                        ada_mul(NCH + e + 1, (j + 1) % 2, NCH // 2 + 2 * i + (j + 1) // 2)

                xT_half(0, 0, 0)
                xT_half(1, 1, 0)
                times_up(0, 0, 0)
                dve.wait_ge(gbc_in, 16 * (2 * l + 2))
                loop_experts(dve, body)

                dve.wait_ge(flag_ready, l + 1)
                most = dve.value_load(flag[0:1, l:l + 1], min_val=0, max_val=SEQ)
                with dve.If(most > P):
                    dve.wait_ge(y_out[1], 16 * (E // 2) * (l + 1))
                    with dve.Fori(0, ROUNDS) as r:
                        dve.wait_ge(ov_link[l], r * (1 + 2 * E))
                        dve.tensor_scalar(posm, posm, float(-P), None, ALU.add).then_inc(ov_link[l], 1)
                        with dve.Fori(0, E) as e:
                            n = r * E + e
                            dve.wait_ge(ov_link[l], r * (1 + 2 * E) + 1 + 2 * e)
                            dve.wait_ge(ov_out[l], 16 * n)
                            dve.tensor_copy(ovr, rtab[:, :, bass.ds(e, 1), :].rearrange("p t a c -> p t (a c)"))
                            dve.tensor_tensor(
                                onehot_ov, cst[:, C_SLOT:C_SLOT + P].unsqueeze(1).broadcast_to([P, T, P]),
                                posm[:, :, bass.ds(e, 1)].broadcast_to([P, T, P]),
                                ALU.is_equal).then_inc(ov_oh[l], 1)
                            dve.wait_ge(ov_tab[l], n + 1)
                            base = r * (1 + 2 * E) + 1 + 2 * e
                            dve.tensor_copy(ovtab[:, 0:6], ps4[:, 0:6]).then_inc(ov_link[l], 1)
                            dve.wait_ge(ov_link[l], base + 1)
                            dve.scalar_tensor_tensor(ovtok, ovtab[:, 0:1], FAR, ovtab[:, 1:2], ALU.add, ALU.add)
                            dve.scalar_tensor_tensor(ovdst, ovtab[:, 0:1], FAR, ovtab[:, 2:3], ALU.add, ALU.add)
                            dve.tensor_tensor(ovgate, ovtab[:, 3:4], ovtab[:, 4:5], ALU.add).then_inc(ov_link[l], 1)
                            dve.wait_ge(ov_link[l], base + 2)
                            dve.tensor_tensor(ovgate, ovgate, ovtab[:, 5:6], ALU.add).then_inc(ov_idx[l], 1)
                            dve.wait_ge(ov_sil[l], n + 1)
                            dve.tensor_tensor(hid[:, 0, :], sil[:, 0, :], ps3[:, FF:2 * FF], ALU.mult
                                              ).then_inc(ov_hid[l], 1)
                            dve.wait_ge(ov_dn[l], n + 1)
                            dve.wait_ge(ov_idx[l], n + 1)
                            for a in range(2):
                                ins = dve.scalar_tensor_tensor(yrow[:, 0, a * 512:(a + 1) * 512],
                                                               psY[:, a * 512:(a + 1) * 512], ovgate[:, 0:1],
                                                               gbc[:, a * 512:(a + 1) * 512], ALU.mult, ALU.mult)
                            ins.then_inc(ov_y[l], 1)

            def pool_means():
                for g in range(4):
                    w = 2 << g
                    src = uT[:, 2 * g:2 * g + 2, :]
                    cur, back = src, 1
                    step = 0
                    while back < w:
                        nxt = run[:, step % 2]
                        dve.tensor_copy(nxt[:, :, 0:back], cur[:, :, 0:back])
                        link(dve.tensor_tensor(nxt[:, :, back:], cur[:, :, back:], cur[:, :, 0:SEQ - back], ALU.add))
                        cur, back, step = nxt, 2 * back, step + 1
                    link(dve.tensor_tensor(cur[:, :, 0:w - 1], cur[:, :, 0:w - 1],
                                           cst[:, C_INV:C_INV + w - 1].unsqueeze(1).broadcast_to([P, 2, w - 1]),
                                           ALU.mult))
                    dve.tensor_tensor(pooled[:, 2 * g:2 * g + 2, 0:w - 1], cur[:, :, 0:w - 1], src[:, :, 0:w - 1],
                                      ALU.subtract)
                    link_next = dve.scalar_tensor_tensor(pooled[:, 2 * g:2 * g + 2, w - 1:], cur[:, :, w - 1:],
                                                         1.0 / w, src[:, :, w - 1:], ALU.mult, ALU.subtract)
                    link_next.then_inc(pooled_ready, 1)
                    dve.wait_ge(pooled_ready, g + 1)

            for l in range(LAYERS):
                if l:
                    norm(2)
                    spread(2)
                    dve.wait_ge(uT_act, (2 * l + 1) * KD // 2)
                    dve.wait_ge(uT_dve, (2 * l + 1) * KD // 2)
                    pool_means()
                    dve.wait_ge(gbc_in, 16 * 3)
                    dve.wait_ge(psc_in, 16)
                    link(dve.tensor_tensor(gbc[:, :], gbc[:, :], psc, ALU.mult))
                    for t in range(T):
                        mix_in(1, t)
                norm(2 * l + 1)
                spread(2 * l + 1)
                route(l)
                expert_loop(l)
                for t in range(T):
                    ffn_in(l, t)
            dve.wait_ge(std_done, 5)
            link(dve.reciprocal(rstd[:, :], rstd[:, :]))
            dve.wait_ge(gbc_in, 16 * 5)
            for t in range(T):
                dve.scalar_tensor_tensor(xhat[:, t, :], h[:, t, :], rstd[:, t:t + 1], gbc[:, :], ALU.mult, ALU.mult
                                         ).then_inc(out_ready, 1)

        @block.tensor
        def _(pe):
            def ada_total(n, b, used):
                pe.wait_ge(ada_mac, n + 1)
                pe.wait_ge(row_copied, n)
                pe.matmul(ps5[0:1, 0:AC], ones[:, 0:1], acc[:, b, 0, :], start=True, stop=False)
                pe.matmul(ps5[0:1, 0:AC], ones[:, 0:1], acc[:, b, 1, :], start=False, stop=False)
                pe.matmul(ps5[0:1, 0:AC], ones[0:1, 0:1], brow[0:1, b, :], start=False, stop=True
                          ).then_inc(ada_sum, 1)

            def transposes(s):
                pe.wait_ge(xhat_ready, (s + 1) * T)
                for k in range(KD):
                    bank = psA[:, (k % 2) * 512:(k % 2 + 1) * 512]
                    if k >= 2:
                        pe.wait_ge(uT_dve if k % 2 else uT_act, s * KD // 2 + k // 2)
                    for t in range(T):
                        if s == 2:
                            src = xhat[:, t, k * P:(k + 1) * P]
                        else:
                            src = xhat[:, t, :].rearrange("p (a k) -> p k a", k=KD)[:, k, :]
                        ins = pe.transpose(bank[:, t * P:(t + 1) * P], src, ident)
                    ins.then_inc(uT_banked, 1)

            pe.wait_ge(const_in, 16)
            for n in range(N_FIRST):
                ada_total(n, n % 2, n // 2)
            transposes(0)

            def project(m):
                name, i = PROJ[m]
                bank = psY[:, (m % 2) * 512:(m % 2 + 1) * 512]
                if m == 0:
                    pe.wait_ge(uT_act, KD // 2)
                    pe.wait_ge(uT_dve, KD // 2)
                    pe.wait_ge(win_in[0], 16)
                if m == 6:
                    pe.wait_ge(win_in[1], 16)
                if m >= 2:
                    if PROJ[m - 2][0] in ACT_SIDE:
                        pe.wait_ge(proj_act, act_before[m - 1])
                    else:
                        pe.wait_ge(proj_dve, m - 1 - act_before[m - 1])
                if name == "v":
                    for t in range(T):
                        for k in range(KD):
                            ins = pe.matmul(bank[:, t * P:(t + 1) * P], uT[:, k, t * P:(t + 1) * P],
                                            win[:, k, V0:V0 + P], start=(k == 0), stop=(k == KD - 1))
                else:
                    for k in range(KD):
                        at0 = {"q": 0, "k": K0, "c": C0, "x": X0, "b": B0}[name] + i * P
                        wt = win[:, k, at0:at0 + P]
                        ins = pe.matmul(bank, wt, uT[:, k, :], start=(k == 0), stop=(k == KD - 1))
                ins.then_inc(proj_ready, 1)

            def scores(u):
                b, kv = u // KVH, u % KVH
                if u == 0:
                    pe.wait_ge(proj_act, 6)
                    pe.wait_ge(kswap_in, 32)
                if u:
                    pe.wait_ge(scores_read, u)
                lo = 0 if b else P
                for g in range(GH):
                    odd, i = g // 2, g % 2
                    rows = slice(odd * HD, (odd + 1) * HD)
                    ins = pe.matmul(psA[:, g * 256 + lo:(g + 1) * 256], qT[rows, kv * 2 + i, b * P:(b + 1) * P],
                                    (kT if odd == kv else kswap)[rows, (b - 1) * P + lo:(b + 1) * P],
                                    start=True, stop=True)
                ins.then_inc(scores_ready, 1)

            def turn_prob(u):
                b = u // KVH
                pe.wait_ge(prob_ready, u + 1)
                if u:
                    pe.wait_ge(probT_ready, u)
                for kb in range(0 if b else 1, 2):
                    for g in range(GH):
                        ins = pe.transpose((ps3 if kb else ps2)[:, g * P:(g + 1) * P],
                                           prob[:, u % 2, g, kb * P:(kb + 1) * P], ident)
                ins.then_inc(probT_banked, 1)

            def attend(u):
                b, kv = u // KVH, u % KVH
                pe.wait_ge(probT_ready, u + 1)
                if kv == 0 and b:
                    pe.wait_ge(att_ready, b)
                for g in range(GH):
                    odd, i = g // 2, g % 2
                    dst = ps4[odd * HD:(odd + 1) * HD, (kv * 2 + i) * P:(kv * 2 + i + 1) * P]
                    for kb in range(0 if b else 1, 2):
                        ins = pe.matmul(dst, vtok[:, b - 1 + kb, kv * HD:(kv + 1) * HD],
                                        probT[:, kb, g * P:(g + 1) * P], start=(kb == 0 or b == 0), stop=(kb == 1))
                ins.then_inc(att_banked, 1)

            for m in range(6):
                project(m)
                ada_total(N_FIRST + m, m % 2, (N_FIRST + m) // 2)
            for u in range(ATT_U + 1):
                if u < ATT_U:
                    scores(u)
                for m in BESIDE[u][0]:
                    project(m)
                if u:
                    turn_prob(u - 1)
                for m in BESIDE[u][1]:
                    project(m)
                if u:
                    attend(u - 1)
                if u < 4:
                    ada_total(12 + u, u % 2, (12 + u) // 2)

            def mix_out(t):
                ps = pair[t % 2]
                if t == 0:
                    pe.wait_ge(wout_in, 32)
                    pe.wait_ge(att_ready, T)
                    pe.wait_ge(proj_dve, len(PROJ) - act_before[-1])
                if t >= 2:
                    pe.wait_ge(h_ready, t - 1)
                for a in range(2):
                    for q in range(8):
                        lhs = attnT[:, q, t * P:(t + 1) * P] if q < 4 else convT[:, q - 4, t * P:(t + 1) * P]
                        wt = wo_att[:, q, :] if q < 4 else wo_conv[:, q - 4, :]
                        ins = pe.matmul(ps[:, a * 512:(a + 1) * 512], lhs, wt[:, a * 512:(a + 1) * 512],
                                        start=(q == 0), stop=(q == 7))
                ins.then_inc(mix_banked, 1)

            def pool_out(t):
                ps = pair[t % 2]
                if t == 0:
                    pe.wait_ge(wpool_in, 16)
                    pe.wait_ge(pooled_ready, 4)
                if t >= 2:
                    pe.wait_ge(h_ready, 2 * T + t - 1)
                for g in range(4):
                    for q in range(2):
                        ins = pe.matmul(ps[:, g * 256:(g + 1) * 256], pooled[:, 2 * g + q, t * P:(t + 1) * P],
                                        wpool[:, 2 * g + q, :], start=(q == 0), stop=(q == 1))
                ins.then_inc(mix_banked, 1)

            def route(l):
                s = 2 * l + 1
                pe.wait_ge(uT_act, (s + 1) * KD // 2)
                pe.wait_ge(uT_dve, (s + 1) * KD // 2)
                pe.wait_ge(small_in, 16 * N_SMALL)
                for t in range(T):
                    for k in range(KD):
                        ins = pe.matmul(ps2[:, t * E:(t + 1) * E], uT[:, k, t * P:(t + 1) * P], wr[:, k, :],
                                        start=(k == 0), stop=(k == KD - 1))
                ins.then_inc(logits_ready, 1)
                pe.wait_ge(sel_ready, l + 1)
                for t in range(T + 1):
                    for q in range(min(t + 1, T)):
                        ins = pe.matmul(ps3[:, t * E:(t + 1) * E], before if q == t else ones,
                                        sel_tile[:, q * E:(q + 1) * E], start=(q == 0), stop=(q == min(t, T - 1)))
                ins.then_inc(pos_ready, 1)
                pe.wait_ge(row_copied, NCH * (l + 1))
                for g in range(EG):
                    pe.wait_ge(onehot_ready, l * EG + g + 1)
                    for e in range(EPG):
                        for t in range(T):
                            ins = pe.matmul((ps5 if g % 2 else ps4)[:, e * 6:(e + 1) * 6], onehot[:, g % 2, t, e, :],
                                            rtab[:, t, g * EPG + e, :], start=(t == 0), stop=(t == T - 1))
                    ins.then_inc(table_banked, 1)

            def expert_loop(l):
                def turn_in(e, j, i):
                    pe.wait_ge(xg_in[j % 4], 16 * (l * (E // 4) + i + 1))
                    pe.wait_ge(xT_act, l * E + e)
                    pe.wait_ge(xT_dve, l * E + e)
                    for k in range(KD):
                        ins = pe.transpose(psA[:, k * P:(k + 1) * P],
                                           xg[:, j % 4, :].rearrange("p (a k) -> p k a", k=KD)[:, k, :], ident)
                    ins.then_inc(xT_banked, 1)

                def first_product(e, j, i):
                    pe.wait_ge(xT_act, l * E + e + 1)
                    pe.wait_ge(xT_dve, l * E + e + 1)
                    pe.wait_ge(gu_in[j % 4], 32 * (l * (E // 4) + i + 1))
                    for k in range(KD):
                        ins = pe.matmul(gu_ps[j % 2][:, :].rearrange("p (a f) -> p a f", a=2), xgT[:, j % 2, k, :],
                                        w_gu(j % 4)[:, :, k, :], start=(k == 0), stop=(k == KD - 1))
                    ins.then_inc(gu_done, 1)

                def body(e, j, i):
                    static = isinstance(e, int)
                    if not static or e + 1 < E:
                        pe.wait_ge(hid_ready, l * E + e)
                        first_product(e + 1, j + 1, i + (j + 1) // 4)
                    pe.wait_ge(hid_ready, l * E + e + 1)
                    pe.wait_ge(hT_ready, l * E + e)
                    for q in range(2):
                        ins = pe.transpose(ps2[:, q * P:(q + 1) * P],
                                           hid[:, j % 2, :].rearrange("p (a c) -> p c a", c=2)[:, q, :], ident)
                    ins.then_inc(hT_banked, 1)
                    if not static or e + 2 < E:
                        turn_in(e + 2, j + 2, i + (j + 2) // 4)
                    pe.wait_ge(hT_ready, l * E + e + 1)
                    pe.wait_ge(y_ready, l * E + e)
                    pe.wait_ge(dn_in[j], 16 * (l * (E // 4) + i + 1))
                    for a in range(2):
                        for q in range(2):
                            ins = pe.matmul(psY[:, a * 512:(a + 1) * 512], hT[:, q, :],
                                            w_dn(j)[:, q, a * 512:(a + 1) * 512], start=(q == 0), stop=(q == 1))
                    ins.then_inc(dn_done, 1)
                    if l == 0:
                        ada_total(NCH + e, j % 2, 0)

                turn_in(0, 0, 0)
                turn_in(1, 1, 0)
                first_product(0, 0, 0)
                loop_experts(pe, body)

                pe.wait_ge(flag_ready, l + 1)
                most = pe.value_load(flag[0:1, l:l + 1], min_val=0, max_val=SEQ)
                with pe.If(most > P):
                    with pe.Fori(0, ROUNDS * E) as n:
                        pe.wait_ge(ov_oh[l], n + 1)
                        for t in range(T):
                            ins = pe.matmul(ps4[:, 0:6], onehot_ov[:, t, :], ovr[:, t, :],
                                            start=(t == 0), stop=(t == T - 1))
                        ins.then_inc(ov_tab[l], 1)
                        pe.wait_ge(ov_xg[l], 16 * n + 16)
                        for k in range(KD):
                            ins = pe.transpose(psA[:, k * P:(k + 1) * P],
                                               xg[:, 0, :].rearrange("p (a k) -> p k a", k=KD)[:, k, :], ident)
                        ins.then_inc(ov_xb[l], 1)
                        pe.wait_ge(ov_xT[l], n + 1)
                        pe.wait_ge(ov_w[l], 48 * n + 48)
                        for k in range(KD):
                            ins = pe.matmul(ps3[:, :].rearrange("p (a f) -> p a f", a=2), xgT[:, 0, k, :],
                                            w_gu(0)[:, :, k, :], start=(k == 0), stop=(k == KD - 1))
                        ins.then_inc(ov_gu[l], 1)
                        pe.wait_ge(ov_hid[l], n + 1)
                        for q in range(2):
                            ins = pe.transpose(ps2[:, q * P:(q + 1) * P],
                                               hid[:, 0, :].rearrange("p (a c) -> p c a", c=2)[:, q, :], ident)
                        ins.then_inc(ov_hb[l], 1)
                        pe.wait_ge(ov_hT[l], n + 1)
                        for a in range(2):
                            for q in range(2):
                                ins = pe.matmul(psY[:, a * 512:(a + 1) * 512], hT[:, q, :],
                                                w_dn(0)[:, q, a * 512:(a + 1) * 512], start=(q == 0), stop=(q == 1))
                        ins.then_inc(ov_dn[l], 1)

            for l in range(LAYERS):
                if l:
                    transposes(2)
                for t in range(T):
                    (pool_out if l else mix_out)(t)
                transposes(2 * l + 1)
                route(l)
                expert_loop(l)


_INS = ['x', 'c', 'w_ada', 'b_ada', 'norm_mix', 'norm_ffn', 'w_in', 'w_out', 'sinks', 'conv_w', 'w_pool', 'pool_scale',
        'w_router', 'b_router', 'w_gate', 'w_up', 'w_down', 'norm_final']


def _constants():
    import numpy as np
    a = np.zeros((P, C_END), np.float32)
    p = np.arange(P)
    a[:, C_ID:C_ID + P] = np.eye(P)
    a[:, C_BEF:C_BEF + P] = p[:, None] < p[None, :]
    dist = p[:, None] + P - np.arange(2 * P)[None, :]
    a[:, C_DIST:C_DIST + 2 * P] = np.where((dist >= 0) & (dist < P), dist, 1e30)
    a[:, C_SLOT:C_SLOT + P] = p[None, :]
    a[:, C_ONE:C_ONE + P] = 1.0
    a[:, C_INV:C_INV + 16] = np.float32(1.0) / np.arange(1, 17, dtype=np.float32)
    tok = np.zeros((P, T, 2), np.float32)
    tok[:, :, 0] = p[:, None]
    tok[:, :, 1] = P * np.arange(T)[None, :] - FAR
    a[:, C_TOK:C_TOK + 8] = tok.reshape(P, 8)
    j = np.arange(4)
    a[:, C_JLT:C_JLT + 16] = (j[None, :] < j[:, None]).reshape(1, 16)
    a[:, C_FST:C_FST + 4] = 4 - j
    return a


def kernel(**inputs):
    import numpy as _np
    import concourse.bacc as _bacc
    from concourse.bass_utils import run_bass_kernel_spmd as _run

    nc = _bacc.Bacc("TRN2", target_bir_lowering=False, num_devices=1)
    arrays, args = {}, []
    for name in _INS:
        a = _np.ascontiguousarray(inputs[name])
        arrays[f"in_{name}_dram"] = a
        args.append(nc.dram_tensor(f"in_{name}_dram", a.shape, mybir.dt.from_np(a.dtype), kind="ExternalInput").ap())
    arrays["constants"] = _constants()
    args.append(nc.dram_tensor("constants", (P, C_END), F32, kind="ExternalInput").ap())
    args.append(nc.dram_tensor("out_dram", (1, SEQ, D), F32, kind="ExternalOutput").ap())
    args.append(nc.dram_tensor("mod_dram", (LAYERS, MODW), F32, kind="Internal").ap())
    args.append([nc.dram_tensor(f"xhat_dram{l}", (SEQ, D), F32, kind="Internal").ap() for l in range(LAYERS)])
    args.append([nc.dram_tensor(f"y_dram{l}", (2 * SEQ, D), F32, kind="Internal").ap() for l in range(LAYERS)])
    trunk(nc, *args)
    return _run(nc, [arrays], core_ids=[0]).results[0]["out_dram"]
```

```python
from contextlib import ExitStack

import concourse.bass as bass
from concourse import mybir

F32 = mybir.dt.float32
BF16 = mybir.dt.bfloat16
I32 = mybir.dt.int32
U32 = mybir.dt.uint32
ALU = mybir.AluOpType
ACT = mybir.ActivationFunctionType
AX = mybir.AxisListType

P = 128
SEQ, D = 512, 1024
T = SEQ // P
KD = D // P
LAYERS = 2
EPS = 1e-6
MODW = 6 * D
AC = 384
NCH = MODW // AC
N_FIRST = 6
IN_W = 2304
HD, HEADS, KVH = 64, 8, 2
GH = HEADS // KVH
AW = HEADS * HD
K0, V0, B0, C0, X0 = AW, AW + 128, AW + 256, AW + 256 + 512, AW + 256 + 1024
CC = 4
E, EG, EPG, FF = 16, 4, 4, 256
NSLOT = 4
FAR = 4096.0
HEAD_AT = [[kv * GH + 2 * (g % 2) + g // 2 for g in range(GH)] for kv in range(KVH)]
ATT_U = T * KVH
HEAD = 1
ROUNDS = SEQ // P - 1

C_ID, C_BEF, C_DIST, C_SLOT, C_ONE, C_INV, C_TOK, C_JLT, C_FST, C_END = (
    0, 128, 256, 512, 640, 768, 784, 792, 808, 812)


def trunk(nc, x, c, w_ada, b_ada, norm_mix, norm_ffn, w_in, w_out, sinks, conv_w, w_pool, pool_scale,
          w_router, b_router, w_gate, w_up, w_down, norm_final, consts, out, mod_dram, xhat_dram, y_dram):
    ctx = ExitStack()
    with ctx:
        ctx.enter_context(nc.allow_non_contiguous_dma(reason="vectors of 1024 channels, 128k + p at partition p"))

        def sb(name, shape, dt=F32):
            return ctx.enter_context(nc.sbuf_tensor(name, shape, dt))

        def sem(name):
            return ctx.enter_context(nc.semaphore(name))

        h = sb("h", [P, T, D])
        xu = sb("xu", [P, 2 * T * D])
        xhat = xu[:, 0:T * D].rearrange("p (t d) -> p t d", t=T)
        uT = xu[:, T * D:2 * T * D].rearrange("p (k s) -> p k s", k=KD)
        cuT = xu[:, 0:CC * SEQ].rearrange("p (c s) -> p c s", c=CC)
        wo_att = xu[:, 0:4 * D].rearrange("p (c n) -> p c n", c=4)
        wo_conv = xu[:, 4 * D:8 * D].rearrange("p (c n) -> p c n", c=4)
        SLOT = 3 * KD * FF
        ring = sb("ring", [P, 3 * SLOT])
        win = ring[:, 0:KD * IN_W].rearrange("p (k n) -> p k n", k=KD)

        def wslot(j):
            return ring[:, j * SLOT:(j + 1) * SLOT] if j < 3 else xu[:, 0:SLOT]

        def w_gu(j):
            return wslot(j)[:, 0:2 * KD * FF].rearrange("p (a k f) -> p a k f", a=2, k=KD)

        def w_dn(j):
            return wslot(j)[:, 2 * KD * FF:SLOT].rearrange("p (a d) -> p a d", a=2)

        adaw = sb("adaw", [P, 2, KD, AC])
        wpool = adaw[:, 0].rearrange("p k n -> p (k n)")[:, 0:KD * 256].rearrange("p (a n) -> p a n", a=KD)
        acc = sb("acc", [P, 4, AC])
        brow = sb("brow", [P, 2, AC])
        mrow = sb("mrow", [1, 2, AC])
        gbc = sb("gbc", [P, D])
        cst = sb("cst", [P, C_END])
        ident, before = cst[:, C_ID:C_ID + P], cst[:, C_BEF:C_BEF + P]
        ones = cst[:, C_ONE:C_ONE + P]

        WORK = 42 * 256
        work = sb("work", [P, WORK])
        at = [0]

        def take(n):
            at[0] += n
            assert at[0] <= WORK, at[0]
            return work[:, at[0] - n:at[0]]

        convT = take(CC * SEQ).rearrange("p (c s) -> p c s", c=CC)
        attnT = take(4 * SEQ).rearrange("p (c s) -> p c s", c=4)
        qT = take(4 * SEQ).rearrange("p (c s) -> p c s", c=4)
        kT = take(SEQ)
        kswap = take(SEQ)
        vtok = take(SEQ).rearrange("p (t n) -> p t n", t=T)
        prob = take(2 * GH * 256).rearrange("p (b h s) -> p b h s", b=2, h=GH)
        probT = take(2 * GH * P).rearrange("p (b n) -> p b n", b=2)
        at[0] = 0
        xg = take(4 * D).rearrange("p (b d) -> p b d", b=4)
        xgT = take(2 * D).rearrange("p (b k s) -> p b k s", b=2, k=KD)
        yrow = take(4 * D).rearrange("p (b d) -> p b d", b=4)[:, 0:2]
        at[0] -= 2 * D
        sil = take(2 * FF).rearrange("p (b f) -> p b f", b=2)
        hid = take(2 * FF).rearrange("p (b f) -> p b f", b=2)
        hT = take(2 * P).rearrange("p (a s) -> p a s", a=2)
        tok_i = take(E).bitcast(U32)
        dst_i = take(E).bitcast(U32)
        gslot = take(E)
        posm = take(T * E).rearrange("p (t e) -> p t e", t=T)
        rtab = take(T * E * 3).bitcast(BF16).rearrange("p (t e c) -> p t e c", t=T, e=E)
        ovtab = take(8)
        ovtok, ovdst = take(1).bitcast(U32), take(1).bitcast(U32)
        ovgate = take(1)
        ovr = take(T * 3).bitcast(BF16).rearrange("p (t c) -> p t c", t=T)
        onehot_ov = yrow[:, 1, 0:T * P // 2].bitcast(BF16).rearrange("p (t s) -> p t s", t=T)
        onehot = yrow.rearrange("p b d -> p (b d)").bitcast(BF16).rearrange(
            "p (b t e s) -> p b t e s", b=2, t=T, e=EPG)
        small = xgT.rearrange("p b k s -> p (b k s)")
        ycomb = work[:, 0:8 * D].rearrange("p (t a d) -> p t a d", t=T, a=2)
        pooled = work[:, 0:4 * D].rearrange("p (k s) -> p k s", k=KD)
        run = work[:, 4 * D:6 * D].rearrange("p (b k s) -> p b k s", b=2, k=2)
        psc = adaw[:, 1].rearrange("p k n -> p (k n)")[:, 0:D]
        gmix = [gbc[:, :], acc[:, :, :].rearrange("p a n -> p (a n)")[:, 0:D]]
        junk = work[:, 10 * D:10 * D + D // 2].bitcast(BF16)
        logT = work[0:E, 10 * D:10 * D + SEQ]
        mixt = work[:, 8 * D:10 * D].rearrange("p (b d) -> p b d", b=2)

        sel_tile = sb("sel_tile", [P, T * E], BF16)[:, :]
        cstb = sb("cstb", [P, 2 * P], BF16)
        sig_tile = sb("sig_tile", [P, T * E])[:, :]
        cond = sb("cond", [P, KD])
        craw = sb("craw", [P, KD])
        modc = sb("modc", [P, 4, 2, KD])
        normc = sb("normc", [P, 4, KD])
        scl = sb("scl", [P, 4, KD])
        wr = sb("wr", [P, KD, E])
        brb = sb("brb", [P, E])
        snk = sb("snk", [P, 2, HEADS])
        cvw = sb("cvw", [P, 3, CC])
        eps = sb("eps", [P, 1])
        ss = sb("ss", [P, T])
        rstd = sb("rstd", [P, T])
        sm = sb("sm", [P, 2, 6, GH])
        flag = sb("flag", [P, LAYERS], I32)
        maxn = sb("maxn", [P, LAYERS])

        psA = ctx.enter_context(nc.psum_tensor("psA", [P, 1024], F32))
        ps2 = ctx.enter_context(nc.psum_tensor("ps2", [P, 512], F32))
        ps3 = ctx.enter_context(nc.psum_tensor("ps3", [P, 512], F32))
        ps4 = ctx.enter_context(nc.psum_tensor("ps4", [P, 512], F32))
        ps5 = ctx.enter_context(nc.psum_tensor("ps5", [P, 512], F32))
        psY = ctx.enter_context(nc.psum_tensor("psY", [P, 1024], F32))
        pair = [psY, psA]
        gu_ps = [ps3, ps4]

        const_in = sem("const_in")
        x_in = sem("x_in")
        c_in, small_in, psc_in = sem("c_in"), sem("small_in"), sem("psc_in")
        eps_ready, brow_clear = sem("eps_ready"), sem("brow_clear")
        ada_in = [sem(f"ada_in{b}{half}") for b in range(2) for half in "ab"]
        win_in = [sem(f"win_in{b}") for b in range(2)]
        wout_in = sem("wout_in")
        wpool_in = sem("wpool_in")
        gu_in = [sem(f"gu_in{j}") for j in range(NSLOT)]
        dn_in = [sem(f"dn_in{j}") for j in range(NSLOT)]
        cond_ready = sem("cond_ready")
        mac_step = sem("mac_step")
        ada_mac = sem("ada_mac")
        ada_sum = sem("ada_sum")
        row_copied = sem("row_copied")
        mod_stored = [sem(f"mod_stored{b}") for b in range(2)]
        modc_in = [sem(f"modc_in{s}") for s in range(4)]
        gbc_in = sem("gbc_in")
        scl_ready = sem("scl_ready")
        sq_done = sem("sq_done")
        std_done = sem("std_done")
        xhat_ready = sem("xhat_ready")
        xhat_stored = sem("xhat_stored")
        uT_banked = sem("uT_banked")
        uT_act, uT_dve = sem("uT_act"), sem("uT_dve")
        h_ready = sem("h_ready")
        link_dve = sem("link_dve")
        link_act = sem("link_act")
        proj_ready = sem("proj_ready")
        kswap_in = sem("kswap_in")
        proj_act, proj_dve = sem("proj_act"), sem("proj_dve")
        scores_ready, scores_read = sem("scores_ready"), sem("scores_read")
        negmax_ready, exp_done = sem("negmax_ready"), sem("exp_done")
        rden_ready, prob_ready = sem("rden_ready"), sem("prob_ready")
        probT_banked, probT_ready = sem("probT_banked"), sem("probT_ready")
        att_banked, att_ready = sem("att_banked"), sem("att_ready")
        mix_banked = sem("mix_banked")
        pooled_ready = sem("pooled_ready")
        logits_ready, sig_ready = sem("logits_ready"), sem("sig_ready")
        logT_ready, logits_turned, cstb_ready = sem("logT_ready"), sem("logits_turned"), sem("cstb_ready")
        sel_ready, pos_ready = sem("sel_ready"), sem("pos_ready")
        onehot_ready = sem("onehot_ready")
        table_banked, table_ready = sem("table_banked"), sem("table_ready")
        flag_ready = sem("flag_ready")
        xg_clear = sem("xg_clear")
        xg_in = [sem(f"xg_in{j}") for j in range(4)]
        xT_banked, xT_act, xT_dve = sem("xT_banked"), sem("xT_act"), sem("xT_dve")
        gu_done, sil_ready, hid_ready = sem("gu_done"), sem("sil_ready"), sem("hid_ready")
        hT_banked, hT_ready = sem("hT_banked"), sem("hT_ready")
        dn_done, y_ready = sem("dn_done"), sem("y_ready")
        y_out = [sem(f"y_out{j}") for j in range(2)]
        y_in = [sem(f"y_in{j}") for j in range(T)]
        out_ready, out_stored = sem("out_ready"), sem("out_stored")
        ov_w = [sem(f"ov_w{l}") for l in range(LAYERS)]
        ov_oh = [sem(f"ov_oh{l}") for l in range(LAYERS)]
        ov_link = [sem(f"ov_link{l}") for l in range(LAYERS)]
        ov_tab = [sem(f"ov_tab{l}") for l in range(LAYERS)]
        ov_idx = [sem(f"ov_idx{l}") for l in range(LAYERS)]
        ov_xg = [sem(f"ov_xg{l}") for l in range(LAYERS)]
        ov_xb = [sem(f"ov_xb{l}") for l in range(LAYERS)]
        ov_xT = [sem(f"ov_xT{l}") for l in range(LAYERS)]
        ov_gu = [sem(f"ov_gu{l}") for l in range(LAYERS)]
        ov_sil = [sem(f"ov_sil{l}") for l in range(LAYERS)]
        ov_hid = [sem(f"ov_hid{l}") for l in range(LAYERS)]
        ov_hb = [sem(f"ov_hb{l}") for l in range(LAYERS)]
        ov_hT = [sem(f"ov_hT{l}") for l in range(LAYERS)]
        ov_dn = [sem(f"ov_dn{l}") for l in range(LAYERS)]
        ov_y = [sem(f"ov_y{l}") for l in range(LAYERS)]
        ov_out = [sem(f"ov_out{l}") for l in range(LAYERS)]
        ov_through = [sem(f"ov_through{l}") for l in range(LAYERS)]

        N_SMALL = 11

        PROJ = [("q", i) for i in range(4)] + [("k", 0), ("v", 0)] + [(n, i) for i in range(CC) for n in "cxb"]
        ACT_SIDE = {"q", "k", "v", "c"}
        act_before = [sum(n in ACT_SIDE for n, _ in PROJ[:m]) for m in range(len(PROJ) + 1)]
        BESIDE = [([6], [7]), ([8], [9]), ([10], [11]), ([12], []), ([13], [14]), ([15], []), ([16], [17]), ([], []),
                  ([], [])]
        N_ATT = N_FIRST + 6
        BY_UNIT = [2, 2, 2, 1, 1, 1, 1, 0]
        N_MIX = N_ATT + sum(BY_UNIT)
        BY_TILE = [3, 3, 3, 1]

        def unit_chunks(u):
            return range(N_ATT + sum(BY_UNIT[:u]), N_ATT + sum(BY_UNIT[:u + 1]))

        def unit_totals(u):
            return range(unit_chunks(u).start - 1, unit_chunks(u).stop - (u < ATT_U - 1))
        assert N_MIX + sum(BY_TILE) == LAYERS * NCH

        def mod_waits(eng, n):
            for q in (n, n - 1):
                eng.wait_ge(mod_stored[q % 2], 16 * (q // 2 + 1))

        def loop_experts(eng, body, first=0):
            for e in range(4 * first):
                body(e, e % 4, e // 4)
            with eng.Fori(first, E // 4 - 1) as i:
                for j in range(4):
                    body(4 * i + j, j, i)
            for j in range(4):
                body(E - 4 + j, j, E // 4 - 1)

        block = ctx.enter_context(nc.Block())

        def overflow_sync(sp, l):
            sp.wait_ge(dn_done, HEAD + E * (l + 1))
            sp.wait_ge(flag_ready, l + 1)
            most = sp.value_load(flag[0:1, l:l + 1], min_val=0, max_val=SEQ)
            with sp.If(most > P):
                with sp.Fori(0, ROUNDS) as r:
                    with sp.Fori(0, E) as e:
                        n = r * E + e
                        gate = w_gate[l, bass.ds(e, 1)].rearrange("a (p k) f -> p (a k f)", k=KD)
                        up = w_up[l, bass.ds(e, 1)].rearrange("a (p k) f -> p (a k f)", k=KD)
                        down = w_down[l, bass.ds(e, 1)].rearrange("a (p c) d -> p (a c d)", c=2)
                        for s in (gate, up, down):
                            sp.lower_ap_dma(s)
                        sp.wait_ge(ov_dn[l], HEAD + n)
                        sp.dma_start(wslot(0)[:, 0:KD * FF], gate).then_inc(ov_w[l], 16)
                        sp.dma_start(wslot(0)[:, KD * FF:2 * KD * FF], up).then_inc(ov_w[l], 16)
                        sp.dma_start(wslot(0)[:, 2 * KD * FF:SLOT], down).then_inc(ov_w[l], 16)
                        sp.wait_ge(ov_out[l], 16 * n + 16)
                        sp.sem_inc(ov_through[l], 1)
                sp.wait_ge(ov_out[l], 16 * ROUNDS * E)

        @block.sync
        def _(sp):
            def load_ada(n):
                b, l, q = n % 2, n // NCH, n % NCH
                if n == 0:
                    sp.wait_ge(brow_clear, 1)
                for half in range(2):
                    ks = slice(half * KD // 2, (half + 1) * KD // 2)
                    if n >= 2:
                        sp.wait_ge(mac_step, (n - 2) * KD + (half + 1) * KD // 2)
                    sp.dma_start(adaw[:, b, ks], w_ada[l, :, q * AC:(q + 1) * AC].rearrange("(p k) n -> p k n", k=KD)
                                 [:, ks]).then_inc(ada_in[2 * b + half], 16)
                    if half == 0:
                        sp.dma_start(brow[0:1, b, :], b_ada[l:l + 1, q * AC:(q + 1) * AC]).then_inc(ada_in[2 * b], 16)

            def load_expert(l, e, j):
                gate = w_gate[l, bass.ds(e, 1)].rearrange("a (p k) f -> p (a k f)", k=KD)
                up = w_up[l, bass.ds(e, 1)].rearrange("a (p k) f -> p (a k f)", k=KD)
                down = w_down[l, bass.ds(e, 1)].rearrange("a (p c) d -> p (a c d)", c=2)
                if not isinstance(e, int):
                    for s in (gate, up, down):
                        sp.lower_ap_dma(s)
                if isinstance(e, int) and l * E + e < NSLOT:
                    pass
                else:
                    sp.wait_ge(dn_done, HEAD + l * E + e - 3)
                flat = wslot(j)
                sp.dma_start(flat[:, 0:KD * FF], gate).then_inc(gu_in[j], 16)
                sp.dma_start(flat[:, KD * FF:2 * KD * FF], up).then_inc(gu_in[j], 16)
                sp.dma_start(flat[:, 2 * KD * FF:SLOT], down).then_inc(dn_in[j], 16)

            for q in ov_through:
                sp.sem_inc(q, HEAD)
            for n in range(N_FIRST):
                if n == 4:
                    for t in range(T):
                        sp.dma_start(h[:, t, :], x[0, t * P:(t + 1) * P, :]).then_inc(x_in, 16)
                load_ada(n)
            wsrc = w_in[0].rearrange("(p k) n -> p k n", k=KD)
            sp.dma_start(win[:, :, 0:B0], wsrc[:, :, 0:B0]).then_inc(win_in[0], 16)
            sp.wait_ge(modc_in[0], 32)
            for n in range(N_FIRST, N_FIRST + 2):
                load_ada(n)
            for n in range(N_FIRST + 2, N_MIX):
                if n < N_FIRST + 5:
                    at0 = (B0, C0, X0)[n - N_FIRST - 2]
                    sp.dma_start(win[:, :, at0:at0 + 512], wsrc[:, :, at0:at0 + 512]).then_inc(win_in[1], 16)
                load_ada(n)
            sp.wait_ge(proj_ready, len(PROJ))
            sp.wait_ge(proj_dve, len(PROJ) - act_before[-1])
            sp.dma_start(wo_conv, w_out[0, AW:, :].rearrange("(c p) n -> p c n", p=P)).then_inc(wout_in, 16)
            sp.dma_start(wo_att, w_out[0, 0:AW, :].rearrange("(c p) n -> p c n", p=P)).then_inc(wout_in, 16)
            for n in range(N_MIX, LAYERS * NCH):
                load_ada(n)
            for e in range(3):
                load_expert(0, e, e)
            sp.wait_ge(ada_mac, LAYERS * NCH)
            sp.dma_start(wpool, w_pool[0].rearrange("g (c p) n -> p (g c) n", p=P)).then_inc(wpool_in, 16)
            sp.dma_start(psc, pool_scale.partition_broadcast(P).rearrange("p a d -> p (a d)")).then_inc(psc_in, 16)
            for l in range(LAYERS):
                for t in range(T):
                    sp.wait_ge(xhat_ready, (2 * l + 1) * T + t + 1)
                    sp.dma_start(xhat_dram[l][t * P:(t + 1) * P, :], xhat[:, t, :]).then_inc(xhat_stored, 16)
                sp.wait_ge(xhat_stored, 16 * T * (l + 1))
                sp.wait_ge(logits_ready, l + 1)
                load_expert(l, 3, 3)
                with sp.Fori(1, E // 4) as i:
                    for j in range(4):
                        load_expert(l, 4 * i + j, j)
                overflow_sync(sp, l)
                for j in range(2):
                    sp.wait_ge(y_out[j], 8 * E * (l + 1))
                sp.wait_ge(dn_done, HEAD + E * (l + 1))
                for t in range(T):
                    for a in range(2):
                        sp.dma_start(ycomb[:, t, a, :], y_dram[l][a * SEQ + t * P:a * SEQ + (t + 1) * P, :]
                                     ).then_inc(y_in[t], 16)
                if l == 0:
                    for e in range(3):
                        load_expert(1, e, e)
            for t in range(T):
                sp.wait_ge(out_ready, t + 1)
                sp.dma_start(out[0, t * P:(t + 1) * P, :], xhat[:, t, :]).then_inc(out_stored, 16)
            sp.wait_ge(out_stored, 16 * T)

        @block.gpsimd
        def _(pool):
            def load_cols(s, last_chunk):
                l, half = s // 2, s % 2
                mod_waits(pool, l * NCH + last_chunk)
                off = 3 * half * D
                for a in range(2):
                    src = mod_dram[l, off + a * D:off + (a + 1) * D]
                    src = src.rearrange("(k p) -> p k", p=P) if s == 2 else src.rearrange("(p k) -> p k", k=KD)
                    pool.dma_start(modc[:, s, a, :], src).then_inc(modc_in[s], 16)

            def load_gate(l, half):
                off = (3 * half + 2) * D
                mod_waits(pool, l * NCH + ((off + D - 1) // AC))
                pool.dma_start(gbc[:, :] if half else gmix[l], mod_dram[l:l + 1, off:off + D].partition_broadcast(P)
                               .rearrange("p a d -> p (a d)")).then_inc(gbc_in, 16)

            load_cols(0, N_FIRST - 1)
            load_gate(0, 0)
            for u in range(ATT_U):
                b = u // KVH
                pool.wait_ge(rden_ready, u + 1)
                lo = 0 if b else P
                part = prob[:, u % 2, :, lo:]
                pool.tensor_tensor(part, part, sm[:, u % 2, 4, :].unsqueeze(2).broadcast_to([P, GH, 256 - lo]),
                                   ALU.mult).then_inc(prob_ready, 1)
            for l in range(LAYERS):
                if l == 0:
                    load_cols(1, (5 * D - 1) // AC)
                pool.wait_ge(h_ready, (2 * l + 1) * T)
                load_gate(l, 1)
                if l == 0:
                    load_cols(2, N_FIRST - 1)
                    load_cols(3, (5 * D - 1) // AC)
                    mod_waits(pool, LAYERS * NCH - 1)
                    load_gate(1, 0)
                pool.memset(xg[:, :, :], 0.0).then_inc(xg_clear, 1)
                pool.wait_ge(xg_clear, l + 1)
                pool.wait_ge(xhat_stored, 16 * T * (l + 1))

                def scatter(e):
                    pool.wait_ge(y_ready, HEAD + l * E + e + 1)
                    pool.indirect_dma_start(
                        out=y_dram[l], out_offset=bass.IndirectOffsetOnAxis(dst_i[:, e:e + 1], 0),
                        in_=yrow[:, e % 2, :], in_offset=None, bounds_check=2 * SEQ - 1, oob_is_err=False
                    ).then_inc(y_out[e % 2], 16)

                for e in range(E):
                    if e % EPG == 0:
                        pool.wait_ge(table_ready, l * EG + e // EPG + 1)
                    if e >= 4:
                        pool.wait_ge(xT_banked, l * E + e - 3)
                    pool.indirect_dma_start(
                        out=xg[:, e % 4, :], out_offset=None, in_=xhat_dram[l],
                        in_offset=bass.IndirectOffsetOnAxis(tok_i[:, e:e + 1], 0),
                        bounds_check=SEQ - 1, oob_is_err=False).then_inc(xg_in[e % 4], 16)
                    if e >= 3:
                        scatter(e - 3)
                for e in range(E - 3, E):
                    scatter(e)
                for j in range(2):
                    pool.wait_ge(y_out[j], 8 * E * (l + 1))

                pool.wait_ge(flag_ready, l + 1)
                most = pool.value_load(flag[0:1, l:l + 1], min_val=0, max_val=SEQ)
                bound, zero = pool.alloc_register(f"bound{l}"), pool.to_reg(0)
                with pool.If(most > P):
                    with pool.Fori(0, ROUNDS * E) as n:
                        pool.wait_ge(ov_idx[l], n + 1)
                        pool.reg_add(bound, zero, SEQ - 1)
                        pool.indirect_dma_start(
                            out=xg[:, 0, :], out_offset=None, in_=xhat_dram[l],
                            in_offset=bass.IndirectOffsetOnAxis(ovtok[:, 0:1], 0),
                            bounds_check=bound, oob_is_err=False).then_inc(ov_xg[l], 16)
                        pool.wait_ge(ov_y[l], n + 1)
                        pool.reg_add(bound, zero, 2 * SEQ - 1)
                        pool.indirect_dma_start(
                            out=y_dram[l], out_offset=bass.IndirectOffsetOnAxis(ovdst[:, 0:1], 0),
                            in_=yrow[:, 0, :], in_offset=None, bounds_check=bound, oob_is_err=False
                        ).then_inc(ov_out[l], 16)

            pool.dma_start(gbc[:, :], norm_final.rearrange("(a d) -> a d", a=1).partition_broadcast(P)
                           .rearrange("p a d -> p (a d)")).then_inc(gbc_in, 16)

        @block.scalar
        def _(act):
            alink = [0]

            def link(ins):
                alink[0] += 1
                ins.then_inc(link_act, 1)
                act.wait_ge(link_act, alink[0])

            act.sem_inc(hT_ready, HEAD)
            act.dma_start(craw[:, :], c[0].rearrange("(p k) -> p k", k=KD)).then_inc(c_in, 16)
            act.dma_start(cst[:, :], consts).then_inc(const_in, 16)
            act.wait_ge(c_in, 16)
            act.activation(cond[:, :], craw[:, :], ACT.Silu).then_inc(cond_ready, 1)
            for s in range(4):
                src = (norm_ffn if s % 2 else norm_mix)[s // 2]
                src = src.rearrange("(k p) -> p k", p=P) if s == 2 else src.rearrange("(p k) -> p k", k=KD)
                act.dma_start(normc[:, s, :], src).then_inc(small_in, 16)
            act.dma_start(wr[:, :, :], w_router.rearrange("(p k) e -> p k e", k=KD)).then_inc(small_in, 16)
            act.dma_start(brb[:, :], b_router.rearrange("(a e) -> a e", a=1).partition_broadcast(P)
                          .rearrange("p a e -> p (a e)")).then_inc(small_in, 16)
            for kv in range(KVH):
                for odd in range(2):
                    src = sinks[:, kv * GH + odd:(kv + 1) * GH:2].partition_broadcast(P).rearrange("p a e -> p (a e)")
                    act.dma_start(snk[:, 0, kv * GH + 2 * odd:kv * GH + 2 * odd + 2], src).then_inc(small_in, 16)
            act.dma_start(cvw[:, :, :], conv_w[0].rearrange("j (c p) -> p j c", p=P)).then_inc(small_in, 16)

            def ada_out(n):
                b, l, q = n % 2, n // NCH, n % NCH
                act.wait_ge(ada_sum, n + 1)
                if n >= 2:
                    act.wait_ge(mod_stored[b], 16 * (n // 2))
                act.activation(mrow[0:1, b, :], ps5[0:1, 0:AC], ACT.Copy).then_inc(row_copied, 1)
                act.wait_ge(row_copied, n + 1)
                act.dma_start(mod_dram[l:l + 1, q * AC:(q + 1) * AC], mrow[0:1, b, :]).then_inc(mod_stored[b], 16)

            def norm(s):
                for t in range(T):
                    if s == 0:
                        act.wait_ge(x_in, 16 * T)
                    else:
                        act.wait_ge(h_ready, (s - 1) * T + t + 1)
                    link(act.activation(junk, h[:, t, :], ACT.Square, accum_out=ss[:, t:t + 1]))
                act.wait_ge(eps_ready, 1)
                act.activation(rstd[:, :], ss[:, :], ACT.Sqrt, bias=eps[:, 0:1], scale=1.0 / D).then_inc(std_done, 1)

            def spread(s):
                for k in range(0, KD, 2):
                    if k == 0:
                        act.wait_ge(scl_ready, s + 1)
                    act.wait_ge(uT_banked, KD * s + k + 1)
                    act.activation(uT[:, k, :], psA[:, 0:512], ACT.Identity, scale=scl[:, s, k:k + 1],
                                   bias=modc[:, s, 0, k:k + 1]).then_inc(uT_act, 1)

            for n in range(N_FIRST):
                ada_out(n)
            norm(0)
            spread(0)

            def empty(m):
                name, i = PROJ[m]
                if name not in ACT_SIDE:
                    return
                act.wait_ge(proj_ready, m + 1)
                bank = psY[:, (m % 2) * 512:(m % 2 + 1) * 512]
                if name == "q":
                    dst = qT[:, i, :]
                elif name == "k":
                    dst = kT
                elif name == "v":
                    dst = vtok.rearrange("p t n -> p (t n)")
                else:
                    dst = cuT[:, i, :]
                act.activation(dst, bank, ACT.Copy).then_inc(proj_act, 1)
                if name == "k":
                    act.wait_ge(proj_act, act_before[m + 1])
                    act.dma_start(kswap[HD:P], kT[0:HD]).then_inc(kswap_in, 16)
                    act.dma_start(kswap[0:HD], kT[HD:P]).then_inc(kswap_in, 16)

            def exps(u):
                b, pb = u // KVH, u % 2
                act.wait_ge(negmax_ready, u + 1)
                lo = 0 if b else P
                for g in range(GH):
                    act.activation(prob[:, pb, g, lo:], prob[:, pb, g, lo:], ACT.Exp, scale=HD ** -0.5,
                                   bias=sm[:, pb, 1, g:g + 1], accum_out=sm[:, pb, 2, g:g + 1])
                act.activation(sm[:, pb, 3, :], sm[:, pb, 5, :], ACT.Exp).then_inc(exp_done, 1)

            def empty_probT(u):
                b = u // KVH
                act.wait_ge(probT_banked, u + 1)
                if u:
                    act.wait_ge(att_banked, u)
                if b:
                    act.activation(probT[:, 0, :], ps2[:, :], ACT.Copy)
                act.activation(probT[:, 1, :], ps3[:, :], ACT.Copy).then_inc(probT_ready, 1)

            def empty_att(b):
                act.wait_ge(att_banked, KVH * (b + 1))
                act.activation(attnT[:, :, b * P:(b + 1) * P], ps4[:, :].rearrange("p (c s) -> p c s", c=4),
                               ACT.Copy).then_inc(att_ready, 1)

            for m in range(6):
                empty(m)
                if m:
                    ada_out(N_FIRST + m - 1)
            for u in range(ATT_U + 1):
                if u:
                    empty_probT(u - 1)
                if u < ATT_U:
                    exps(u)
                for m in BESIDE[u][0]:
                    empty(m)
                if u and u % KVH == 0:
                    empty_att(u // KVH - 1)
                if u:
                    for n in unit_totals(u - 1):
                        ada_out(n)
                for m in BESIDE[u][1]:
                    empty(m)
            n = N_MIX
            for count in BY_TILE:
                for _ in range(count):
                    ada_out(n)
                    n += 1

            def expert_loop(l):
                def xT_half(e, j, i):
                    act.wait_ge(xT_banked, l * E + e + 1)
                    for k in range(KD // 2):
                        ins = act.activation(xgT[:, j % 2, k, :], psA[:, k * P:(k + 1) * P], ACT.Identity,
                                             scale=scl[:, 2 * l + 1, k:k + 1], bias=modc[:, 2 * l + 1, 0, k:k + 1])
                    ins.then_inc(xT_act, 1)

                def silu(e, j, i):
                    act.wait_ge(gu_done, l * E + e + 1)
                    act.activation(sil[:, j % 2, :], gu_ps[j % 2][:, 0:FF], ACT.Silu).then_inc(sil_ready, 1)

                def body(e, j, i):
                    static = isinstance(e, int)
                    if not static or e + 1 < E:
                        act.wait_ge(hid_ready, HEAD + l * E + e)
                        silu(e + 1, j + 1, i)
                    act.wait_ge(hT_banked, HEAD + l * E + e + 1)
                    act.wait_ge(dn_done, HEAD + l * E + e)
                    act.activation(hT.rearrange("p a s -> p (a s)"), ps2[:, 0:2 * P], ACT.Copy).then_inc(hT_ready, 1)
                    if not static or e + 2 < E:
                        act.wait_ge(gu_done, l * E + e + 1)
                        xT_half(e + 2, j, i)

                act.wait_ge(table_ready, EG * (l + 1))
                xT_half(0, 0, 0)
                xT_half(1, 1, 0)
                silu(0, 0, 0)
                loop_experts(act, body)

                act.wait_ge(flag_ready, l + 1)
                most = act.value_load(flag[0:1, l:l + 1], min_val=0, max_val=SEQ)
                with act.If(most > P):
                    with act.Fori(0, ROUNDS * E) as n:
                        act.wait_ge(ov_xb[l], n + 1)
                        for k in range(KD):
                            ins = act.activation(xgT[:, 0, k, :], psA[:, k * P:(k + 1) * P], ACT.Identity,
                                                 scale=scl[:, 2 * l + 1, k:k + 1],
                                                 bias=modc[:, 2 * l + 1, 0, k:k + 1])
                        ins.then_inc(ov_xT[l], 1)
                        act.wait_ge(ov_gu[l], n + 1)
                        act.activation(sil[:, 0, :], ps3[:, 0:FF], ACT.Silu).then_inc(ov_sil[l], 1)
                        act.wait_ge(ov_hb[l], n + 1)
                        act.activation(hT.rearrange("p a s -> p (a s)"), ps2[:, 0:2 * P], ACT.Copy
                                       ).then_inc(ov_hT[l], 1)

            for l in range(LAYERS):
                if l:
                    norm(2)
                    spread(2)
                norm(2 * l + 1)
                spread(2 * l + 1)
                act.wait_ge(logits_ready, l + 1)
                act.activation(logT, ps2[0:E, :], ACT.Copy).then_inc(logT_ready, 1)
                act.wait_ge(logits_turned, l + 1)
                act.activation(sig_tile, ps3[:, 0:T * E], ACT.Sigmoid).then_inc(sig_ready, 1)
                expert_loop(l)
            norm(4)

        @block.vector
        def _(dve):
            dlink = [0]

            def link(ins):
                dlink[0] += 1
                ins.then_inc(link_dve, 1)
                dve.wait_ge(link_dve, dlink[0])

            def ada_mul(n):
                b = n % 2
                if n >= 3:
                    dve.wait_ge(ada_sum, n - 2)
                for k in range(KD):
                    if k == 0:
                        dve.wait_ge(ada_in[2 * b], 32 * (n // 2 + 1))
                    if k == 1 and n:
                        dve.wait_ge(ada_mac, n)
                    if k == KD // 2:
                        dve.wait_ge(ada_in[2 * b + 1], 16 * (n // 2 + 1))
                    part = acc[:, 3 if k % 2 else n % 3, :]
                    if k < 2:
                        if k == 0:
                            ins = dve.scalar_tensor_tensor(part, adaw[:, b, k, :], cond[:, k:k + 1], brow[:, b, :],
                                                           ALU.mult, ALU.add)
                        else:
                            ins = dve.tensor_scalar(part, adaw[:, b, k, :], cond[:, k:k + 1], None, ALU.mult)
                    else:
                        dve.wait_ge(mac_step, n * KD + k - 1)
                        ins = dve.scalar_tensor_tensor(part, adaw[:, b, k, :], cond[:, k:k + 1], part,
                                                       ALU.mult, ALU.add)
                    ins.then_inc(mac_step, 1)
                dve.wait_ge(mac_step, (n + 1) * KD)
                dve.tensor_tensor(acc[:, n % 3, :], acc[:, n % 3, :], acc[:, 3, :], ALU.add).then_inc(ada_mac, 1)

            def norm(s):
                dve.wait_ge(std_done, s + 1)
                link(dve.reciprocal(rstd[:, :], rstd[:, :]))
                for t in range(T):
                    dve.tensor_scalar(xhat[:, t, :], h[:, t, :], rstd[:, t:t + 1], None, ALU.mult
                                      ).then_inc(xhat_ready, 1)

            def spread(s):
                dve.wait_ge(modc_in[s], 32)
                dve.scalar_tensor_tensor(scl[:, s, :], modc[:, s, 1, :], 1.0, normc[:, s, :], ALU.add, ALU.mult
                                         ).then_inc(scl_ready, 1)
                dve.wait_ge(scl_ready, s + 1)
                for k in range(1, KD, 2):
                    dve.wait_ge(uT_banked, KD * s + k + 1)
                    dve.tensor_scalar(uT[:, k, :], psA[:, 512:1024], scl[:, s, k:k + 1], modc[:, s, 0, k:k + 1],
                                      ALU.mult, ALU.add).then_inc(uT_dve, 1)

            def mix_in(l, t):
                dve.wait_ge(mix_banked, l * T + t + 1)
                link(dve.tensor_tensor(mixt[:, t % 2, :], pair[t % 2][:, :], gmix[l], ALU.mult))
                dve.tensor_tensor(h[:, t, :], h[:, t, :], mixt[:, t % 2, :], ALU.add).then_inc(h_ready, 1)

            def ffn_in(l, t):
                dve.wait_ge(y_in[t], 32 * (l + 1))
                link(dve.tensor_tensor(h[:, t, :], h[:, t, :], ycomb[:, t, 0, :], ALU.add))
                dve.tensor_tensor(h[:, t, :], h[:, t, :], ycomb[:, t, 1, :], ALU.add).then_inc(h_ready, 1)

            for q in (hid_ready, y_ready, *ov_link):
                dve.sem_inc(q, HEAD)
            dve.memset(eps[:, :], EPS).then_inc(eps_ready, 1)
            dve.memset(brow[:, :, :], 0.0).then_inc(brow_clear, 1)
            dve.wait_ge(cond_ready, 1)
            dve.wait_ge(const_in, 16)
            dve.tensor_copy(cstb[:, 0:P], before)
            dve.tensor_copy(cstb[:, P:2 * P], ones).then_inc(cstb_ready, 1)
            for n in range(N_FIRST):
                ada_mul(n)
            norm(0)
            dve.wait_ge(small_in, 16 * N_SMALL)
            spread(0)
            link(dve.tensor_scalar(snk[:, 1, :], snk[:, 0, :], HD ** 0.5, None, ALU.mult))

            def empty(m):
                name, i = PROJ[m]
                if name in ACT_SIDE:
                    return
                dve.wait_ge(proj_ready, m + 1)
                bank = psY[:, (m % 2) * 512:(m % 2 + 1) * 512]
                if name == "x":
                    dve.wait_ge(proj_act, act_before[m])
                    ins = dve.tensor_tensor(cuT[:, i, :], cuT[:, i, :], bank, ALU.mult)
                    ins.then_inc(proj_dve, 1)
                    dve.wait_ge(proj_dve, m - act_before[m] + 1)
                    link(dve.tensor_scalar(convT[:, i, :], cuT[:, i, :], cvw[:, 2, i:i + 1], None, ALU.mult))
                    for back in (1, 2):
                        link(dve.scalar_tensor_tensor(convT[:, i, back:], cuT[:, i, 0:SEQ - back],
                                                      cvw[:, 2 - back, i:i + 1], convT[:, i, back:],
                                                      ALU.mult, ALU.add))
                else:
                    dve.tensor_tensor(convT[:, i, :], convT[:, i, :], bank, ALU.mult).then_inc(proj_dve, 1)

            def soften(u):
                b, kv, pb = u // KVH, u % KVH, u % 2
                lo = 0 if b else P
                dve.wait_ge(scores_ready, u + 1)
                if u >= 2:
                    dve.wait_ge(probT_banked, u - 1)
                for g in range(GH):
                    slope = 2.0 ** (-8.0 * (HEAD_AT[kv][g] + 1) / HEADS)
                    ins = dve.scalar_tensor_tensor(prob[:, pb, g, lo:], cst[:, C_DIST + lo:C_DIST + 256],
                                                   -slope * HD ** 0.5, psA[:, g * 256 + lo:(g + 1) * 256],
                                                   ALU.mult, ALU.add)
                ins.then_inc(scores_read, 1)
                dve.wait_ge(scores_read, u + 1)
                link(dve.tensor_reduce(sm[:, pb, 0, :], prob[:, pb, :, lo:], AX.X, ALU.max))
                link(dve.tensor_tensor(sm[:, pb, 0, :], sm[:, pb, 0, :], snk[:, 1, kv * GH:(kv + 1) * GH], ALU.max))
                link(dve.tensor_scalar(sm[:, pb, 1, :], sm[:, pb, 0, :], -(HD ** -0.5), None, ALU.mult))
                dve.tensor_tensor(sm[:, pb, 5, :], sm[:, pb, 1, :], snk[:, 0, kv * GH:(kv + 1) * GH], ALU.add
                                  ).then_inc(negmax_ready, 1)

            def divide(u):
                pb = u % 2
                dve.wait_ge(exp_done, u + 1)
                link(dve.tensor_tensor(sm[:, pb, 2, :], sm[:, pb, 2, :], sm[:, pb, 3, :], ALU.add))
                dve.reciprocal(sm[:, pb, 4, :], sm[:, pb, 2, :]).then_inc(rden_ready, 1)

            for m in range(6):
                ada_mul(N_FIRST + m)
            for u in range(ATT_U):
                soften(u)
                for m in BESIDE[u][0]:
                    empty(m)
                divide(u)
                for m in BESIDE[u][1]:
                    empty(m)
                for n in unit_chunks(u):
                    ada_mul(n)
            dve.wait_ge(gbc_in, 16)
            n = N_MIX
            for t in range(T):
                for _ in range(BY_TILE[t]):
                    ada_mul(n)
                    n += 1
                mix_in(0, t)

            def tiny(n, at0):
                return small[:, at0:at0 + n]

            bia = tiny(64, 64)
            prs = tiny(96, 128)
            gs = tiny(16, 224)
            gm = tiny(4, 240)
            ing = tiny(16, 244)
            vmx = tiny(4, 260)
            gtt = tiny(256, 264)
            eqt = tiny(256, 520)
            rank = tiny(64, 776)
            sel = sel_tile
            ws = tiny(64, 904)
            wsum = tiny(4, 968)
            gate = tiny(64, 972)
            rest = tiny(64, 1036)
            tab = tiny(24, 1100)

            def route(l):
                dve.wait_ge(sig_ready, l + 1)
                b3 = bia.rearrange("p (g i) -> p g i", i=EPG)
                pr = prs.rearrange("p (g c) -> p g c", c=6)
                link(dve.tensor_tensor(bia.rearrange("p (t e) -> p t e", t=T), sig_tile.rearrange("p (t e) -> p t e", t=T),
                                       brb[:, :].unsqueeze(1).broadcast_to([P, T, E]), ALU.add))
                b4 = bia.rearrange("p (g a i) -> p g a i", a=2, i=2)
                dve.tensor_tensor(pr[:, :, 0:2], b4[:, :, :, 0], b4[:, :, :, 1], ALU.add)
                dve.tensor_tensor(pr[:, :, 2:4], b3[:, :, 0:2], b3[:, :, 2:4], ALU.add)
                dve.tensor_tensor(pr[:, :, 4:5], b3[:, :, 0:1], b3[:, :, 3:4], ALU.add)
                link(dve.tensor_tensor(pr[:, :, 5:6], b3[:, :, 1:2], b3[:, :, 2:3], ALU.add))
                link(dve.tensor_reduce(gs, pr, AX.X, ALU.max))
                g3 = gs.rearrange("p (t g) -> p t g", t=T)
                v3 = ing.rearrange("p (t g) -> p t g", t=T)
                link(dve.tensor_reduce(gm, g3, AX.X, ALU.max))
                link(dve.tensor_tensor(v3, g3, gm.unsqueeze(2).broadcast_to([P, T, EG]), ALU.is_equal))
                link(dve.tensor_tensor(v3, v3, cst[:, C_FST:C_FST + EG].unsqueeze(1).broadcast_to([P, T, EG]), ALU.mult))
                link(dve.tensor_reduce(vmx, v3, AX.X, ALU.max))
                link(dve.tensor_tensor(v3, v3, vmx.unsqueeze(2).broadcast_to([P, T, EG]), ALU.is_equal))
                bj = b3.unsqueeze(2).broadcast_to([P, E, EPG, EPG])
                bi = b3.unsqueeze(3).broadcast_to([P, E, EPG, EPG])
                gt4 = gtt.rearrange("p (g i j) -> p g i j", i=EPG, j=EPG)
                eq4 = eqt.rearrange("p (g i j) -> p g i j", i=EPG, j=EPG)
                dve.tensor_tensor(gt4, bj, bi, ALU.is_gt)
                link(dve.tensor_tensor(eq4, bj, bi, ALU.is_equal))
                link(dve.tensor_tensor(eqt.rearrange("p (g q) -> p g q", q=16), eqt.rearrange("p (g q) -> p g q", q=16),
                                       cst[:, C_JLT:C_JLT + 16].unsqueeze(1).broadcast_to([P, E, 16]), ALU.mult))
                link(dve.tensor_tensor(gtt, gtt, eqt, ALU.add))
                link(dve.tensor_reduce(rank, gtt.rearrange("p (g j) -> p g j", j=EPG), AX.X, ALU.add))
                dve.scalar_tensor_tensor(sel.rearrange("p (g i) -> p g i", i=EPG), rank.rearrange("p (g i) -> p g i", i=EPG),
                                         2.0, ing.unsqueeze(2).broadcast_to([P, E, EPG]), ALU.is_lt, ALU.mult
                                         ).then_inc(sel_ready, 1)
                dve.wait_ge(sel_ready, l + 1)
                link(dve.tensor_tensor(ws, sig_tile, sel, ALU.mult))
                ws3 = ws.rearrange("p (t e) -> p t e", t=T)
                link(dve.tensor_reduce(wsum, ws3, AX.X, ALU.add))
                link(dve.reciprocal(wsum, wsum))
                gt3 = gate.rearrange("p (t e) -> p t e", t=T)
                rs3 = rest.rearrange("p (t e) -> p t e", t=T)
                link(dve.tensor_tensor(gt3, ws3, wsum.unsqueeze(2).broadcast_to([P, T, E]), ALU.mult))
                tokc = cst[:, C_TOK:C_TOK + 8].rearrange("p (t c) -> p t c", t=T)
                dve.tensor_copy(rtab[:, :, :, 0:2], tokc.unsqueeze(2).broadcast_to([P, T, E, 2]))
                dve.scalar_tensor_tensor(rtab[:, :, :, 2], rank.rearrange("p (t e) -> p t e", t=T), float(SEQ),
                                         tokc[:, :, 1:2].broadcast_to([P, T, E]), ALU.mult, ALU.add)
                link(dve.tensor_copy(rtab[:, :, :, 3], gt3))
                link(dve.tensor_tensor(rs3, gt3, rtab[:, :, :, 3], ALU.subtract))
                link(dve.tensor_copy(rtab[:, :, :, 4], rs3))
                link(dve.tensor_tensor(rs3, rs3, rtab[:, :, :, 4], ALU.subtract))
                link(dve.tensor_copy(rtab[:, :, :, 5], rs3))
                dve.wait_ge(pos_ready, l + 1)
                sel3 = sel.rearrange("p (t e) -> p t e", t=T)
                pos3 = ps2[:, 0:T * E].rearrange("p (t e) -> p t e", t=T)
                dve.tensor_reduce(maxn[:, l:l + 1], ps2[:, T * E:T * E + E], AX.X, ALU.max)
                link(dve.scalar_tensor_tensor(posm, pos3, 1.0, sel3, ALU.add, ALU.mult))
                dve.tensor_copy(flag[:, l:l + 1], maxn[:, l:l + 1]).then_inc(flag_ready, 1)
                link(dve.tensor_scalar(posm, posm, -1.0, None, ALU.add))
                for g in range(EG + 1):
                    if g < EG:
                        if g >= 2:
                            dve.wait_ge(table_banked, l * EG + g - 1)
                        dve.tensor_tensor(
                            onehot[:, g % 2], cst[:, C_SLOT:C_SLOT + P].unsqueeze(1).unsqueeze(1).broadcast_to(
                                [P, T, EPG, P]),
                            posm[:, :, g * EPG:(g + 1) * EPG].unsqueeze(3).broadcast_to([P, T, EPG, P]),
                            ALU.is_equal).then_inc(onehot_ready, 1)
                    if g >= 1:
                        q = g - 1
                        cols = slice(q * EPG, (q + 1) * EPG)
                        t3 = tab.rearrange("p (e c) -> p e c", c=6)
                        dve.wait_ge(table_banked, l * EG + q + 1)
                        link(dve.tensor_copy(tab, (ps5 if q % 2 else ps4)[:, 0:24]))
                        dve.scalar_tensor_tensor(tok_i[:, cols], t3[:, :, 0], FAR, t3[:, :, 1], ALU.add, ALU.add)
                        dve.scalar_tensor_tensor(dst_i[:, cols], t3[:, :, 0], FAR, t3[:, :, 2], ALU.add, ALU.add)
                        link(dve.tensor_tensor(gslot[:, cols], t3[:, :, 3], t3[:, :, 4], ALU.add))
                        dve.tensor_tensor(gslot[:, cols], gslot[:, cols], t3[:, :, 5], ALU.add).then_inc(table_ready, 1)
                        dve.wait_ge(table_ready, l * EG + g)

            def expert_loop(l):
                def xT_half(e, j, i):
                    dve.wait_ge(xT_banked, l * E + e + 1)
                    for k in range(KD // 2, KD):
                        ins = dve.tensor_scalar(xgT[:, j % 2, k, :], psA[:, k * P:(k + 1) * P],
                                                scl[:, 2 * l + 1, k:k + 1], modc[:, 2 * l + 1, 0, k:k + 1],
                                                ALU.mult, ALU.add)
                    ins.then_inc(xT_dve, 1)

                def times_up(e, j, i):
                    dve.wait_ge(sil_ready, l * E + e + 1)
                    dve.tensor_tensor(hid[:, j % 2, :], sil[:, j % 2, :], gu_ps[j % 2][:, FF:2 * FF], ALU.mult
                                      ).then_inc(hid_ready, 1)

                def body(e, j, i):
                    static = isinstance(e, int)
                    if not static or e + 1 < E:
                        dve.wait_ge(hT_banked, HEAD + l * E + e)
                        times_up(e + 1, j + 1, i)
                    if not static or e + 2 < E:
                        dve.wait_ge(gu_done, l * E + e + 1)
                        xT_half(e + 2, j, i)
                    dve.wait_ge(dn_done, HEAD + l * E + e + 1)
                    if not static or l * E + e >= 2:
                        dve.wait_ge(y_out[j % 2], 16 * (l * (E // 2) + 2 * i + j // 2))
                    for a in range(2):
                        ins = dve.scalar_tensor_tensor(yrow[:, j % 2, a * 512:(a + 1) * 512],
                                                       psY[:, a * 512:(a + 1) * 512], gslot[:, bass.ds(e, 1)],
                                                       gbc[:, a * 512:(a + 1) * 512], ALU.mult, ALU.mult)
                    ins.then_inc(y_ready, 1)

                xT_half(0, 0, 0)
                xT_half(1, 1, 0)
                times_up(0, 0, 0)
                dve.wait_ge(gbc_in, 16 * (2 * l + 2))
                loop_experts(dve, body, first=1)

                dve.wait_ge(flag_ready, l + 1)
                most = dve.value_load(flag[0:1, l:l + 1], min_val=0, max_val=SEQ)
                with dve.If(most > P):
                    dve.wait_ge(y_out[1], 8 * E * (l + 1))
                    with dve.Fori(0, ROUNDS) as r:
                        dve.wait_ge(ov_link[l], HEAD + r * (1 + 2 * E))
                        dve.tensor_scalar(posm, posm, float(-P), None, ALU.add).then_inc(ov_link[l], 1)
                        with dve.Fori(0, E) as e:
                            n = r * E + e
                            dve.wait_ge(ov_link[l], HEAD + r * (1 + 2 * E) + 1 + 2 * e)
                            dve.wait_ge(ov_through[l], HEAD + n)
                            dve.tensor_copy(ovr, rtab[:, :, bass.ds(e, 1), :].rearrange("p t a c -> p t (a c)"))
                            dve.tensor_tensor(
                                onehot_ov, cst[:, C_SLOT:C_SLOT + P].unsqueeze(1).broadcast_to([P, T, P]),
                                posm[:, :, bass.ds(e, 1)].broadcast_to([P, T, P]),
                                ALU.is_equal).then_inc(ov_oh[l], 1)
                            dve.wait_ge(ov_tab[l], n + 1)
                            base = r * (1 + 2 * E) + 1 + 2 * e
                            dve.tensor_copy(ovtab[:, 0:6], ps4[:, 0:6]).then_inc(ov_link[l], 1)
                            dve.wait_ge(ov_link[l], HEAD + base + 1)
                            dve.scalar_tensor_tensor(ovtok, ovtab[:, 0:1], FAR, ovtab[:, 1:2], ALU.add, ALU.add)
                            dve.scalar_tensor_tensor(ovdst, ovtab[:, 0:1], FAR, ovtab[:, 2:3], ALU.add, ALU.add)
                            dve.tensor_tensor(ovgate, ovtab[:, 3:4], ovtab[:, 4:5], ALU.add).then_inc(ov_link[l], 1)
                            dve.wait_ge(ov_link[l], HEAD + base + 2)
                            dve.tensor_tensor(ovgate, ovgate, ovtab[:, 5:6], ALU.add).then_inc(ov_idx[l], 1)
                            dve.wait_ge(ov_sil[l], n + 1)
                            dve.tensor_tensor(hid[:, 0, :], sil[:, 0, :], ps3[:, FF:2 * FF], ALU.mult
                                              ).then_inc(ov_hid[l], 1)
                            dve.wait_ge(ov_dn[l], HEAD + n + 1)
                            dve.wait_ge(ov_idx[l], n + 1)
                            for a in range(2):
                                ins = dve.scalar_tensor_tensor(yrow[:, 0, a * 512:(a + 1) * 512],
                                                               psY[:, a * 512:(a + 1) * 512], ovgate[:, 0:1],
                                                               gbc[:, a * 512:(a + 1) * 512], ALU.mult, ALU.mult)
                            ins.then_inc(ov_y[l], 1)

            def pool_means():
                for g in range(4):
                    w = 2 << g
                    src = uT[:, 2 * g:2 * g + 2, :]
                    cur, back = src, 1
                    step = 0
                    while back < w:
                        nxt = run[:, step % 2]
                        dve.tensor_copy(nxt[:, :, 0:back], cur[:, :, 0:back])
                        link(dve.tensor_tensor(nxt[:, :, back:], cur[:, :, back:], cur[:, :, 0:SEQ - back], ALU.add))
                        cur, back, step = nxt, 2 * back, step + 1
                    link(dve.tensor_tensor(cur[:, :, 0:w - 1], cur[:, :, 0:w - 1],
                                           cst[:, C_INV:C_INV + w - 1].unsqueeze(1).broadcast_to([P, 2, w - 1]),
                                           ALU.mult))
                    dve.tensor_tensor(pooled[:, 2 * g:2 * g + 2, 0:w - 1], cur[:, :, 0:w - 1], src[:, :, 0:w - 1],
                                      ALU.subtract)
                    link_next = dve.scalar_tensor_tensor(pooled[:, 2 * g:2 * g + 2, w - 1:], cur[:, :, w - 1:],
                                                         1.0 / w, src[:, :, w - 1:], ALU.mult, ALU.subtract)
                    link_next.then_inc(pooled_ready, 1)
                    dve.wait_ge(pooled_ready, g + 1)

            for l in range(LAYERS):
                if l:
                    norm(2)
                    spread(2)
                    dve.wait_ge(uT_act, (2 * l + 1) * KD // 2)
                    dve.wait_ge(uT_dve, (2 * l + 1) * KD // 2)
                    pool_means()
                    for t in range(T):
                        mix_in(1, t)
                norm(2 * l + 1)
                spread(2 * l + 1)
                route(l)
                expert_loop(l)
                if l == 0:
                    dve.wait_ge(gbc_in, 16 * 3)
                    dve.wait_ge(psc_in, 16)
                    link(dve.tensor_tensor(gmix[1], gmix[1], psc, ALU.mult))
                for t in range(T):
                    ffn_in(l, t)
            dve.wait_ge(std_done, 5)
            link(dve.reciprocal(rstd[:, :], rstd[:, :]))
            dve.wait_ge(gbc_in, 16 * 5)
            for t in range(T):
                dve.scalar_tensor_tensor(xhat[:, t, :], h[:, t, :], rstd[:, t:t + 1], gbc[:, :], ALU.mult, ALU.mult
                                         ).then_inc(out_ready, 1)

        @block.tensor
        def _(pe):
            def ada_total(n):
                pe.wait_ge(ada_mac, n + 1)
                if n:
                    pe.wait_ge(row_copied, n)
                pe.matmul(ps5[0:1, 0:AC], ones[:, 0:1], acc[:, n % 3, :], start=True, stop=True
                          ).then_inc(ada_sum, 1)

            def logits(s, k):
                if s == 1 and k == 0:
                    pe.wait_ge(small_in, 16 * N_SMALL)
                pe.wait_ge(uT_dve if k % 2 else uT_act, s * KD // 2 + k // 2 + 1)
                ins = pe.matmul(ps2[0:E, :], wr[:, k, :], uT[:, k, :], start=(k == 0), stop=(k == KD - 1))
                if k == KD - 1:
                    ins.then_inc(logits_ready, 1)

            def transposes(s):
                pe.wait_ge(xhat_ready, (s + 1) * T)
                for k in range(KD):
                    bank = psA[:, (k % 2) * 512:(k % 2 + 1) * 512]
                    if k >= 2:
                        pe.wait_ge(uT_dve if k % 2 else uT_act, s * KD // 2 + k // 2)
                    for t in range(T):
                        if s == 2:
                            src = xhat[:, t, k * P:(k + 1) * P]
                        else:
                            src = xhat[:, t, :].rearrange("p (a k) -> p k a", k=KD)[:, k, :]
                        ins = pe.transpose(bank[:, t * P:(t + 1) * P], src, ident)
                    ins.then_inc(uT_banked, 1)
                    if s % 2 and k:
                        logits(s, k - 1)
                if s % 2:
                    logits(s, KD - 1)

            for q in (dn_done, hT_banked, *ov_dn):
                pe.sem_inc(q, HEAD)
            pe.wait_ge(const_in, 16)
            for n in range(N_FIRST):
                ada_total(n)
            transposes(0)

            def project(m):
                name, i = PROJ[m]
                bank = psY[:, (m % 2) * 512:(m % 2 + 1) * 512]
                if m == 0:
                    pe.wait_ge(uT_act, KD // 2)
                    pe.wait_ge(uT_dve, KD // 2)
                    pe.wait_ge(win_in[0], 16)
                if m == 6:
                    pe.wait_ge(win_in[1], 48)
                if m >= 2:
                    if PROJ[m - 2][0] in ACT_SIDE:
                        pe.wait_ge(proj_act, act_before[m - 1])
                    else:
                        pe.wait_ge(proj_dve, m - 1 - act_before[m - 1])
                if name == "v":
                    for t in range(T):
                        for k in range(KD):
                            ins = pe.matmul(bank[:, t * P:(t + 1) * P], uT[:, k, t * P:(t + 1) * P],
                                            win[:, k, V0:V0 + P], start=(k == 0), stop=(k == KD - 1))
                else:
                    for k in range(KD):
                        at0 = {"q": 0, "k": K0, "c": C0, "x": X0, "b": B0}[name] + i * P
                        wt = win[:, k, at0:at0 + P]
                        ins = pe.matmul(bank, wt, uT[:, k, :], start=(k == 0), stop=(k == KD - 1))
                ins.then_inc(proj_ready, 1)

            def scores(u):
                b, kv = u // KVH, u % KVH
                if u == 0:
                    pe.wait_ge(proj_act, 6)
                    pe.wait_ge(kswap_in, 32)
                if u:
                    pe.wait_ge(scores_read, u)
                lo = 0 if b else P
                for g in range(GH):
                    odd, i = g // 2, g % 2
                    rows = slice(odd * HD, (odd + 1) * HD)
                    ins = pe.matmul(psA[:, g * 256 + lo:(g + 1) * 256], qT[rows, kv * 2 + i, b * P:(b + 1) * P],
                                    (kT if odd == kv else kswap)[rows, (b - 1) * P + lo:(b + 1) * P],
                                    start=True, stop=True)
                ins.then_inc(scores_ready, 1)

            def turn_prob(u):
                b = u // KVH
                pe.wait_ge(prob_ready, u + 1)
                if u:
                    pe.wait_ge(probT_ready, u)
                for kb in range(0 if b else 1, 2):
                    for g in range(GH):
                        ins = pe.transpose((ps3 if kb else ps2)[:, g * P:(g + 1) * P],
                                           prob[:, u % 2, g, kb * P:(kb + 1) * P], ident)
                ins.then_inc(probT_banked, 1)

            def attend(u):
                b, kv = u // KVH, u % KVH
                pe.wait_ge(probT_ready, u + 1)
                if kv == 0 and b:
                    pe.wait_ge(att_ready, b)
                for g in range(GH):
                    odd, i = g // 2, g % 2
                    dst = ps4[odd * HD:(odd + 1) * HD, (kv * 2 + i) * P:(kv * 2 + i + 1) * P]
                    for kb in range(0 if b else 1, 2):
                        ins = pe.matmul(dst, vtok[:, b - 1 + kb, kv * HD:(kv + 1) * HD],
                                        probT[:, kb, g * P:(g + 1) * P], start=(kb == 0 or b == 0), stop=(kb == 1))
                ins.then_inc(att_banked, 1)

            for m in range(6):
                project(m)
                if m:
                    ada_total(N_FIRST + m - 1)
            for u in range(ATT_U + 1):
                if u < ATT_U:
                    scores(u)
                if u:
                    turn_prob(u - 1)
                for m in BESIDE[u][0]:
                    project(m)
                if u:
                    attend(u - 1)
                    for n in unit_totals(u - 1):
                        ada_total(n)
                for m in BESIDE[u][1]:
                    project(m)

            def mix_out(t):
                ps = pair[t % 2]
                if t == 0:
                    pe.wait_ge(wout_in, 32)
                    pe.wait_ge(att_ready, T)
                    pe.wait_ge(proj_dve, len(PROJ) - act_before[-1])
                if t >= 2:
                    pe.wait_ge(h_ready, t - 1)
                n = N_MIX + sum(BY_TILE[:t])
                for a in range(2):
                    for q in range(8):
                        lhs = attnT[:, q, t * P:(t + 1) * P] if q < 4 else convT[:, q - 4, t * P:(t + 1) * P]
                        wt = wo_att[:, q, :] if q < 4 else wo_conv[:, q - 4, :]
                        ins = pe.matmul(ps[:, a * 512:(a + 1) * 512], lhs, wt[:, a * 512:(a + 1) * 512],
                                        start=(q == 0), stop=(q == 7))
                        quarter = 2 * a + q // 4
                        if a == 1 and q == 7:
                            ins.then_inc(mix_banked, 1)
                        if q % 4 == 3 and quarter < BY_TILE[t]:
                            ada_total(n + quarter)

            def pool_out(t):
                ps = pair[t % 2]
                if t == 0:
                    pe.wait_ge(wpool_in, 16)
                    pe.wait_ge(pooled_ready, 4)
                if t >= 2:
                    pe.wait_ge(h_ready, 2 * T + t - 1)
                for g in range(4):
                    for q in range(2):
                        ins = pe.matmul(ps[:, g * 256:(g + 1) * 256], pooled[:, 2 * g + q, t * P:(t + 1) * P],
                                        wpool[:, 2 * g + q, :], start=(q == 0), stop=(q == 1))
                ins.then_inc(mix_banked, 1)

            def route(l):
                pe.wait_ge(logT_ready, l + 1)
                for t in range(T):
                    ins = pe.transpose(ps3[:, t * E:(t + 1) * E], logT[:, t * P:(t + 1) * P], ident[0:E, 0:E])
                ins.then_inc(logits_turned, 1)
                pe.wait_ge(sel_ready, l + 1)
                pe.wait_ge(cstb_ready, 1)
                for t in range(T + 1):
                    for q in range(min(t + 1, T)):
                        ins = pe.matmul(ps2[:, t * E:(t + 1) * E], cstb[:, 0:P] if q == t else cstb[:, P:2 * P],
                                        sel_tile[:, q * E:(q + 1) * E], start=(q == 0), stop=(q == min(t, T - 1)))
                ins.then_inc(pos_ready, 1)
                pe.wait_ge(row_copied, LAYERS * NCH)
                for g in range(EG):
                    pe.wait_ge(onehot_ready, l * EG + g + 1)
                    for e in range(EPG):
                        for t in range(T):
                            ins = pe.matmul((ps5 if g % 2 else ps4)[:, e * 6:(e + 1) * 6], onehot[:, g % 2, t, e, :],
                                            rtab[:, t, g * EPG + e, :], start=(t == 0), stop=(t == T - 1))
                    ins.then_inc(table_banked, 1)

            def expert_loop(l):
                def turn_in(e, j, i):
                    pe.wait_ge(xg_in[j % 4], 16 * (l * (E // 4) + i + 1))
                    if not isinstance(e, int) or l * E + e > 0:
                        pe.wait_ge(xT_act, l * E + e)
                        pe.wait_ge(xT_dve, l * E + e)
                    for k in range(KD):
                        ins = pe.transpose(psA[:, k * P:(k + 1) * P],
                                           xg[:, j % 4, :].rearrange("p (a k) -> p k a", k=KD)[:, k, :], ident)
                    ins.then_inc(xT_banked, 1)

                def first_product(e, j, i):
                    pe.wait_ge(xT_act, l * E + e + 1)
                    pe.wait_ge(xT_dve, l * E + e + 1)
                    pe.wait_ge(gu_in[j % 4], 32 * (l * (E // 4) + i + 1))
                    for k in range(KD):
                        ins = pe.matmul(gu_ps[j % 2][:, :].rearrange("p (a f) -> p a f", a=2), xgT[:, j % 2, k, :],
                                        w_gu(j % 4)[:, :, k, :], start=(k == 0), stop=(k == KD - 1))
                    ins.then_inc(gu_done, 1)

                def body(e, j, i):
                    static = isinstance(e, int)
                    if not static or e + 1 < E:
                        pe.wait_ge(hid_ready, HEAD + l * E + e)
                        first_product(e + 1, j + 1, i + (j + 1) // 4)
                    pe.wait_ge(hid_ready, HEAD + l * E + e + 1)
                    pe.wait_ge(hT_ready, HEAD + l * E + e)
                    for q in range(2):
                        ins = pe.transpose(ps2[:, q * P:(q + 1) * P],
                                           hid[:, j % 2, :].rearrange("p (a c) -> p c a", c=2)[:, q, :], ident)
                    ins.then_inc(hT_banked, 1)
                    if not static or e + 2 < E:
                        turn_in(e + 2, j + 2, i + (j + 2) // 4)
                    pe.wait_ge(hT_ready, HEAD + l * E + e + 1)
                    pe.wait_ge(y_ready, HEAD + l * E + e)
                    pe.wait_ge(dn_in[j], 16 * (l * (E // 4) + i + 1))
                    for a in range(2):
                        for q in range(2):
                            ins = pe.matmul(psY[:, a * 512:(a + 1) * 512], hT[:, q, :],
                                            w_dn(j)[:, q, a * 512:(a + 1) * 512], start=(q == 0), stop=(q == 1))
                    ins.then_inc(dn_done, 1)

                turn_in(0, 0, 0)
                turn_in(1, 1, 0)
                first_product(0, 0, 0)
                loop_experts(pe, body)

                pe.wait_ge(flag_ready, l + 1)
                most = pe.value_load(flag[0:1, l:l + 1], min_val=0, max_val=SEQ)
                with pe.If(most > P):
                    with pe.Fori(0, ROUNDS * E) as n:
                        pe.wait_ge(ov_oh[l], n + 1)
                        for t in range(T):
                            ins = pe.matmul(ps4[:, 0:6], onehot_ov[:, t, :], ovr[:, t, :],
                                            start=(t == 0), stop=(t == T - 1))
                        ins.then_inc(ov_tab[l], 1)
                        pe.wait_ge(ov_xg[l], 16 * n + 16)
                        for k in range(KD):
                            ins = pe.transpose(psA[:, k * P:(k + 1) * P],
                                               xg[:, 0, :].rearrange("p (a k) -> p k a", k=KD)[:, k, :], ident)
                        ins.then_inc(ov_xb[l], 1)
                        pe.wait_ge(ov_xT[l], n + 1)
                        pe.wait_ge(ov_w[l], 48 * n + 48)
                        for k in range(KD):
                            ins = pe.matmul(ps3[:, :].rearrange("p (a f) -> p a f", a=2), xgT[:, 0, k, :],
                                            w_gu(0)[:, :, k, :], start=(k == 0), stop=(k == KD - 1))
                        ins.then_inc(ov_gu[l], 1)
                        pe.wait_ge(ov_hid[l], n + 1)
                        for q in range(2):
                            ins = pe.transpose(ps2[:, q * P:(q + 1) * P],
                                               hid[:, 0, :].rearrange("p (a c) -> p c a", c=2)[:, q, :], ident)
                        ins.then_inc(ov_hb[l], 1)
                        pe.wait_ge(ov_hT[l], n + 1)
                        for a in range(2):
                            for q in range(2):
                                ins = pe.matmul(psY[:, a * 512:(a + 1) * 512], hT[:, q, :],
                                                w_dn(0)[:, q, a * 512:(a + 1) * 512], start=(q == 0), stop=(q == 1))
                        ins.then_inc(ov_dn[l], 1)

            for l in range(LAYERS):
                if l:
                    transposes(2)
                for t in range(T):
                    (pool_out if l else mix_out)(t)
                transposes(2 * l + 1)
                route(l)
                expert_loop(l)


_INS = ['x', 'c', 'w_ada', 'b_ada', 'norm_mix', 'norm_ffn', 'w_in', 'w_out', 'sinks', 'conv_w', 'w_pool', 'pool_scale',
        'w_router', 'b_router', 'w_gate', 'w_up', 'w_down', 'norm_final']


def _constants():
    import numpy as np
    a = np.zeros((P, C_END), np.float32)
    p = np.arange(P)
    a[:, C_ID:C_ID + P] = np.eye(P)
    a[:, C_BEF:C_BEF + P] = p[:, None] < p[None, :]
    dist = p[:, None] + P - np.arange(2 * P)[None, :]
    a[:, C_DIST:C_DIST + 2 * P] = np.where((dist >= 0) & (dist < P), dist, 1e30)
    a[:, C_SLOT:C_SLOT + P] = p[None, :]
    a[:, C_ONE:C_ONE + P] = 1.0
    a[:, C_INV:C_INV + 16] = np.float32(1.0) / np.arange(1, 17, dtype=np.float32)
    tok = np.zeros((P, T, 2), np.float32)
    tok[:, :, 0] = p[:, None]
    tok[:, :, 1] = P * np.arange(T)[None, :] - FAR
    a[:, C_TOK:C_TOK + 8] = tok.reshape(P, 8)
    j = np.arange(4)
    a[:, C_JLT:C_JLT + 16] = (j[None, :] < j[:, None]).reshape(1, 16)
    a[:, C_FST:C_FST + 4] = 4 - j
    return a


def kernel(**inputs):
    import numpy as _np
    import concourse.bacc as _bacc
    from concourse.bass_utils import run_bass_kernel_spmd as _run

    nc = _bacc.Bacc("TRN2", target_bir_lowering=False, num_devices=1)
    arrays, args = {}, []
    for name in _INS:
        a = _np.ascontiguousarray(inputs[name])
        arrays[f"in_{name}_dram"] = a
        args.append(nc.dram_tensor(f"in_{name}_dram", a.shape, mybir.dt.from_np(a.dtype), kind="ExternalInput").ap())
    arrays["constants"] = _constants()
    args.append(nc.dram_tensor("constants", (P, C_END), F32, kind="ExternalInput").ap())
    args.append(nc.dram_tensor("out_dram", (1, SEQ, D), F32, kind="ExternalOutput").ap())
    args.append(nc.dram_tensor("mod_dram", (LAYERS, MODW), F32, kind="Internal").ap())
    args.append([nc.dram_tensor(f"xhat_dram{l}", (SEQ, D), F32, kind="Internal").ap() for l in range(LAYERS)])
    args.append([nc.dram_tensor(f"y_dram{l}", (2 * SEQ, D), F32, kind="Internal").ap() for l in range(LAYERS)])
    trunk(nc, *args)
    return _run(nc, [arrays], core_ids=[0]).results[0]["out_dram"]
```

```python
from contextlib import ExitStack

import concourse.bass as bass
from concourse import mybir

F32 = mybir.dt.float32
BF16 = mybir.dt.bfloat16
I32 = mybir.dt.int32
U32 = mybir.dt.uint32
ALU = mybir.AluOpType
ACT = mybir.ActivationFunctionType
AX = mybir.AxisListType

P = 128
SEQ, D = 512, 1024
T = SEQ // P
KD = D // P
LAYERS = 2
EPS = 1e-6
MODW = 6 * D
AC = 384
NCH = MODW // AC
N_FIRST = 6
K_VEC = [KD - 2 if n < N_FIRST else KD for n in range(LAYERS * NCH)]
MACS = [sum(K_VEC[:n]) for n in range(LAYERS * NCH + 1)]
HD, HEADS, KVH = 64, 8, 2
GH = HEADS // KVH
AW = HEADS * HD
K0, V0, B0, C0, X0 = AW, AW + 128, AW + 256, AW + 256 + 512, AW + 256 + 1024
CC = 4
E, EG, EPG, FF = 16, 4, 4, 256
NSLOT = 4
FAR = 4096.0
HEAD_AT = [[kv * GH + 2 * (g % 2) + g // 2 for g in range(GH)] for kv in range(KVH)]
ATT_U = T * KVH
TABLE = [(0,), (1,), (2, 3)]
TABLES = len(TABLE)
TC = 5
HEAD = 1
ROUNDS = SEQ // P - 1

C_ID, C_BEF, C_DIST, C_SLOT, C_ONE, C_TOK, C_JLT, C_FST, C_END = (
    0, 128, 256, 512, 640, 768, 776, 792, 796)
POOL_MAX = 16
M_IN, M_BACK, M_FIRST, M_END = 0, P, P + POOL_MAX, 2 * P + POOL_MAX


def trunk(nc, x, c, w_ada, b_ada, norm_mix, norm_ffn, w_in, w_out, sinks, conv_w, w_pool, pool_scale,
          w_router, b_router, w_gate, w_up, w_down, norm_final, consts, pool_mats, out, mod_dram, xhat_dram, h_dram):
    ctx = ExitStack()
    with ctx:
        ctx.enter_context(nc.allow_non_contiguous_dma(reason="vectors of 1024 channels, 128k + p at partition p"))

        def sb(name, shape, dt=F32):
            return ctx.enter_context(nc.sbuf_tensor(name, shape, dt))

        def sem(name):
            return ctx.enter_context(nc.semaphore(name))

        h = sb("h", [P, T, D])
        xu = sb("xu", [P, 2 * T * D])
        xhat = xu[:, 0:T * D].rearrange("p (t d) -> p t d", t=T)
        uT = xu[:, T * D:2 * T * D].rearrange("p (k s) -> p k s", k=KD)
        cuT = xu[:, 0:CC * SEQ].rearrange("p (c s) -> p c s", c=CC)
        SLOT = 3 * KD * FF
        ring = sb("ring", [P, 3 * SLOT])
        WQKV, WC = KD * B0, KD * 512
        win_qkv = ring[:, 0:WQKV].rearrange("p (k n) -> p k n", k=KD)
        win_c, win_x, win_b = (ring[:, WQKV + i * WC:WQKV + (i + 1) * WC].rearrange("p (k n) -> p k n", k=KD)
                               for i in range(3))
        wo = ring[:, 0:KD * D].rearrange("p (c n) -> p c n", c=KD)
        WO_EARLY = WQKV // D

        def wslot(j):
            return ring[:, j * SLOT:(j + 1) * SLOT] if j < 3 else xu[:, 0:SLOT]

        def w_gu(j):
            return wslot(j)[:, 0:2 * KD * FF].rearrange("p (a k f) -> p a k f", a=2, k=KD)

        def w_dn(j):
            return wslot(j)[:, 2 * KD * FF:SLOT].rearrange("p (a d) -> p a d", a=2)

        adaw = sb("adaw", [P, 2, KD, AC])
        wpool = adaw[:, 0].rearrange("p k n -> p (k n)")[:, 0:KD * 256].rearrange("p (a n) -> p a n", a=KD)
        pmat = adaw[:, 1].rearrange("p k n -> p (k n)")[:, D:D + 4 * M_END].rearrange("p (g n) -> p g n", g=4)
        acc = sb("acc", [P, 4, AC])
        brow = sb("brow", [P, 2, AC])
        mrow = sb("mrow", [1, 2, AC])
        gbc = sb("gbc", [P, D])
        cst = sb("cst", [P, C_END])
        ident, before = cst[:, C_ID:C_ID + P], cst[:, C_BEF:C_BEF + P]
        ones = cst[:, C_ONE:C_ONE + P]

        WORK = 42 * 256
        work = sb("work", [P, WORK])
        at = [0]

        def take(n):
            at[0] += n
            assert at[0] <= WORK, at[0]
            return work[:, at[0] - n:at[0]]

        convT = take(CC * SEQ).rearrange("p (c s) -> p c s", c=CC)
        attnT = take(4 * SEQ).rearrange("p (c s) -> p c s", c=4)
        qT = take(4 * SEQ).rearrange("p (c s) -> p c s", c=4)
        kT = take(SEQ)
        kswap = take(SEQ)
        vtok = take(SEQ).rearrange("p (t n) -> p t n", t=T)
        prob = take(2 * GH * 256).rearrange("p (b h s) -> p b h s", b=2, h=GH)
        probT = take(2 * GH * P).rearrange("p (b n) -> p b n", b=2)
        at[0] = 0
        xg = take(4 * D).rearrange("p (b d) -> p b d", b=4)
        xgT = take(2 * D).rearrange("p (b k s) -> p b k s", b=2, k=KD)
        yrow = take(4 * D).rearrange("p (b d) -> p b d", b=4)[:, 0:2]
        at[0] -= 2 * D
        sil = take(2 * FF).rearrange("p (b f) -> p b f", b=2)
        hid = take(2 * FF).rearrange("p (b f) -> p b f", b=2)
        hT = take(2 * P).rearrange("p (a s) -> p a s", a=2)
        tok_i = take(E).bitcast(U32)
        gslot = take(E)
        posm = take(T * E).rearrange("p (t e) -> p t e", t=T)
        rtab = take(T * E * TC // 2).bitcast(BF16).rearrange("p (t e c) -> p t e c", t=T, e=E)
        tab = take(2 * EPG * TC)
        ovtab = take(8)
        ovtok = take(1).bitcast(U32)
        ovgate = take(1)
        ovr = take(T * TC // 2).bitcast(BF16).rearrange("p (t c) -> p t c", t=T)
        onehot_ov = yrow[:, 1, 0:T * P // 2].bitcast(BF16).rearrange("p (t s) -> p t s", t=T)
        onehot = yrow.rearrange("p b d -> p (b d)").bitcast(BF16).rearrange(
            "p (b t e s) -> p b t e s", b=2, t=T, e=EPG)
        small = xgT.rearrange("p b k s -> p (b k s)")
        pooled = uT
        psc = adaw[:, 1].rearrange("p k n -> p (k n)")[:, 0:D]
        gmix = [gbc[:, :], acc[:, :, :].rearrange("p a n -> p (a n)")[:, 0:D]]
        nfin = gmix[1]
        junk = work[:, 10 * D:10 * D + D // 2].bitcast(BF16)
        mixt = [at0.rearrange("p (b d) -> p b d", b=2) for at0 in (xu[:, 2 * D:4 * D], work[:, 8 * D:10 * D])]

        sel_tile = sb("sel_tile", [P, T * E], BF16)[:, :]
        cstb = sb("cstb", [P, 2 * P], BF16)
        sig_tile = sb("sig_tile", [P, T * E])[:, :]
        cond = sb("cond", [P, KD])
        craw = sb("craw", [P, KD])
        modc = sb("modc", [P, 4, 2, KD])
        normc = sb("normc", [P, 4, KD])
        scl = sb("scl", [P, 4, KD])
        wr = sb("wr", [P, KD, E])
        brb = sb("brb", [P, E])
        snk = sb("snk", [P, 2, HEADS])
        cvw = sb("cvw", [P, 3, CC])
        eps = sb("eps", [P, 1])
        idle = sb("idle", [P, 1])
        ss = sb("ss", [P, T])
        rstd = sb("rstd", [P, T])
        sm = sb("sm", [P, 2, 6, GH])
        flag = sb("flag", [P, LAYERS], I32)
        maxn = sb("maxn", [P, LAYERS])

        psA = ctx.enter_context(nc.psum_tensor("psA", [P, 1024], F32))
        ps2 = ctx.enter_context(nc.psum_tensor("ps2", [P, 512], F32))
        ps3 = ctx.enter_context(nc.psum_tensor("ps3", [P, 512], F32))
        ps4 = ctx.enter_context(nc.psum_tensor("ps4", [P, 512], F32))
        ps5 = ctx.enter_context(nc.psum_tensor("ps5", [P, 512], F32))
        psY = ctx.enter_context(nc.psum_tensor("psY", [P, 1024], F32))
        mix_ps = [[psY, psY, psA, psY], [psY, psA, psY, psA]]
        gu_ps = [ps3, ps4]
        tile_ps = [ps3, ps4]

        def first_bank(k):
            return (ps2[:, :], ps3[:, :], ps4[:, :], psA[:, 0:512], psA[:, 512:1024], psY[:, 0:512],
                    psY[:, 512:1024])[k % 7]


        const_in = sem("const_in")
        x_in = [sem(f"x_in{t}") for t in range(T)]
        c_in, small_in, psc_in = sem("c_in"), sem("small_in"), sem("psc_in")
        eps_ready, brow_clear = sem("eps_ready"), sem("brow_clear")
        ada_in = [sem(f"ada_in{b}{half}") for b in range(2) for half in "ab"]
        win_in = {part: sem(f"win_in_{part}") for part in ("q", "qkv", "c", "x", "b")}
        wout_in = [sem(f"wout_in{i}") for i in range(2)]
        wpool_in = sem("wpool_in")
        gu_in = [sem(f"gu_in{j}") for j in range(NSLOT)]
        dn_in = [sem(f"dn_in{j}") for j in range(NSLOT)]
        cond_ready = sem("cond_ready")
        mac_step = sem("mac_step")
        ada_mac = sem("ada_mac")
        ada_sum = sem("ada_sum")
        row_copied = sem("row_copied")
        mod_stored = [sem(f"mod_stored{b}") for b in range(2)]
        modc_in = [sem(f"modc_in{s}") for s in range(4)]
        gbc_in = sem("gbc_in")
        scl_ready = sem("scl_ready")
        std_done = [sem(f"std_done{s}") for s in range(5)]
        xhat_ready = [sem(f"xhat_ready{s}") for s in range(4)]
        xhat_stored = sem("xhat_stored")
        uT_banked = sem("uT_banked")
        tile_banked = [sem(f"tile_banked{s}") for s in range(4)]
        uT_act, uT_dve = sem("uT_act"), sem("uT_dve")
        h_ready = [sem(f"h_ready{l}") for l in range(LAYERS)]
        link_dve = sem("link_dve")
        link_act = sem("link_act")
        proj_ready = sem("proj_ready")
        kswap_in = sem("kswap_in")
        proj_act, proj_dve = sem("proj_act"), sem("proj_dve")
        scores_ready, scores_read = sem("scores_ready"), sem("scores_read")
        negmax_ready, exp_done = sem("negmax_ready"), sem("exp_done")
        rden_ready, prob_ready = sem("rden_ready"), sem("prob_ready")
        probT_banked, probT_ready = sem("probT_banked"), sem("probT_ready")
        att_banked, att_ready = sem("att_banked"), sem("att_ready")
        mix_banked = sem("mix_banked")
        pooled_ready = sem("pooled_ready")
        logits_ready, sig_ready = sem("logits_ready"), sem("sig_ready")
        cstb_ready = sem("cstb_ready")
        sel_ready, pos_ready = sem("sel_ready"), sem("pos_ready")
        onehot_ready = sem("onehot_ready")
        table_banked, table_ready = sem("table_banked"), sem("table_ready")
        flag_ready = sem("flag_ready")
        xg_clear = sem("xg_clear")
        xg_in = [sem(f"xg_in{j}") for j in range(4)]
        xT_banked, xT_act, xT_dve = sem("xT_banked"), sem("xT_act"), sem("xT_dve")
        gu_done, sil_ready, hid_ready = sem("gu_done"), sem("sil_ready"), sem("hid_ready")
        hT_banked, hT_ready = sem("hT_banked"), sem("hT_ready")
        dn_done, y_ready = sem("dn_done"), sem("y_ready")
        y_out = [sem(f"y_out{j}") for j in range(2)]
        h_stored = sem("h_stored")
        h_back = [sem(f"h_back{t}") for t in range(T)]
        nfin_in = sem("nfin_in")
        out_ready, out_stored = sem("out_ready"), sem("out_stored")
        ov_w = [sem(f"ov_w{l}") for l in range(LAYERS)]
        ov_oh = [sem(f"ov_oh{l}") for l in range(LAYERS)]
        ov_link = [sem(f"ov_link{l}") for l in range(LAYERS)]
        ov_tab = [sem(f"ov_tab{l}") for l in range(LAYERS)]
        ov_idx = [sem(f"ov_idx{l}") for l in range(LAYERS)]
        ov_xg = [sem(f"ov_xg{l}") for l in range(LAYERS)]
        ov_xb = [sem(f"ov_xb{l}") for l in range(LAYERS)]
        ov_xT = [sem(f"ov_xT{l}") for l in range(LAYERS)]
        ov_gu = [sem(f"ov_gu{l}") for l in range(LAYERS)]
        ov_sil = [sem(f"ov_sil{l}") for l in range(LAYERS)]
        ov_hid = [sem(f"ov_hid{l}") for l in range(LAYERS)]
        ov_hb = [sem(f"ov_hb{l}") for l in range(LAYERS)]
        ov_hT = [sem(f"ov_hT{l}") for l in range(LAYERS)]
        ov_dn = [sem(f"ov_dn{l}") for l in range(LAYERS)]
        ov_y = [sem(f"ov_y{l}") for l in range(LAYERS)]
        ov_out = [sem(f"ov_out{l}") for l in range(LAYERS)]
        ov_through = [sem(f"ov_through{l}") for l in range(LAYERS)]

        N_SMALL = 11

        PROJ = [("q", i) for i in range(4)] + [("k", 0), ("v", 0)] + [(n, i) for i in range(CC) for n in "cxb"]
        ACT_SIDE = {"q", "k", "v", "c"}
        act_before = [sum(n in ACT_SIDE for n, _ in PROJ[:m]) for m in range(len(PROJ) + 1)]
        BESIDE = [([6], [7]), ([8], [9]), ([10], [11]), ([12], [13]), ([14], [15]), ([16], [17])] + [([], [])] * 3
        LAG = 2
        BY_PROJ = [1, 1, 1, 1, 2, 2]
        BY_UNIT = [1, 1, 0, 1, 1, 1, 1, 1, 0, 1, 1, 1, 1, 1, 0, 1, 1, 1, 1, 1, 0, 1, 0, 0, 0, 0, 0]
        PLACES = BY_PROJ + BY_UNIT
        assert N_FIRST + sum(PLACES) == LAYERS * NCH

        def place_chunks(i):
            at = N_FIRST + sum(PLACES[:i])
            return range(at, at + PLACES[i])

        def place_totals(i):
            def summed(i):
                if i < 0:
                    return N_FIRST
                if i == len(PLACES) - 1:
                    return LAYERS * NCH
                return max(N_FIRST, place_chunks(i - 2).stop if i >= 2 else 0, place_chunks(i).stop - LAG)
            return range(summed(i - 1), summed(i))

        def unit_places(u, q, what):
            i = len(BY_PROJ) + 3 * u + q
            return what(i) if i < len(PLACES) else ()
        WO_AT = [18, 28]

        def mod_waits(eng, n):
            for q in (n, n - 1):
                eng.wait_ge(mod_stored[q % 2], 16 * (q // 2 + 1))

        def loop_experts(eng, body, first=0):
            for e in range(4 * first):
                body(e, e % 4, e // 4)
            with eng.Fori(first, E // 4 - 1) as i:
                for j in range(4):
                    body(4 * i + j, j, i)
            for j in range(4):
                body(E - 4 + j, j, E // 4 - 1)

        def turned_ps(e):
            return psY if isinstance(e, int) and e == 1 else psA

        block = ctx.enter_context(nc.Block())

        def overflow_sync(sp, l):
            sp.wait_ge(dn_done, HEAD + E * (l + 1))
            sp.wait_ge(flag_ready, l + 1)
            most = sp.value_load(flag[0:1, l:l + 1], min_val=0, max_val=SEQ)
            with sp.If(most > P):
                with sp.Fori(0, ROUNDS) as r:
                    with sp.Fori(0, E) as e:
                        n = r * E + e
                        gate = w_gate[l, bass.ds(e, 1)].rearrange("a (p k) f -> p (a k f)", k=KD)
                        up = w_up[l, bass.ds(e, 1)].rearrange("a (p k) f -> p (a k f)", k=KD)
                        down = w_down[l, bass.ds(e, 1)].rearrange("a (p c) d -> p (a c d)", c=2)
                        for s in (gate, up, down):
                            sp.lower_ap_dma(s)
                        sp.wait_ge(ov_dn[l], HEAD + n)
                        sp.dma_start(wslot(0)[:, 0:KD * FF], gate).then_inc(ov_w[l], 16)
                        sp.dma_start(wslot(0)[:, KD * FF:2 * KD * FF], up).then_inc(ov_w[l], 16)
                        sp.dma_start(wslot(0)[:, 2 * KD * FF:SLOT], down).then_inc(ov_w[l], 16)
                        sp.wait_ge(ov_out[l], 16 * n + 16)
                        sp.sem_inc(ov_through[l], 1)
                sp.wait_ge(ov_out[l], 16 * ROUNDS * E)

        @block.sync
        def _(sp):
            def load_ada(n):
                b, l, q = n % 2, n // NCH, n % NCH
                if n == 0:
                    sp.wait_ge(brow_clear, 1)
                for half in range(2):
                    ks = slice(half * KD // 2, (half + 1) * KD // 2)
                    if n >= 2:
                        sp.wait_ge(mac_step, MACS[n - 1] if half else MACS[n - 2] + KD // 2)
                        if half and K_VEC[n - 2] < KD:
                            sp.wait_ge(ada_sum, n - 1)
                    sp.dma_start(adaw[:, b, ks], w_ada[l, :, q * AC:(q + 1) * AC].rearrange("(p k) n -> p k n", k=KD)
                                 [:, ks]).then_inc(ada_in[2 * b + half], 16)
                    if half == 0:
                        sp.dma_start(brow[0:1, b, :], b_ada[l:l + 1, q * AC:(q + 1) * AC]).then_inc(ada_in[2 * b], 16)

            def load_expert(l, e, j):
                gate = w_gate[l, bass.ds(e, 1)].rearrange("a (p k) f -> p (a k f)", k=KD)
                up = w_up[l, bass.ds(e, 1)].rearrange("a (p k) f -> p (a k f)", k=KD)
                down = w_down[l, bass.ds(e, 1)].rearrange("a (p c) d -> p (a c d)", c=2)
                if not isinstance(e, int):
                    for s in (gate, up, down):
                        sp.lower_ap_dma(s)
                if isinstance(e, int) and l * E + e < NSLOT:
                    pass
                else:
                    sp.wait_ge(dn_done, HEAD + l * E + e - 3)
                flat = wslot(j)
                sp.dma_start(flat[:, 0:KD * FF], gate).then_inc(gu_in[j], 16)
                sp.dma_start(flat[:, KD * FF:2 * KD * FF], up).then_inc(gu_in[j], 16)
                sp.dma_start(flat[:, 2 * KD * FF:SLOT], down).then_inc(dn_in[j], 16)

            for q in ov_through:
                sp.sem_inc(q, HEAD)
            for t in range(T):
                sp.dma_start(h[:, t, :], x[0, t * P:(t + 1) * P, :]).then_inc(x_in[t], 16)
            for n in range(N_FIRST):
                load_ada(n)
            wsrc = w_in[0].rearrange("(p k) n -> p k n", k=KD)
            sp.dma_start(win_qkv[:, :, 0:2 * P], wsrc[:, :, 0:2 * P]).then_inc(win_in["q"], 16)
            sp.wait_ge(modc_in[0], 32)
            sp.dma_start(win_qkv[:, :, 2 * P:B0], wsrc[:, :, 2 * P:B0]).then_inc(win_in["qkv"], 16)
            wo_src = w_out[0].rearrange("(c p) n -> p c n", p=P)
            for n in range(N_FIRST, LAYERS * NCH):
                for name, place, dst, at0 in (("c", 3, win_c, C0), ("x", 4, win_x, X0), ("b", 5, win_b, B0)):
                    if n == N_FIRST + place:
                        sp.dma_start(dst, wsrc[:, :, at0:at0 + 512]).then_inc(win_in[name], 16)
                if n == WO_AT[0]:
                    sp.wait_ge(proj_ready, 6)
                    sp.dma_start(wo[:, 0:WO_EARLY], wo_src[:, 0:WO_EARLY]).then_inc(wout_in[0], 16)
                if n == WO_AT[1]:
                    sp.wait_ge(proj_ready, 16)
                    sp.dma_start(wo[:, WO_EARLY:], wo_src[:, WO_EARLY:]).then_inc(wout_in[1], 16)
                load_ada(n)
            sp.wait_ge(proj_ready, len(PROJ))
            load_expert(0, 2, 2)
            sp.wait_ge(ada_mac, LAYERS * NCH)
            sp.dma_start(wpool, w_pool[0].rearrange("g (c p) n -> p (g c) n", p=P)).then_inc(wpool_in, 16)
            sp.dma_start(pmat, pool_mats).then_inc(wpool_in, 16)
            sp.dma_start(psc, pool_scale.partition_broadcast(P).rearrange("p a d -> p (a d)")).then_inc(psc_in, 16)
            for l in range(LAYERS):
                for t in range(T):
                    sp.wait_ge(xhat_ready[2 * l + 1], t + 1)
                    sp.dma_start(h_dram[l][t * P:(t + 1) * P, :], h[:, t, :]).then_inc(h_stored, 16)
                    sp.dma_start(xhat_dram[l][t * P:(t + 1) * P, :], xhat[:, t, :]).then_inc(xhat_stored, 16)
                if l == 0:
                    sp.wait_ge(mix_banked, T)
                    for e in range(2):
                        load_expert(0, e, e)
                if l == 0:
                    sp.wait_ge(xg_in[3], 16)
                sp.wait_ge(xhat_stored, 16 * T * (l + 1))
                sp.wait_ge(logits_ready, T * (l + 1))
                load_expert(l, 3, 3)
                with sp.Fori(1, E // 4) as i:
                    for j in range(4):
                        load_expert(l, 4 * i + j, j)
                overflow_sync(sp, l)
                for j in range(2):
                    sp.wait_ge(y_out[j], 8 * E * (l + 1))
                for t in range(T):
                    sp.dma_start(h[:, t, :], h_dram[l][t * P:(t + 1) * P, :]).then_inc(h_back[t], 16)
                if l == 0:
                    for e in range(3):
                        load_expert(1, e, e)
            for t in range(T):
                sp.wait_ge(out_ready, t + 1)
                sp.dma_start(out[0, t * P:(t + 1) * P, :], xhat[:, t, :]).then_inc(out_stored, 16)
            sp.wait_ge(out_stored, 16 * T)

        @block.gpsimd
        def _(pool):
            def load_cols(s, last_chunk):
                l, half = s // 2, s % 2
                mod_waits(pool, l * NCH + last_chunk)
                off = 3 * half * D
                for a in range(s == 2, 2):
                    src = mod_dram[l, off + a * D:off + (a + 1) * D]
                    src = src.rearrange("(k p) -> p k", p=P) if s == 2 else src.rearrange("(p k) -> p k", k=KD)
                    pool.dma_start(modc[:, s, a, :], src).then_inc(modc_in[s], 16)

            def load_gate(l, half):
                off = (3 * half + 2) * D
                mod_waits(pool, l * NCH + ((off + D - 1) // AC))
                pool.dma_start(gbc[:, :] if half else gmix[l], mod_dram[l:l + 1, off:off + D].partition_broadcast(P)
                               .rearrange("p a d -> p (a d)")).then_inc(gbc_in, 16)

            load_cols(0, N_FIRST - 1)
            load_gate(0, 0)
            for u in range(ATT_U):
                b = u // KVH
                pool.wait_ge(rden_ready, u + 1)
                lo = 0 if b else P
                part = prob[:, u % 2, :, lo:]
                pool.tensor_tensor(part, part, sm[:, u % 2, 4, :].unsqueeze(2).broadcast_to([P, GH, 256 - lo]),
                                   ALU.mult).then_inc(prob_ready, 1)
            for l in range(LAYERS):
                if l == 0:
                    load_cols(1, (5 * D - 1) // AC)
                pool.wait_ge(h_ready[l], T)
                load_gate(l, 1)
                if l:
                    pool.dma_start(nfin, norm_final.rearrange("(a d) -> a d", a=1).partition_broadcast(P)
                                   .rearrange("p a d -> p (a d)")).then_inc(nfin_in, 16)
                if l == 0:
                    load_cols(2, N_FIRST - 1)
                    load_cols(3, (5 * D - 1) // AC)
                    mod_waits(pool, LAYERS * NCH - 1)
                    load_gate(1, 0)
                pool.memset(xg[:, :, :], 0.0).then_inc(xg_clear, 1)
                pool.wait_ge(xg_clear, l + 1)
                pool.wait_ge(xhat_stored, 16 * T * (l + 1))

                def scatter(e):
                    pool.wait_ge(y_ready, HEAD + l * E + e + 1)
                    if e:
                        pool.wait_ge(y_out[(e - 1) % 2], 16 * (l * E // 2 + (e - 1) // 2 + 1))
                    else:
                        pool.wait_ge(h_stored, 16 * T * (l + 1))
                    pool.indirect_dma_start(
                        out=h_dram[l], out_offset=bass.IndirectOffsetOnAxis(tok_i[:, e:e + 1], 0),
                        in_=yrow[:, e % 2, :], in_offset=None, bounds_check=SEQ - 1, oob_is_err=False,
                        compute_op=ALU.add).then_inc(y_out[e % 2], 16)

                for e in range(E):
                    if e % EPG == 0 and e // EPG < TABLES:
                        pool.wait_ge(table_ready, l * TABLES + e // EPG + 1)
                    if e >= 4:
                        pool.wait_ge(xT_banked, l * E + e - 3)
                    pool.indirect_dma_start(
                        out=xg[:, e % 4, :], out_offset=None, in_=xhat_dram[l],
                        in_offset=bass.IndirectOffsetOnAxis(tok_i[:, e:e + 1], 0),
                        bounds_check=SEQ - 1, oob_is_err=False).then_inc(xg_in[e % 4], 16)
                    if e >= 3:
                        scatter(e - 3)
                for e in range(E - 3, E):
                    scatter(e)
                for j in range(2):
                    pool.wait_ge(y_out[j], 8 * E * (l + 1))

                pool.wait_ge(flag_ready, l + 1)
                most = pool.value_load(flag[0:1, l:l + 1], min_val=0, max_val=SEQ)
                bound, zero = pool.alloc_register(f"bound{l}"), pool.to_reg(0)
                with pool.If(most > P):
                    with pool.Fori(0, ROUNDS * E) as n:
                        pool.wait_ge(ov_idx[l], n + 1)
                        pool.reg_add(bound, zero, SEQ - 1)
                        pool.indirect_dma_start(
                            out=xg[:, 0, :], out_offset=None, in_=xhat_dram[l],
                            in_offset=bass.IndirectOffsetOnAxis(ovtok[:, 0:1], 0),
                            bounds_check=bound, oob_is_err=False).then_inc(ov_xg[l], 16)
                        pool.wait_ge(ov_y[l], n + 1)
                        pool.reg_add(bound, zero, SEQ - 1)
                        pool.indirect_dma_start(
                            out=h_dram[l], out_offset=bass.IndirectOffsetOnAxis(ovtok[:, 0:1], 0),
                            in_=yrow[:, 0, :], in_offset=None, bounds_check=bound, oob_is_err=False,
                            compute_op=ALU.add).then_inc(ov_out[l], 16)

        @block.scalar
        def _(act):
            alink = [0]

            def link(ins):
                alink[0] += 1
                ins.then_inc(link_act, 1)
                act.wait_ge(link_act, alink[0])

            act.sem_inc(hT_ready, HEAD)
            act.dma_start(craw[:, :], c[0].rearrange("(p k) -> p k", k=KD)).then_inc(c_in, 16)
            act.dma_start(cst[:, :], consts).then_inc(const_in, 16)
            act.wait_ge(c_in, 16)
            act.activation(cond[:, :], craw[:, :], ACT.Silu).then_inc(cond_ready, 1)
            for s in range(4):
                src = (norm_ffn if s % 2 else norm_mix)[s // 2]
                src = src.rearrange("(k p) -> p k", p=P) if s == 2 else src.rearrange("(p k) -> p k", k=KD)
                act.dma_start(normc[:, s, :], src).then_inc(small_in, 16)
            act.dma_start(wr[:, :, :], w_router.rearrange("(p k) e -> p k e", k=KD)).then_inc(small_in, 16)
            act.dma_start(brb[:, :], b_router.rearrange("(a e) -> a e", a=1).partition_broadcast(P)
                          .rearrange("p a e -> p (a e)")).then_inc(small_in, 16)
            for kv in range(KVH):
                for odd in range(2):
                    src = sinks[:, kv * GH + odd:(kv + 1) * GH:2].partition_broadcast(P).rearrange("p a e -> p (a e)")
                    act.dma_start(snk[:, 0, kv * GH + 2 * odd:kv * GH + 2 * odd + 2], src).then_inc(small_in, 16)
            act.dma_start(cvw[:, :, :], conv_w[0].rearrange("j (c p) -> p j c", p=P)).then_inc(small_in, 16)

            def ada_out(n):
                b, l, q = n % 2, n // NCH, n % NCH
                act.wait_ge(ada_sum, n + 1)
                if n >= 2:
                    act.wait_ge(mod_stored[b], 16 * (n // 2))
                act.activation(mrow[0:1, b, :], ps5[0:1, 0:AC], ACT.Copy).then_inc(row_copied, 1)
                act.wait_ge(row_copied, n + 1)
                act.dma_start(mod_dram[l:l + 1, q * AC:(q + 1) * AC], mrow[0:1, b, :]).then_inc(mod_stored[b], 16)

            def root_ahead():
                act.activation(idle[:, 0:1], eps[:, 0:1], ACT.Sqrt)

            def norm(s, t):
                if s == 0:
                    if t == 0:
                        act.wait_ge(eps_ready, 1)
                        root_ahead()
                    act.wait_ge(x_in[t], 16)
                elif s % 2:
                    act.wait_ge(h_ready[s // 2], t + 1)
                else:
                    act.wait_ge(h_back[t], 16 * (s // 2))
                link(act.activation(junk, h[:, t, :], ACT.Square, accum_out=ss[:, t:t + 1]))
                act.activation(rstd[:, t:t + 1], ss[:, t:t + 1], ACT.Sqrt, bias=eps[:, 0:1], scale=1.0 / D
                               ).then_inc(std_done[s], 1)

            def spread_all():
                for k in range(0, KD, 2):
                    if k == 0:
                        act.wait_ge(scl_ready, 1)
                    act.wait_ge(uT_banked, k + 1)
                    act.activation(uT[:, k, :], first_bank(k), ACT.Identity, scale=scl[:, 0, k:k + 1],
                                   bias=modc[:, 0, 0, k:k + 1]).then_inc(uT_act, 1)

            def spread(s, t):
                if t == 0:
                    act.wait_ge(scl_ready, s + 1)
                for half in range(2 if s == 2 else 1):
                    act.wait_ge(tile_banked[s], 2 * t + half + 1)
                    for q in range(KD // 2):
                        k = half * KD // 2 + q
                        src = tile_ps[half][:, q * P:(q + 1) * P]
                        if s == 2:
                            ins = act.activation(pooled[:, k, t * P:(t + 1) * P], src, ACT.Identity,
                                                 scale=scl[:, 2, k:k + 1])
                        else:
                            ins = act.activation(uT[:, k, t * P:(t + 1) * P], src, ACT.Identity,
                                                 scale=scl[:, s, k:k + 1], bias=modc[:, s, 0, k:k + 1])
                ins.then_inc(pooled_ready if s == 2 else uT_act, 1)

            for t in range(T):
                norm(0, t)
            for n in range(N_FIRST):
                ada_out(n)
            spread_all()

            def empty(m):
                name, i = PROJ[m]
                if name not in ACT_SIDE:
                    return
                act.wait_ge(proj_ready, m + 1)
                bank = psY[:, (m % 2) * 512:(m % 2 + 1) * 512]
                if name == "q":
                    dst = qT[:, i, :]
                elif name == "k":
                    dst = kT
                elif name == "v":
                    dst = vtok.rearrange("p t n -> p (t n)")
                else:
                    dst = cuT[:, i, :]
                act.activation(dst, bank, ACT.Copy).then_inc(proj_act, 1)
                if name == "k":
                    act.wait_ge(proj_act, act_before[m + 1])
                    act.dma_start(kswap[HD:P], kT[0:HD]).then_inc(kswap_in, 16)
                    act.dma_start(kswap[0:HD], kT[HD:P]).then_inc(kswap_in, 16)

            def exps(u):
                b, pb = u // KVH, u % 2
                act.wait_ge(negmax_ready, u + 1)
                lo = 0 if b else P
                for g in range(GH):
                    act.activation(prob[:, pb, g, lo:], prob[:, pb, g, lo:], ACT.Exp, scale=HD ** -0.5,
                                   bias=sm[:, pb, 1, g:g + 1], accum_out=sm[:, pb, 2, g:g + 1])
                act.activation(sm[:, pb, 3, :], sm[:, pb, 5, :], ACT.Exp).then_inc(exp_done, 1)

            def empty_probT(u):
                b = u // KVH
                act.wait_ge(probT_banked, u + 1)
                if u:
                    act.wait_ge(att_banked, u)
                if b:
                    act.activation(probT[:, 0, :], ps2[:, :], ACT.Copy)
                act.activation(probT[:, 1, :], ps3[:, :], ACT.Copy).then_inc(probT_ready, 1)

            def empty_att(b):
                act.wait_ge(att_banked, KVH * (b + 1))
                act.activation(attnT[:, :, b * P:(b + 1) * P], ps4[:, :].rearrange("p (c s) -> p c s", c=4),
                               ACT.Copy).then_inc(att_ready, 1)

            for m in range(6):
                empty(m)
                for n in place_totals(m):
                    ada_out(n)
            for u in range(ATT_U + 1):
                if u:
                    empty_probT(u - 1)
                if u < ATT_U:
                    exps(u)
                for n in unit_places(u, 0, place_totals):
                    ada_out(n)
                for m in BESIDE[u][0]:
                    empty(m)
                if u and u % KVH == 0:
                    empty_att(u // KVH - 1)
                for n in unit_places(u, 1, place_totals):
                    ada_out(n)
                for m in BESIDE[u][1]:
                    empty(m)
                for n in unit_places(u, 2, place_totals):
                    ada_out(n)

            def expert_loop(l):
                def xT_half(e, j, i):
                    act.wait_ge(xT_banked, l * E + e + 1)
                    for k in range(KD // 2):
                        ins = act.activation(xgT[:, j % 2, k, :], turned_ps(e)[:, k * P:(k + 1) * P], ACT.Identity,
                                             scale=scl[:, 2 * l + 1, k:k + 1], bias=modc[:, 2 * l + 1, 0, k:k + 1])
                    ins.then_inc(xT_act, 1)

                def silu(e, j, i):
                    act.wait_ge(gu_done, l * E + e + 1)
                    act.activation(sil[:, j % 2, :], gu_ps[j % 2][:, 0:FF], ACT.Silu).then_inc(sil_ready, 1)

                def body(e, j, i):
                    static = isinstance(e, int)
                    if not static or e + 1 < E:
                        act.wait_ge(hid_ready, HEAD + l * E + e)
                        silu(e + 1, j + 1, i)
                    act.wait_ge(hT_banked, HEAD + l * E + e + 1)
                    act.wait_ge(dn_done, HEAD + l * E + e)
                    act.activation(hT.rearrange("p a s -> p (a s)"), ps2[:, 0:2 * P], ACT.Copy).then_inc(hT_ready, 1)
                    if not static or e + 2 < E:
                        act.wait_ge(gu_done, l * E + e + 1)
                        xT_half(e + 2, j, i)

                act.wait_ge(onehot_ready, EG * l + 1)
                xT_half(0, 0, 0)
                xT_half(1, 1, 0)
                silu(0, 0, 0)
                loop_experts(act, body)

                act.wait_ge(flag_ready, l + 1)
                most = act.value_load(flag[0:1, l:l + 1], min_val=0, max_val=SEQ)
                with act.If(most > P):
                    with act.Fori(0, ROUNDS * E) as n:
                        act.wait_ge(ov_xb[l], n + 1)
                        for k in range(KD):
                            ins = act.activation(xgT[:, 0, k, :], psA[:, k * P:(k + 1) * P], ACT.Identity,
                                                 scale=scl[:, 2 * l + 1, k:k + 1],
                                                 bias=modc[:, 2 * l + 1, 0, k:k + 1])
                        ins.then_inc(ov_xT[l], 1)
                        act.wait_ge(ov_gu[l], n + 1)
                        act.activation(sil[:, 0, :], ps3[:, 0:FF], ACT.Silu).then_inc(ov_sil[l], 1)
                        act.wait_ge(ov_hb[l], n + 1)
                        act.activation(hT.rearrange("p a s -> p (a s)"), ps2[:, 0:2 * P], ACT.Copy
                                       ).then_inc(ov_hT[l], 1)

            for l in range(LAYERS):
                if l == 0:
                    for t in range(2):
                        norm(1, t)
                    spread(1, 0)
                    norm(1, 2)
                    spread(1, 1)
                    spread(1, 2)
                    norm(1, 3)
                    spread(1, 3)
                else:
                    root_ahead()
                    norm(2, 0)
                    for t in range(1, T):
                        norm(2, t)
                        spread(2, t - 1)
                    norm(3, 0)
                    spread(2, T - 1)
                    norm(3, 1)
                    for t in range(2, T):
                        spread(3, t - 2)
                        norm(3, t)
                    for t in range(T - 2, T):
                        spread(3, t)
                act.wait_ge(logits_ready, T * (l + 1))
                act.activation(sig_tile, ps2[:, 0:T * E], ACT.Sigmoid).then_inc(sig_ready, 1)
                expert_loop(l)
            root_ahead()
            for t in range(T):
                norm(4, t)

        @block.vector
        def _(dve):
            dlink = [0]

            def link(ins):
                dlink[0] += 1
                ins.then_inc(link_dve, 1)
                dve.wait_ge(link_dve, dlink[0])

            def ada_mul(n):
                b = n % 2
                if n >= 3:
                    dve.wait_ge(ada_sum, n - 2)
                for k in range(K_VEC[n]):
                    if k == 0:
                        dve.wait_ge(ada_in[2 * b], 32 * (n // 2 + 1))
                    if k == 1 and n:
                        dve.wait_ge(ada_mac, n)
                    if k == KD // 2:
                        dve.wait_ge(ada_in[2 * b + 1], 16 * (n // 2 + 1))
                    part = acc[:, 3 if k % 2 else n % 3, :]
                    if k < 2:
                        if k == 0:
                            ins = dve.scalar_tensor_tensor(part, adaw[:, b, k, :], cond[:, k:k + 1], brow[:, b, :],
                                                           ALU.mult, ALU.add)
                        else:
                            ins = dve.tensor_scalar(part, adaw[:, b, k, :], cond[:, k:k + 1], None, ALU.mult)
                    else:
                        dve.wait_ge(mac_step, MACS[n] + k - 1)
                        ins = dve.scalar_tensor_tensor(part, adaw[:, b, k, :], cond[:, k:k + 1], part,
                                                       ALU.mult, ALU.add)
                    ins.then_inc(mac_step, 1)
                dve.wait_ge(mac_step, MACS[n + 1])
                dve.tensor_tensor(acc[:, n % 3, :], acc[:, n % 3, :], acc[:, 3, :], ALU.add).then_inc(ada_mac, 1)

            def norm(s, t):
                dve.wait_ge(std_done[s], t + 1)
                link(dve.reciprocal(rstd[:, t:t + 1], rstd[:, t:t + 1]))
                dve.tensor_scalar(xhat[:, t, :], h[:, t, :], rstd[:, t:t + 1], None, ALU.mult
                                  ).then_inc(xhat_ready[s], 1)

            def scales(s):
                dve.wait_ge(modc_in[s], 16 if s == 2 else 32)
                dve.scalar_tensor_tensor(scl[:, s, :], modc[:, s, 1, :], 1.0, normc[:, s, :], ALU.add, ALU.mult
                                         ).then_inc(scl_ready, 1)
                dve.wait_ge(scl_ready, s + 1)

            def spread_all():
                for k in range(1, KD, 2):
                    dve.wait_ge(uT_banked, k + 1)
                    dve.tensor_scalar(uT[:, k, :], first_bank(k), scl[:, 0, k:k + 1], modc[:, 0, 0, k:k + 1],
                                      ALU.mult, ALU.add).then_inc(uT_dve, 1)

            def spread(s, t):
                dve.wait_ge(tile_banked[s], 2 * t + 2)
                for q in range(KD // 2):
                    k = KD // 2 + q
                    ins = dve.tensor_scalar(uT[:, k, t * P:(t + 1) * P], tile_ps[1][:, q * P:(q + 1) * P],
                                            scl[:, s, k:k + 1], modc[:, s, 0, k:k + 1], ALU.mult, ALU.add)
                ins.then_inc(uT_dve, 1)

            def mix_in(l, t):
                dve.wait_ge(mix_banked, l * T + t + 1)
                link(dve.tensor_tensor(mixt[l][:, t % 2, :], mix_ps[l][t][:, :], gmix[l], ALU.mult))
                dve.tensor_tensor(h[:, t, :], h[:, t, :], mixt[l][:, t % 2, :], ALU.add
                                  ).then_inc(h_ready[l], 1)

            for q in (hid_ready, y_ready, *ov_link):
                dve.sem_inc(q, HEAD)
            dve.memset(eps[:, :], EPS).then_inc(eps_ready, 1)
            dve.memset(brow[:, :, :], 0.0).then_inc(brow_clear, 1)
            dve.wait_ge(cond_ready, 1)
            dve.wait_ge(const_in, 16)
            dve.tensor_copy(cstb[:, 0:P], before)
            dve.tensor_copy(cstb[:, P:2 * P], ones).then_inc(cstb_ready, 1)
            for t in range(T):
                norm(0, t)
            for n in range(N_FIRST):
                ada_mul(n)
            dve.wait_ge(small_in, 16 * N_SMALL)
            scales(0)
            spread_all()
            link(dve.tensor_scalar(snk[:, 1, :], snk[:, 0, :], HD ** 0.5, None, ALU.mult))

            def empty(m):
                name, i = PROJ[m]
                if name in ACT_SIDE:
                    return
                dve.wait_ge(proj_ready, m + 1)
                bank = psY[:, (m % 2) * 512:(m % 2 + 1) * 512]
                if name == "x":
                    dve.wait_ge(proj_act, act_before[m])
                    ins = dve.tensor_tensor(cuT[:, i, :], cuT[:, i, :], bank, ALU.mult)
                    ins.then_inc(proj_dve, 1)
                    dve.wait_ge(proj_dve, m - act_before[m] + 1)
                    link(dve.tensor_scalar(convT[:, i, :], cuT[:, i, :], cvw[:, 2, i:i + 1], None, ALU.mult))
                    for back in (1, 2):
                        link(dve.scalar_tensor_tensor(convT[:, i, back:], cuT[:, i, 0:SEQ - back],
                                                      cvw[:, 2 - back, i:i + 1], convT[:, i, back:],
                                                      ALU.mult, ALU.add))
                else:
                    dve.tensor_tensor(convT[:, i, :], convT[:, i, :], bank, ALU.mult).then_inc(proj_dve, 1)

            def soften(u):
                b, kv, pb = u // KVH, u % KVH, u % 2
                lo = 0 if b else P
                dve.wait_ge(scores_ready, u + 1)
                if u >= 2:
                    dve.wait_ge(probT_banked, u - 1)
                for g in range(GH):
                    slope = 2.0 ** (-8.0 * (HEAD_AT[kv][g] + 1) / HEADS)
                    ins = dve.scalar_tensor_tensor(prob[:, pb, g, lo:], cst[:, C_DIST + lo:C_DIST + 256],
                                                   -slope * HD ** 0.5, psA[:, g * 256 + lo:(g + 1) * 256],
                                                   ALU.mult, ALU.add)
                ins.then_inc(scores_read, 1)
                dve.wait_ge(scores_read, u + 1)
                link(dve.tensor_reduce(sm[:, pb, 0, :], prob[:, pb, :, lo:], AX.X, ALU.max))
                link(dve.tensor_tensor(sm[:, pb, 0, :], sm[:, pb, 0, :], snk[:, 1, kv * GH:(kv + 1) * GH], ALU.max))
                link(dve.tensor_scalar(sm[:, pb, 1, :], sm[:, pb, 0, :], -(HD ** -0.5), None, ALU.mult))
                dve.tensor_tensor(sm[:, pb, 5, :], sm[:, pb, 1, :], snk[:, 0, kv * GH:(kv + 1) * GH], ALU.add
                                  ).then_inc(negmax_ready, 1)

            def divide(u):
                pb = u % 2
                dve.wait_ge(exp_done, u + 1)
                link(dve.tensor_tensor(sm[:, pb, 2, :], sm[:, pb, 2, :], sm[:, pb, 3, :], ALU.add))
                dve.reciprocal(sm[:, pb, 4, :], sm[:, pb, 2, :]).then_inc(rden_ready, 1)

            for m in range(6):
                for n in place_chunks(m):
                    ada_mul(n)
            for u in range(ATT_U):
                if u == ATT_U - 1:
                    dve.wait_ge(gbc_in, 16)
                    mix_in(0, 0)
                soften(u)
                for n in unit_places(u, 0, place_chunks):
                    ada_mul(n)
                divide(u)
                for m in BESIDE[u][0]:
                    empty(m)
                for n in unit_places(u, 1, place_chunks):
                    ada_mul(n)
                for m in BESIDE[u][1]:
                    empty(m)
                for n in unit_places(u, 2, place_chunks):
                    ada_mul(n)
            mix_in(0, 1)
            norm(1, 0)
            norm(1, 1)
            scales(1)
            mix_in(0, 2)
            spread(1, 0)
            norm(1, 2)
            spread(1, 1)
            spread(1, 2)
            mix_in(0, 3)
            norm(1, 3)
            spread(1, 3)

            def tiny(n, at0):
                return small[:, at0:at0 + n]

            bia = tiny(64, 64)
            prs = tiny(96, 128)
            gs = tiny(16, 224)
            gm = tiny(4, 240)
            ing = tiny(16, 244)
            vmx = tiny(4, 260)
            gtt = tiny(256, 264)
            eqt = tiny(256, 520)
            rank = tiny(64, 776)
            sel = sel_tile
            ws = tiny(64, 904)
            wsum = tiny(4, 968)
            gate = tiny(64, 972)
            rest = tiny(64, 1036)

            def route(l):
                dve.wait_ge(sig_ready, l + 1)
                b3 = bia.rearrange("p (g i) -> p g i", i=EPG)
                pr = prs.rearrange("p (g c) -> p g c", c=6)
                link(dve.tensor_tensor(bia.rearrange("p (t e) -> p t e", t=T),
                                       sig_tile.rearrange("p (t e) -> p t e", t=T),
                                       brb[:, :].unsqueeze(1).broadcast_to([P, T, E]), ALU.add))
                b4 = bia.rearrange("p (g a i) -> p g a i", a=2, i=2)
                dve.tensor_tensor(pr[:, :, 0:2], b4[:, :, :, 0], b4[:, :, :, 1], ALU.add)
                dve.tensor_tensor(pr[:, :, 2:4], b3[:, :, 0:2], b3[:, :, 2:4], ALU.add)
                dve.tensor_tensor(pr[:, :, 4:5], b3[:, :, 0:1], b3[:, :, 3:4], ALU.add)
                link(dve.tensor_tensor(pr[:, :, 5:6], b3[:, :, 1:2], b3[:, :, 2:3], ALU.add))
                link(dve.tensor_reduce(gs, pr, AX.X, ALU.max))
                g3 = gs.rearrange("p (t g) -> p t g", t=T)
                v3 = ing.rearrange("p (t g) -> p t g", t=T)
                link(dve.tensor_reduce(gm, g3, AX.X, ALU.max))
                link(dve.tensor_tensor(v3, g3, gm.unsqueeze(2).broadcast_to([P, T, EG]), ALU.is_equal))
                link(dve.tensor_tensor(v3, v3, cst[:, C_FST:C_FST + EG].unsqueeze(1).broadcast_to([P, T, EG]),
                                       ALU.mult))
                link(dve.tensor_reduce(vmx, v3, AX.X, ALU.max))
                link(dve.tensor_tensor(v3, v3, vmx.unsqueeze(2).broadcast_to([P, T, EG]), ALU.is_equal))
                bj = b3.unsqueeze(2).broadcast_to([P, E, EPG, EPG])
                bi = b3.unsqueeze(3).broadcast_to([P, E, EPG, EPG])
                gt4 = gtt.rearrange("p (g i j) -> p g i j", i=EPG, j=EPG)
                eq4 = eqt.rearrange("p (g i j) -> p g i j", i=EPG, j=EPG)
                dve.tensor_tensor(gt4, bj, bi, ALU.is_gt)
                link(dve.tensor_tensor(eq4, bj, bi, ALU.is_equal))
                link(dve.tensor_tensor(eqt.rearrange("p (g q) -> p g q", q=16), eqt.rearrange("p (g q) -> p g q", q=16),
                                       cst[:, C_JLT:C_JLT + 16].unsqueeze(1).broadcast_to([P, E, 16]), ALU.mult))
                link(dve.tensor_tensor(gtt, gtt, eqt, ALU.add))
                link(dve.tensor_reduce(rank, gtt.rearrange("p (g j) -> p g j", j=EPG), AX.X, ALU.add))
                dve.scalar_tensor_tensor(sel.rearrange("p (g i) -> p g i", i=EPG),
                                         rank.rearrange("p (g i) -> p g i", i=EPG),
                                         2.0, ing.unsqueeze(2).broadcast_to([P, E, EPG]), ALU.is_lt, ALU.mult
                                         ).then_inc(sel_ready, 1)
                dve.wait_ge(sel_ready, l + 1)
                link(dve.tensor_tensor(ws, sig_tile, sel, ALU.mult))
                ws3 = ws.rearrange("p (t e) -> p t e", t=T)
                link(dve.tensor_reduce(wsum, ws3, AX.X, ALU.add))
                link(dve.reciprocal(wsum, wsum))
                gt3 = gate.rearrange("p (t e) -> p t e", t=T)
                rs3 = rest.rearrange("p (t e) -> p t e", t=T)
                link(dve.tensor_tensor(gt3, ws3, wsum.unsqueeze(2).broadcast_to([P, T, E]), ALU.mult))
                tokc = cst[:, C_TOK:C_TOK + 8].rearrange("p (t c) -> p t c", t=T)
                dve.tensor_copy(rtab[:, :, :, 0:2], tokc.unsqueeze(2).broadcast_to([P, T, E, 2]))
                link(dve.tensor_copy(rtab[:, :, :, 2], gt3))
                link(dve.tensor_tensor(rs3, gt3, rtab[:, :, :, 2], ALU.subtract))
                link(dve.tensor_copy(rtab[:, :, :, 3], rs3))
                link(dve.tensor_tensor(rs3, rs3, rtab[:, :, :, 3], ALU.subtract))
                link(dve.tensor_copy(rtab[:, :, :, 4], rs3))
                dve.wait_ge(pos_ready, l + 1)
                sel3 = sel.rearrange("p (t e) -> p t e", t=T)
                pos3 = ps2[:, 0:T * E].rearrange("p (t e) -> p t e", t=T)
                dve.tensor_reduce(maxn[:, l:l + 1], ps2[:, T * E:T * E + E], AX.X, ALU.max)
                link(dve.scalar_tensor_tensor(posm, pos3, 1.0, sel3, ALU.add, ALU.mult))
                dve.tensor_copy(flag[:, l:l + 1], maxn[:, l:l + 1]).then_inc(flag_ready, 1)
                link(dve.tensor_scalar(posm, posm, -1.0, None, ALU.add))
                def one_hots(g):
                    if g >= 2:
                        dve.wait_ge(table_banked, l * TABLES + g - 1)
                    dve.tensor_tensor(
                        onehot[:, g % 2], cst[:, C_SLOT:C_SLOT + P].unsqueeze(1).unsqueeze(1).broadcast_to(
                            [P, T, EPG, P]),
                        posm[:, :, g * EPG:(g + 1) * EPG].unsqueeze(3).broadcast_to([P, T, EPG, P]),
                        ALU.is_equal).then_inc(onehot_ready, 1)

                def table(i):
                    n = len(TABLE[i]) * EPG
                    cols = slice(TABLE[i][0] * EPG, TABLE[i][0] * EPG + n)
                    t3 = tab[:, 0:n * TC].rearrange("p (e c) -> p e c", c=TC)
                    dve.wait_ge(table_banked, l * TABLES + i + 1)
                    link(dve.tensor_copy(tab[:, 0:n * TC], (ps4 if i == 1 else ps5)[:, 0:n * TC]))
                    dve.scalar_tensor_tensor(tok_i[:, cols], t3[:, :, 0], FAR, t3[:, :, 1], ALU.add, ALU.add)
                    link(dve.tensor_tensor(gslot[:, cols], t3[:, :, 2], t3[:, :, 3], ALU.add))
                    dve.tensor_tensor(gslot[:, cols], gslot[:, cols], t3[:, :, 4], ALU.add).then_inc(table_ready, 1)
                    dve.wait_ge(table_ready, l * TABLES + i + 1)

                one_hots(0)
                table(0)
                one_hots(1)
                table(1)
                return one_hots, table

            def expert_loop(l, one_hots, table):
                def xT_half(e, j, i):
                    dve.wait_ge(xT_banked, l * E + e + 1)
                    for k in range(KD // 2, KD):
                        ins = dve.tensor_scalar(xgT[:, j % 2, k, :], turned_ps(e)[:, k * P:(k + 1) * P],
                                                scl[:, 2 * l + 1, k:k + 1], modc[:, 2 * l + 1, 0, k:k + 1],
                                                ALU.mult, ALU.add)
                    ins.then_inc(xT_dve, 1)

                def times_up(e, j, i):
                    dve.wait_ge(sil_ready, l * E + e + 1)
                    dve.tensor_tensor(hid[:, j % 2, :], sil[:, j % 2, :], gu_ps[j % 2][:, FF:2 * FF], ALU.mult
                                      ).then_inc(hid_ready, 1)

                def body(e, j, i):
                    static = isinstance(e, int)
                    if not static or e + 1 < E:
                        dve.wait_ge(hT_banked, HEAD + l * E + e)
                        times_up(e + 1, j + 1, i)
                    if not static or e + 2 < E:
                        dve.wait_ge(gu_done, l * E + e + 1)
                        xT_half(e + 2, j, i)
                    dve.wait_ge(dn_done, HEAD + l * E + e + 1)
                    if not static or l * E + e >= 2:
                        dve.wait_ge(y_out[j % 2], 16 * (l * (E // 2) + 2 * i + j // 2))
                    for a in range(2):
                        ins = dve.scalar_tensor_tensor(yrow[:, j % 2, a * 512:(a + 1) * 512],
                                                       psY[:, a * 512:(a + 1) * 512], gslot[:, bass.ds(e, 1)],
                                                       gbc[:, a * 512:(a + 1) * 512], ALU.mult, ALU.mult)
                    ins.then_inc(y_ready, 1)

                xT_half(0, 0, 0)
                xT_half(1, 1, 0)
                one_hots(2)
                one_hots(3)
                table(2)
                times_up(0, 0, 0)
                dve.wait_ge(gbc_in, 16 * (2 * l + 2))
                loop_experts(dve, body, first=1)

                dve.wait_ge(flag_ready, l + 1)
                most = dve.value_load(flag[0:1, l:l + 1], min_val=0, max_val=SEQ)
                with dve.If(most > P):
                    dve.wait_ge(y_out[1], 8 * E * (l + 1))
                    with dve.Fori(0, ROUNDS) as r:
                        dve.wait_ge(ov_link[l], HEAD + r * (1 + 2 * E))
                        dve.tensor_scalar(posm, posm, float(-P), None, ALU.add).then_inc(ov_link[l], 1)
                        with dve.Fori(0, E) as e:
                            n = r * E + e
                            dve.wait_ge(ov_link[l], HEAD + r * (1 + 2 * E) + 1 + 2 * e)
                            dve.wait_ge(ov_through[l], HEAD + n)
                            dve.tensor_copy(ovr, rtab[:, :, bass.ds(e, 1), :].rearrange("p t a c -> p t (a c)"))
                            dve.tensor_tensor(
                                onehot_ov, cst[:, C_SLOT:C_SLOT + P].unsqueeze(1).broadcast_to([P, T, P]),
                                posm[:, :, bass.ds(e, 1)].broadcast_to([P, T, P]),
                                ALU.is_equal).then_inc(ov_oh[l], 1)
                            dve.wait_ge(ov_tab[l], n + 1)
                            base = r * (1 + 2 * E) + 1 + 2 * e
                            dve.tensor_copy(ovtab[:, 0:TC], ps4[:, 0:TC]).then_inc(ov_link[l], 1)
                            dve.wait_ge(ov_link[l], HEAD + base + 1)
                            dve.scalar_tensor_tensor(ovtok, ovtab[:, 0:1], FAR, ovtab[:, 1:2], ALU.add, ALU.add)
                            dve.tensor_tensor(ovgate, ovtab[:, 2:3], ovtab[:, 3:4], ALU.add).then_inc(ov_link[l], 1)
                            dve.wait_ge(ov_link[l], HEAD + base + 2)
                            dve.tensor_tensor(ovgate, ovgate, ovtab[:, 4:5], ALU.add).then_inc(ov_idx[l], 1)
                            dve.wait_ge(ov_sil[l], n + 1)
                            dve.tensor_tensor(hid[:, 0, :], sil[:, 0, :], ps3[:, FF:2 * FF], ALU.mult
                                              ).then_inc(ov_hid[l], 1)
                            dve.wait_ge(ov_dn[l], HEAD + n + 1)
                            dve.wait_ge(ov_idx[l], n + 1)
                            for a in range(2):
                                ins = dve.scalar_tensor_tensor(yrow[:, 0, a * 512:(a + 1) * 512],
                                                               psY[:, a * 512:(a + 1) * 512], ovgate[:, 0:1],
                                                               gbc[:, a * 512:(a + 1) * 512], ALU.mult, ALU.mult)
                            ins.then_inc(ov_y[l], 1)

            for l in range(LAYERS):
                if l:
                    scales(2)
                    scales(3)
                    for t in range(T):
                        norm(2, t)
                    mix_in(1, 0)
                    norm(3, 0)
                    for t in range(1, T):
                        mix_in(1, t)
                        spread(3, t - 1)
                        norm(3, t)
                    spread(3, T - 1)
                expert_loop(l, *route(l))
                if l == 0:
                    dve.wait_ge(gbc_in, 16 * 3)
                    dve.wait_ge(psc_in, 16)
                    link(dve.tensor_tensor(gmix[1], gmix[1], psc, ALU.mult))
            dve.wait_ge(nfin_in, 16)
            for t in range(T):
                dve.wait_ge(std_done[4], t + 1)
                link(dve.reciprocal(rstd[:, t:t + 1], rstd[:, t:t + 1]))
                dve.scalar_tensor_tensor(xhat[:, t, :], h[:, t, :], rstd[:, t:t + 1], nfin, ALU.mult, ALU.mult
                                         ).then_inc(out_ready, 1)

        @block.tensor
        def _(pe):
            def keep_clock(count, bank=psY[:, 0:512]):
                for _ in range(count):
                    pe.matmul(bank, ident, cst[:, 0:512], start=True, stop=True)

            def ada_total(n):
                if n:
                    pe.wait_ge(row_copied, n)
                if K_VEC[n] < KD:
                    pe.wait_ge(ada_in[2 * (n % 2) + 1], 16 * (n // 2 + 1))
                    pe.wait_ge(cond_ready, 1)
                    for k in range(K_VEC[n], KD):
                        pe.matmul(ps5[0:1, 0:AC], cond[:, k:k + 1], adaw[:, n % 2, k, :], start=(k == K_VEC[n]),
                                  stop=False)
                pe.wait_ge(ada_mac, n + 1)
                pe.matmul(ps5[0:1, 0:AC], ones[:, 0:1], acc[:, n % 3, :], start=(K_VEC[n] == KD), stop=True
                          ).then_inc(ada_sum, 1)

            def transposes_all(ks):
                for k in ks:
                    if k == 0:
                        pe.wait_ge(xhat_ready[0], T)
                    if k == KD - 1:
                        pe.wait_ge(uT_act, 1)
                    for t in range(T):
                        ins = pe.transpose(first_bank(k)[:, t * P:(t + 1) * P],
                                           xhat[:, t, :].rearrange("p (a k) -> p k a", k=KD)[:, k, :], ident)
                    ins.then_inc(uT_banked, 1)

            def turn_tile(s, t):
                pe.wait_ge(xhat_ready[s], t + 1)
                if s == 1 and t == 0:
                    pe.wait_ge(att_ready, T)
                for half in range(2):
                    turned_wait(s, t, half)
                    for q in range(KD // 2):
                        src = xhat[:, t, :].rearrange("p (a k) -> p k a", k=KD)[:, half * KD // 2 + q, :]
                        ins = pe.transpose(tile_ps[half][:, q * P:(q + 1) * P], src, ident)
                    ins.then_inc(tile_banked[s], 1)

            def turned_wait(s, t, half):
                if s == 1 and t:
                    pe.wait_ge(uT_dve if half else uT_act, KD // 2 + t)
                if s == 2 and t:
                    pe.wait_ge(pooled_ready, t)
                if s == 3:
                    pe.wait_ge(pooled_ready, T)
                    if t:
                        pe.wait_ge(uT_dve if half else uT_act, KD // 2 + T + t)

            def pool_tile(t):
                pe.wait_ge(xhat_ready[2], t + 1)
                if t == 0:
                    pe.wait_ge(wpool_in, 32)
                for half in range(2):
                    turned_wait(2, t, half)
                    for q in range(KD // 2):
                        k = half * KD // 2 + q
                        g = k // 2
                        dst = tile_ps[half][:, q * P:(q + 1) * P]
                        here = xhat[:, t, k * P:(k + 1) * P]
                        ins = pe.matmul(dst, here, pmat[:, g, M_IN:M_IN + P] if t else pmat[:, g, M_FIRST:M_FIRST + P],
                                        start=True, stop=(t == 0))
                        if t:
                            ins = pe.matmul(dst[:, 0:POOL_MAX], xhat[:, t - 1, k * P:(k + 1) * P],
                                            pmat[:, g, M_BACK:M_BACK + POOL_MAX], start=False, stop=True)
                    ins.then_inc(tile_banked[2], 1)

            def logits(s, t):
                if s == 1 and t == 0:
                    pe.wait_ge(small_in, 16 * N_SMALL)
                done = KD // 2 + (s // 2) * T + t + 1
                pe.wait_ge(uT_act, done)
                pe.wait_ge(uT_dve, done)
                for k in range(KD):
                    ins = pe.matmul(ps2[:, t * E:(t + 1) * E], uT[:, k, t * P:(t + 1) * P], wr[:, k, :],
                                    start=(k == 0), stop=(k == KD - 1))
                ins.then_inc(logits_ready, 1)

            for q in (dn_done, hT_banked, *ov_dn):
                pe.sem_inc(q, HEAD)
            pe.wait_ge(const_in, 16)
            for n in range(N_FIRST):
                if n == 2:
                    transposes_all(range(KD - 1))
                ada_total(n)
            pe.wait_ge(row_copied, N_FIRST)
            keep_clock(4, ps5[:, :])
            transposes_all(range(KD - 1, KD))

            def project(m):
                name, i = PROJ[m]
                bank = psY[:, (m % 2) * 512:(m % 2 + 1) * 512]
                if m == 0:
                    pe.wait_ge(uT_act, KD // 2)
                    pe.wait_ge(uT_dve, KD // 2)
                    pe.wait_ge(win_in["q"], 16)
                if m == 2:
                    pe.wait_ge(win_in["qkv"], 16)
                if 6 <= m < 9:
                    pe.wait_ge(win_in[name], 16)
                if m >= 2:
                    if PROJ[m - 2][0] in ACT_SIDE:
                        pe.wait_ge(proj_act, act_before[m - 1])
                    else:
                        pe.wait_ge(proj_dve, m - 1 - act_before[m - 1])
                if name == "v":
                    for t in range(T):
                        for k in range(KD):
                            ins = pe.matmul(bank[:, t * P:(t + 1) * P], uT[:, k, t * P:(t + 1) * P],
                                            win_qkv[:, k, V0:V0 + P], start=(k == 0), stop=(k == KD - 1))
                else:
                    for k in range(KD):
                        src, at0 = {"q": (win_qkv, 0), "k": (win_qkv, K0), "c": (win_c, 0), "x": (win_x, 0),
                                    "b": (win_b, 0)}[name]
                        wt = src[:, k, at0 + i * P:at0 + (i + 1) * P]
                        ins = pe.matmul(bank, wt, uT[:, k, :], start=(k == 0), stop=(k == KD - 1))
                ins.then_inc(proj_ready, 1)

            def scores(u):
                b, kv = u // KVH, u % KVH
                if u == 0:
                    pe.wait_ge(proj_act, 6)
                    pe.wait_ge(kswap_in, 32)
                if u:
                    pe.wait_ge(scores_read, u)
                lo = 0 if b else P
                for g in range(GH):
                    odd, i = g // 2, g % 2
                    rows = slice(odd * HD, (odd + 1) * HD)
                    ins = pe.matmul(psA[:, g * 256 + lo:(g + 1) * 256], qT[rows, kv * 2 + i, b * P:(b + 1) * P],
                                    (kT if odd == kv else kswap)[rows, (b - 1) * P + lo:(b + 1) * P],
                                    start=True, stop=True)
                ins.then_inc(scores_ready, 1)

            def turn_prob(u):
                b = u // KVH
                pe.wait_ge(prob_ready, u + 1)
                if u:
                    pe.wait_ge(probT_ready, u)
                for kb in range(0 if b else 1, 2):
                    for g in range(GH):
                        ins = pe.transpose((ps3 if kb else ps2)[:, g * P:(g + 1) * P],
                                           prob[:, u % 2, g, kb * P:(kb + 1) * P], ident)
                ins.then_inc(probT_banked, 1)

            def attend(u):
                b, kv = u // KVH, u % KVH
                pe.wait_ge(probT_ready, u + 1)
                if kv == 0 and b:
                    pe.wait_ge(att_ready, b)
                for g in range(GH):
                    odd, i = g // 2, g % 2
                    dst = ps4[odd * HD:(odd + 1) * HD, (kv * 2 + i) * P:(kv * 2 + i + 1) * P]
                    for kb in range(0 if b else 1, 2):
                        ins = pe.matmul(dst, vtok[:, b - 1 + kb, kv * HD:(kv + 1) * HD],
                                        probT[:, kb, g * P:(g + 1) * P], start=(kb == 0 or b == 0), stop=(kb == 1))
                ins.then_inc(att_banked, 1)

            def mix_half(t, a, qs=range(8)):
                ps = mix_ps[0][t]
                if t == 0 and a == 0:
                    for q in wout_in:
                        pe.wait_ge(q, 16)
                    pe.wait_ge(proj_dve, len(PROJ) - act_before[-1])
                if a == 0:
                    pe.wait_ge(att_ready, t + 1)
                    if t in (1, 3):
                        pe.wait_ge(h_ready[0], t)
                    if t == 2:
                        pe.wait_ge(scores_read, ATT_U)
                for q in qs:
                    lhs = attnT[:, q, t * P:(t + 1) * P] if q < 4 else convT[:, q - 4, t * P:(t + 1) * P]
                    ins = pe.matmul(ps[:, a * 512:(a + 1) * 512], lhs, wo[:, q, a * 512:(a + 1) * 512],
                                    start=(q == 0), stop=(q == 7))
                if a == 1 and q == 7:
                    ins.then_inc(mix_banked, 1)

            for m in range(6):
                project(m)
                for n in place_totals(m):
                    ada_total(n)
            for u in range(ATT_U + 1):
                if u < ATT_U:
                    scores(u)
                if u:
                    turn_prob(u - 1)
                for n in unit_places(u, 0, place_totals):
                    ada_total(n)
                for m in BESIDE[u][0]:
                    project(m)
                if u >= ATT_U - 2:
                    mix_half(u - ATT_U + 2, 0)
                if u:
                    attend(u - 1)
                for n in unit_places(u, 1, place_totals):
                    ada_total(n)
                for m in BESIDE[u][1]:
                    project(m)
                if u >= ATT_U - 2:
                    mix_half(u - ATT_U + 2, 1)
                for n in unit_places(u, 2, place_totals):
                    ada_total(n)

            def pool_out(t):
                ps = mix_ps[1][t]
                pe.wait_ge(pooled_ready, t + 1)
                if t >= 2:
                    pe.wait_ge(h_ready[1], t - 1)
                for g in range(4):
                    for q in range(2):
                        ins = pe.matmul(ps[:, g * 256:(g + 1) * 256], pooled[:, 2 * g + q, t * P:(t + 1) * P],
                                        wpool[:, 2 * g + q, :], start=(q == 0), stop=(q == 1))
                ins.then_inc(mix_banked, 1)

            def route(l):
                pe.wait_ge(sel_ready, l + 1)
                pe.wait_ge(cstb_ready, 1)
                for t in range(T + 1):
                    for q in range(min(t + 1, T)):
                        ins = pe.matmul(ps2[:, t * E:(t + 1) * E], cstb[:, 0:P] if q == t else cstb[:, P:2 * P],
                                        sel_tile[:, q * E:(q + 1) * E], start=(q == 0), stop=(q == min(t, T - 1)))
                ins.then_inc(pos_ready, 1)
                pe.wait_ge(row_copied, LAYERS * NCH)
                for i in range(2):
                    table(l, i)

            def table(l, i):
                if i == 2:
                    pe.wait_ge(table_ready, l * TABLES + 1)
                for n, g in enumerate(TABLE[i]):
                    pe.wait_ge(onehot_ready, l * EG + g + 1)
                    for e in range(EPG):
                        at0 = (n * EPG + e) * TC
                        for t in range(T):
                            ins = pe.matmul((ps4 if i == 1 else ps5)[:, at0:at0 + TC], onehot[:, g % 2, t, e, :],
                                            rtab[:, t, g * EPG + e, :], start=(t == 0), stop=(t == T - 1))
                ins.then_inc(table_banked, 1)

            def expert_loop(l):
                def turn_in(e, j, i):
                    pe.wait_ge(xg_in[j % 4], 16 * (l * (E // 4) + i + 1))
                    if not isinstance(e, int) or l * E + e > 1:
                        done = l * E if isinstance(e, int) and e == 1 else l * E + e
                        pe.wait_ge(xT_act, done)
                        pe.wait_ge(xT_dve, done)
                    for k in range(KD):
                        ins = pe.transpose(turned_ps(e)[:, k * P:(k + 1) * P],
                                           xg[:, j % 4, :].rearrange("p (a k) -> p k a", k=KD)[:, k, :], ident)
                    ins.then_inc(xT_banked, 1)

                def first_product(e, j, i):
                    pe.wait_ge(xT_act, l * E + e + 1)
                    pe.wait_ge(xT_dve, l * E + e + 1)
                    pe.wait_ge(gu_in[j % 4], 32 * (l * (E // 4) + i + 1))
                    for k in range(KD):
                        ins = pe.matmul(gu_ps[j % 2][:, :].rearrange("p (a f) -> p a f", a=2), xgT[:, j % 2, k, :],
                                        w_gu(j % 4)[:, :, k, :], start=(k == 0), stop=(k == KD - 1))
                    ins.then_inc(gu_done, 1)

                def body(e, j, i):
                    static = isinstance(e, int)
                    if not static or e + 1 < E:
                        pe.wait_ge(hid_ready, HEAD + l * E + e)
                        first_product(e + 1, j + 1, i + (j + 1) // 4)
                    pe.wait_ge(hid_ready, HEAD + l * E + e + 1)
                    pe.wait_ge(hT_ready, HEAD + l * E + e)
                    for q in range(2):
                        ins = pe.transpose(ps2[:, q * P:(q + 1) * P],
                                           hid[:, j % 2, :].rearrange("p (a c) -> p c a", c=2)[:, q, :], ident)
                    ins.then_inc(hT_banked, 1)
                    if not static or e + 2 < E:
                        turn_in(e + 2, j + 2, i + (j + 2) // 4)
                    pe.wait_ge(hT_ready, HEAD + l * E + e + 1)
                    pe.wait_ge(y_ready, HEAD + l * E + e)
                    pe.wait_ge(dn_in[j], 16 * (l * (E // 4) + i + 1))
                    for a in range(2):
                        for q in range(2):
                            ins = pe.matmul(psY[:, a * 512:(a + 1) * 512], hT[:, q, :],
                                            w_dn(j)[:, q, a * 512:(a + 1) * 512], start=(q == 0), stop=(q == 1))
                    ins.then_inc(dn_done, 1)

                keep_clock(1)
                turn_in(0, 0, 0)
                turn_in(1, 1, 0)
                first_product(0, 0, 0)
                table(l, 2)
                loop_experts(pe, body)

                pe.wait_ge(flag_ready, l + 1)
                most = pe.value_load(flag[0:1, l:l + 1], min_val=0, max_val=SEQ)
                with pe.If(most > P):
                    with pe.Fori(0, ROUNDS * E) as n:
                        pe.wait_ge(ov_oh[l], n + 1)
                        for t in range(T):
                            ins = pe.matmul(ps4[:, 0:TC], onehot_ov[:, t, :], ovr[:, t, :],
                                            start=(t == 0), stop=(t == T - 1))
                        ins.then_inc(ov_tab[l], 1)
                        pe.wait_ge(ov_xg[l], 16 * n + 16)
                        for k in range(KD):
                            ins = pe.transpose(psA[:, k * P:(k + 1) * P],
                                               xg[:, 0, :].rearrange("p (a k) -> p k a", k=KD)[:, k, :], ident)
                        ins.then_inc(ov_xb[l], 1)
                        pe.wait_ge(ov_xT[l], n + 1)
                        pe.wait_ge(ov_w[l], 48 * n + 48)
                        for k in range(KD):
                            ins = pe.matmul(ps3[:, :].rearrange("p (a f) -> p a f", a=2), xgT[:, 0, k, :],
                                            w_gu(0)[:, :, k, :], start=(k == 0), stop=(k == KD - 1))
                        ins.then_inc(ov_gu[l], 1)
                        pe.wait_ge(ov_hid[l], n + 1)
                        for q in range(2):
                            ins = pe.transpose(ps2[:, q * P:(q + 1) * P],
                                               hid[:, 0, :].rearrange("p (a c) -> p c a", c=2)[:, q, :], ident)
                        ins.then_inc(ov_hb[l], 1)
                        pe.wait_ge(ov_hT[l], n + 1)
                        for a in range(2):
                            for q in range(2):
                                ins = pe.matmul(psY[:, a * 512:(a + 1) * 512], hT[:, q, :],
                                                w_dn(0)[:, q, a * 512:(a + 1) * 512], start=(q == 0), stop=(q == 1))
                        ins.then_inc(ov_dn[l], 1)

            for l in range(LAYERS):
                if l == 0:
                    turn_tile(1, 0)
                    mix_half(3, 0)
                    turn_tile(1, 1)
                    mix_half(3, 1, range(0, 4))
                    turn_tile(1, 2)
                    mix_half(3, 1, range(4, 8))
                    for t in range(3):
                        logits(1, t)
                    turn_tile(1, 3)
                    logits(1, 3)
                else:
                    pe.wait_ge(h_back[0], 16)
                    keep_clock(2)
                    pool_tile(0)
                    for t in range(1, T):
                        pool_tile(t)
                        pool_out(t - 1)
                    turn_tile(3, 0)
                    pool_out(T - 1)
                    for t in range(1, T):
                        if t > 1:
                            keep_clock(1, ps5[:, :])
                        turn_tile(3, t)
                        logits(3, t - 1)
                    logits(3, T - 1)
                route(l)
                expert_loop(l)


_INS = ['x', 'c', 'w_ada', 'b_ada', 'norm_mix', 'norm_ffn', 'w_in', 'w_out', 'sinks', 'conv_w', 'w_pool', 'pool_scale',
        'w_router', 'b_router', 'w_gate', 'w_up', 'w_down', 'norm_final']


def _constants():
    import numpy as np
    a = np.zeros((P, C_END), np.float32)
    p = np.arange(P)
    a[:, C_ID:C_ID + P] = np.eye(P)
    a[:, C_BEF:C_BEF + P] = p[:, None] < p[None, :]
    dist = p[:, None] + P - np.arange(2 * P)[None, :]
    a[:, C_DIST:C_DIST + 2 * P] = np.where((dist >= 0) & (dist < P), dist, 1e30)
    a[:, C_SLOT:C_SLOT + P] = p[None, :]
    a[:, C_ONE:C_ONE + P] = 1.0
    tok = np.zeros((P, T, 2), np.float32)
    tok[:, :, 0] = p[:, None]
    tok[:, :, 1] = P * np.arange(T)[None, :] - FAR
    a[:, C_TOK:C_TOK + 8] = tok.reshape(P, 8)
    j = np.arange(4)
    a[:, C_JLT:C_JLT + 16] = (j[None, :] < j[:, None]).reshape(1, 16)
    a[:, C_FST:C_FST + 4] = 4 - j
    return a


def _pool_matrices():
    import numpy as np
    a = np.zeros((P, 4, M_END), np.float32)
    read, to = np.arange(P)[:, None], np.arange(P)[None, :]
    for g in range(4):
        w = 2 << g
        inside = (read <= to) & (read > to - w)
        a[:, g, M_IN:M_IN + P] = np.where(inside, 1.0 / w, 0.0) - (read == to)
        a[:, g, M_BACK:M_BACK + POOL_MAX] = np.where(read - P > to - w, 1.0 / w, 0.0)[:, 0:POOL_MAX]
        first = np.where(inside, 1.0 / np.minimum(to + 1, w), 0.0) - (read == to)
        a[:, g, M_FIRST:M_FIRST + P] = first
    return a


def kernel(**inputs):
    import numpy as _np
    import concourse.bacc as _bacc
    from concourse.bass_utils import run_bass_kernel_spmd as _run

    nc = _bacc.Bacc("TRN2", target_bir_lowering=False, num_devices=1)
    arrays, args = {}, []
    for name in _INS:
        a = _np.ascontiguousarray(inputs[name])
        arrays[f"in_{name}_dram"] = a
        args.append(nc.dram_tensor(f"in_{name}_dram", a.shape, mybir.dt.from_np(a.dtype), kind="ExternalInput").ap())
    arrays["constants"] = _constants()
    args.append(nc.dram_tensor("constants", (P, C_END), F32, kind="ExternalInput").ap())
    arrays["pool_matrices"] = _pool_matrices()
    args.append(nc.dram_tensor("pool_matrices", (P, 4, M_END), F32, kind="ExternalInput").ap())
    args.append(nc.dram_tensor("out_dram", (1, SEQ, D), F32, kind="ExternalOutput").ap())
    args.append(nc.dram_tensor("mod_dram", (LAYERS, MODW), F32, kind="Internal").ap())
    args.append([nc.dram_tensor(f"xhat_dram{l}", (SEQ, D), F32, kind="Internal").ap() for l in range(LAYERS)])
    args.append([nc.dram_tensor(f"h_dram{l}", (SEQ, D), F32, kind="Internal").ap() for l in range(LAYERS)])
    trunk(nc, *args)
    return _run(nc, [arrays], core_ids=[0]).results[0]["out_dram"]
```
